# Optimizing a Trainium2 kernel written in Bass

```python
import jax, jax.numpy as jnp
from jax import lax
import numpy as np

D_MODEL = 1024
BATCH = 1
SEQ = 1024
DEPTH = 1

HEAD_DIM = 64
N_Q_HEADS = D_MODEL // HEAD_DIM
N_KV_HEADS = max(1, N_Q_HEADS // 8)
GROUP = N_Q_HEADS // N_KV_HEADS
WINDOW = 128
ATTN_BLOCK = 128
ROPE_THETA = 500000.0
ROPE_DIM = HEAD_DIM // 4
Q_WIDTH = N_Q_HEADS * HEAD_DIM
KV_WIDTH = N_KV_HEADS * HEAD_DIM
NEG_INF = -1e30

POOL_WINDOWS = (2, 4, 8, 16)
N_POOL_GROUPS = len(POOL_WINDOWS)
POOL_WIDTH = D_MODEL // 2
POOL_GROUP_WIDTH = POOL_WIDTH // N_POOL_GROUPS

IN_WIDTH = Q_WIDTH + 2 * KV_WIDTH + POOL_WIDTH + 2 * D_MODEL

N_EXPERTS = 32
TOP_K = 4
D_FF = D_MODEL
SWIGLU_ALPHA = 1.702
SWIGLU_LIMIT = 7.0
MOE_BLOCK = 128

RMS_EPS = 1e-5

kernel_name = "hybrid_gated_swa_pool_moe"

def rmsnorm(x, g):
    xf = x.astype(jnp.float32)
    y = xf * lax.rsqrt(jnp.mean(xf * xf, axis=-1, keepdims=True) + RMS_EPS)
    return (y * g.astype(jnp.float32)).astype(x.dtype)

def partial_rope(t, positions):
    half = ROPE_DIM // 2
    inv_freq = jnp.power(jnp.float32(ROPE_THETA), -jnp.arange(half, dtype=jnp.float32) * (2.0 / ROPE_DIM))
    ang = positions.astype(jnp.float32)[..., None] * inv_freq
    cos = jnp.cos(ang)[:, :, None, :]
    sin = jnp.sin(ang)[:, :, None, :]
    tr = t[..., :ROPE_DIM].astype(jnp.float32)
    t1, t2 = tr[..., :half], tr[..., half:]
    rot = jnp.concatenate([t1 * cos - t2 * sin, t2 * cos + t1 * sin], axis=-1).astype(t.dtype)
    return jnp.concatenate([rot, t[..., ROPE_DIM:]], axis=-1)

def sliding_window_gqa(q, k, v, sinks):
    B, S = q.shape[0], q.shape[1]
    NB = S // ATTN_BLOCK
    qb = q.reshape(B, NB, ATTN_BLOCK, N_KV_HEADS, GROUP, HEAD_DIM)

    def band(t):
        tb = t.reshape(B, NB, ATTN_BLOCK, N_KV_HEADS, HEAD_DIM)
        prev = jnp.concatenate([jnp.zeros_like(tb[:, :1]), tb[:, :-1]], axis=1)
        return jnp.concatenate([prev, tb], axis=2)

    kb, vb = band(k), band(v)
    scores = jnp.einsum('bnqhgd,bnkhd->bnhgqk', qb, kb,
                        preferred_element_type=jnp.float32) * (HEAD_DIM ** -0.5)
    qi = jnp.arange(ATTN_BLOCK)[:, None]
    kj = jnp.arange(2 * ATTN_BLOCK)[None, :]
    dist = qi + ATTN_BLOCK - kj
    blk = jnp.arange(NB)[:, None, None]
    valid = (dist >= 0) & (dist < WINDOW) & (blk * ATTN_BLOCK + kj[None] - ATTN_BLOCK >= 0)
    scores = jnp.where(valid[None, :, None, None], scores, NEG_INF)
    sink = jnp.broadcast_to(sinks.astype(jnp.float32).reshape(1, 1, N_KV_HEADS, GROUP, 1, 1),
                            scores.shape[:-1] + (1,))
    probs = jax.nn.softmax(jnp.concatenate([scores, sink], axis=-1), axis=-1)[..., :-1]
    out = jnp.einsum('bnhgqk,bnkhd->bnqhgd', probs.astype(v.dtype), vb)
    return out.reshape(B, S, Q_WIDTH)

def multiscale_causal_pool(u, pool_w, pool_scale):
    B, S = u.shape[0], u.shape[1]
    uf = u.astype(jnp.float32)
    cs0 = jnp.pad(jnp.cumsum(uf, axis=1), ((0, 0), (1, 0), (0, 0)))
    outs = []
    for g, w in enumerate(POOL_WINDOWS):
        sl = slice(g * POOL_GROUP_WIDTH, (g + 1) * POOL_GROUP_WIDTH)
        c = cs0[:, :, sl]
        lower = jnp.pad(c, ((0, 0), (w - 1, 0), (0, 0)))[:, :S]
        total = c[:, 1:] - lower
        count = jnp.minimum(jnp.arange(1, S + 1), w).astype(jnp.float32)[None, :, None]
        outs.append(total / count - uf[:, :, sl])
    pooled = jnp.stack(outs, axis=2)
    mixed = jnp.einsum('bsgc,gcd->bsgd', pooled, pool_w.astype(jnp.float32))
    return (mixed.reshape(B, S, POOL_WIDTH) * pool_scale.astype(jnp.float32)).astype(u.dtype)

def clamped_swiglu(u):
    glu, lin = u[..., :D_FF], u[..., D_FF:]
    glu = jnp.minimum(glu, SWIGLU_LIMIT)
    lin = jnp.clip(lin, -SWIGLU_LIMIT, SWIGLU_LIMIT)
    return glu * jax.nn.sigmoid(SWIGLU_ALPHA * glu) * (lin + 1.0)

def moe_ffn(h, w_router, b_router, w_up, b_up, w_down, b_down):
    T, D = h.shape
    logits = (h @ w_router + b_router).astype(jnp.float32)
    top_vals, top_idx = lax.top_k(logits, TOP_K)
    gates = jax.nn.softmax(top_vals, axis=-1)
    A = T * TOP_K
    e_flat = top_idx.reshape(A).astype(jnp.int32)
    tok_flat = jnp.arange(A, dtype=jnp.int32) // TOP_K
    g_flat = gates.reshape(A)
    order = jnp.argsort(e_flat)
    e_sorted = e_flat[order]
    counts = jnp.bincount(e_flat, length=N_EXPERTS).astype(jnp.int32)
    padded = (counts + MOE_BLOCK - 1) // MOE_BLOCK * MOE_BLOCK
    start = jnp.cumsum(counts) - counts
    pend = jnp.cumsum(padded)
    pstart = pend - padded
    dest = pstart[e_sorted] + jnp.arange(A, dtype=jnp.int32) - start[e_sorted]
    n_slots = (A + MOE_BLOCK - 1) // MOE_BLOCK * MOE_BLOCK + N_EXPERTS * MOE_BLOCK
    n_blocks = n_slots // MOE_BLOCK
    slot_tok = jnp.full((n_slots,), T, jnp.int32).at[dest].set(tok_flat[order])
    slot_gate = jnp.zeros((n_slots,), jnp.float32).at[dest].set(g_flat[order])
    blk_expert = jnp.minimum(
        jnp.searchsorted(pend, jnp.arange(n_blocks, dtype=jnp.int32) * MOE_BLOCK, side='right'),
        N_EXPERTS - 1).astype(jnp.int32)
    h_pad = jnp.concatenate([h, jnp.zeros((1, D), h.dtype)], axis=0)
    xs = h_pad[slot_tok].reshape(n_blocks, MOE_BLOCK, D)

    def expert_block(args):
        xb, e = args
        u = xb @ w_up[e] + b_up[e]
        return clamped_swiglu(u) @ w_down[e] + b_down[e]

    ys = lax.map(expert_block, (xs, blk_expert)).reshape(n_slots, D)
    out = jnp.zeros((T + 1, D), jnp.float32).at[slot_tok].add(
        ys.astype(jnp.float32) * slot_gate[:, None])[:T]
    return out.astype(h.dtype)

def setup_inputs(seed: int = 0) -> dict:
    key = jax.random.key(seed)
    ks = jax.random.split(key, 20)
    L, D = DEPTH, D_MODEL
    nrm = jax.random.normal
    return {
        "x": nrm(ks[0], (BATCH, SEQ, D), jnp.float32),
        "positions": jnp.broadcast_to(jnp.arange(SEQ, dtype=jnp.int32), (BATCH, SEQ)),
        "norm1_g": 1.0 + 0.05 * nrm(ks[1], (L, D), jnp.float32),
        "w_in": nrm(ks[2], (L, D, IN_WIDTH), jnp.float32) * D ** -0.5,
        "b_in": 0.02 * nrm(ks[3], (L, IN_WIDTH), jnp.float32),
        "attn_sinks": nrm(ks[4], (L, N_Q_HEADS), jnp.float32),
        "w_attn_br": nrm(ks[5], (L, Q_WIDTH, D), jnp.float32) * Q_WIDTH ** -0.5,
        "pool_w": nrm(ks[6], (L, N_POOL_GROUPS, POOL_GROUP_WIDTH, POOL_GROUP_WIDTH), jnp.float32) * POOL_GROUP_WIDTH ** -0.5,
        "pool_scale": 1.0 + 0.1 * nrm(ks[7], (L, POOL_WIDTH), jnp.float32),
        "w_pool_br": nrm(ks[8], (L, POOL_WIDTH, D), jnp.float32) * POOL_WIDTH ** -0.5,
        "w_out": nrm(ks[9], (L, D, D), jnp.float32) * D ** -0.5,
        "norm2_g": 1.0 + 0.05 * nrm(ks[10], (L, D), jnp.float32),
        "w_router": nrm(ks[11], (L, D, N_EXPERTS), jnp.float32) * D ** -0.5,
        "b_router": 0.01 * nrm(ks[12], (L, N_EXPERTS), jnp.float32),
        "w_up": nrm(ks[13], (L, N_EXPERTS, D, 2 * D_FF), jnp.float32) * D ** -0.5,
        "b_up": 0.02 * nrm(ks[14], (L, N_EXPERTS, 2 * D_FF), jnp.float32),
        "w_down": nrm(ks[15], (L, N_EXPERTS, D_FF, D), jnp.float32) * D_FF ** -0.5,
        "b_down": 0.02 * nrm(ks[16], (L, N_EXPERTS, D), jnp.float32),
        "normf_g": 1.0 + 0.05 * nrm(ks[17], (D,), jnp.float32),
    }

def reference(x, positions, norm1_g, w_in, b_in, attn_sinks, w_attn_br, pool_w, pool_scale,
              w_pool_br, w_out, norm2_g, w_router, b_router, w_up, b_up, w_down, b_down, normf_g):
    B, S, D = x.shape
    o_q = Q_WIDTH
    o_k = o_q + KV_WIDTH
    o_v = o_k + KV_WIDTH
    o_p = o_v + POOL_WIDTH
    o_ga = o_p + D_MODEL
    for l in range(DEPTH):
        h = rmsnorm(x, norm1_g[l])
        proj = jnp.einsum('bsd,de->bse', h, w_in[l]) + b_in[l]
        q = proj[..., :o_q].reshape(B, S, N_Q_HEADS, HEAD_DIM)
        k = proj[..., o_q:o_k].reshape(B, S, N_KV_HEADS, HEAD_DIM)
        v = proj[..., o_k:o_v].reshape(B, S, N_KV_HEADS, HEAD_DIM)
        u_pool = proj[..., o_v:o_p]
        g_attn = jax.nn.sigmoid(proj[..., o_p:o_ga].astype(jnp.float32))
        g_pool = jax.nn.sigmoid(proj[..., o_ga:].astype(jnp.float32))
        q = partial_rope(q, positions)
        k = partial_rope(k, positions)
        y_attn = sliding_window_gqa(q, k, v, attn_sinks[l]) @ w_attn_br[l]
        y_pool = multiscale_causal_pool(u_pool, pool_w[l], pool_scale[l]) @ w_pool_br[l]
        merged = (g_attn * y_attn.astype(jnp.float32) + g_pool * y_pool.astype(jnp.float32)).astype(x.dtype)
        x = x + merged @ w_out[l]
        h2 = rmsnorm(x, norm2_g[l]).reshape(B * S, D)
        x = x + moe_ffn(h2, w_router[l], b_router[l], w_up[l], b_up[l], w_down[l], b_down[l]).reshape(B, S, D)
    return rmsnorm(x, normf_g)


_drawn_inputs = setup_inputs


def setup_inputs(seed=0):
    import zlib

    import numpy as np

    out = dict(_drawn_inputs(seed))
    spreads = {}
    factors = {'attn_sinks': 4.491, 'b_up': 5.541, 'b_down': 6.387}
    for name, (base, spread) in spreads.items():
        noise = np.random.default_rng([zlib.crc32(name.encode()), seed]).standard_normal(out[name].shape)
        drawn = base * np.exp(spread * noise) if base else spread * noise
        out[name] = __import__('jax').numpy.asarray(drawn.astype(out[name].dtype))
    for name, factor in factors.items():
        out[name] = (out[name] * factor).astype(out[name].dtype)
    return out
```

```python
from contextlib import ExitStack

import numpy as np

import concourse.bass as bass
from concourse import mybir

F32 = mybir.dt.float32
F32R = mybir.dt.float32r
I32 = mybir.dt.int32
U32 = mybir.dt.uint32
ALU = mybir.AluOpType
ACT = mybir.ActivationFunctionType
AX_X = mybir.AxisListType.X

P = 128
D = 1024
SEQ = 1024
KT = D // P
HALF = 512
TT = HALF // P
HEADS, KVH, HD = 16, 2, 64
ROPE_DIM, ROPE_THETA = HD // 4, 500000.0
PW = D // 2
POOL_WINDOWS = (2, 4, 8, 16)
NG = len(POOL_WINDOWS)
HIST = 16
O_K = HEADS * HD
O_V = O_K + KVH * HD
O_U = O_V + KVH * HD
O_GA = O_U + PW
O_GP = O_GA + D
E, TOPK, DFF = 32, 4, 1024
EPS = 1e-5
ALPHA, LIMIT = 1.702, 7.0
NEG = -1e30

ITEM = 160
SUB = ITEM // 2
ROUNDS = -(-SEQ // ITEM)
SLOTS_PER_EXPERT = ROUNDS * ITEM
NCODES = SEQ * TOPK
MAX_ITEMS = E + NCODES // ITEM
ITEM_ROW = 64
FREE_CODE = 1 << 20

RAW = 4
SPLIT = 2
SLOT = 2048

PROJ_SLOTS = 8
GATE0 = PROJ_SLOTS
OUT0 = GATE0 + 2 * KT
MIX_SLOTS = OUT0 + 4
SPLITS = PROJ_SLOTS + KT
TILES = ["k0", "k1", "v"] + [f"q{i}" for i in range(8)] + [f"u{i}" for i in range(4)]
ROPED = [0, 1] + list(range(3, 11))
UNITS = TT * HEADS // 2
B_Q, B_U, B_GA, B_GP, B_PS, NB = 2, 10, 14, 22, 30, 34

UP_SLOTS, DOWN_SLOTS = 8, 4
ITEM_SLOTS = UP_SLOTS + DOWN_SLOTS


def rope_freqs():
    half = ROPE_DIM // 2
    f = np.power(np.float32(ROPE_THETA), -np.arange(half, dtype=np.float32) * np.float32(2.0 / ROPE_DIM))
    col = np.zeros((P, 1), np.float32)
    for h in range(P // HD):
        for j in range(ROPE_DIM):
            col[h * HD + j, 0] = f[j % half]
    return col


def shape_constants():
    half = ROPE_DIM // 2
    swap = np.zeros((P, P), np.float32)
    for h in range(P // HD):
        for j in range(half):
            swap[h * HD + j + half, h * HD + j] = -1.0
            swap[h * HD + j, h * HD + j + half] = 1.0
    q, k = np.arange(P)[:, None], np.arange(2 * P)[None, :]
    dist = q + P - k
    band = (dist >= 0) & (dist < P)
    masks = np.stack([np.where(band & (k >= P), 0.0, NEG), np.where(band, 0.0, NEG)], 1).astype(np.float32)
    fix = np.ones((P, 2, NG, HIST), np.float32)
    for g, w in enumerate(POOL_WINDOWS):
        fix[:, 0, g, :] = w / np.minimum(np.arange(1, HIST + 1), w)
    return {
        "c_ident": np.eye(P, dtype=np.float32),
        "c_before": np.triu(np.ones((P, P), np.float32), 1),
        "c_swap": swap,
        "c_masks": masks,
        "c_freq": rope_freqs(),
        "c_fix": fix.reshape(P, 2, NG * HIST),
    }


def cut_pi():
    two_pi, parts = 2 * np.pi, []
    for _ in range(2):
        m, e = np.frexp(two_pi)
        part = float(np.floor(m * 256) / 256 * 2.0**e)
        parts.append(part)
        two_pi -= part
    return parts + [float(np.float32(two_pi))]


class Steps:

    def __init__(self, eng, sem, base=0):
        self.eng, self.sem, self.base, self.n = eng, sem, base, 0

    def done(self, ins):
        self.n += 1
        ins.then_inc(self.sem, 1)
        return self.n

    def wait(self, n=None):
        self.eng.wait_ge(self.sem, self.base + (self.n if n is None else n))

    def link(self, ins):
        self.done(ins)
        self.wait()


N_CONSTS = 22
MIX_VECTOR_STEPS = 170
MIX_POOL_STEPS = 22


def decoder_layer(nc, x, positions, norm1_g, w_in, b_in, attn_sinks, w_attn_br, pool_w, pool_scale,
                  w_pool_br, w_out, norm2_g, w_router, b_router, w_up, b_up, w_down, b_down, normf_g,
                  c_ident, c_before, c_swap, c_masks, c_freq, c_fix, out):
    x_rows = x[0]
    out_rows = out[0]
    w_in, w_attn, w_pool, w_o = w_in[0], w_attn_br[0], w_pool_br[0], w_out[0]
    w_up, w_down = w_up[0], w_down[0]

    x2_dram = nc.dram_tensor("x2_rows", [SEQ, D], F32, kind="Internal").ap()
    h2_dram = nc.dram_tensor("h2_rows", [SEQ, D], F32, kind="Internal").ap()
    y_dram = nc.dram_tensor("y_rows", [NCODES, D], F32, kind="Internal").ap()
    slot_dram = nc.dram_tensor("slot_entries", [E * SLOTS_PER_EXPERT, 2], I32, kind="Internal").ap()
    item_dram = nc.dram_tensor("item_entries", [ITEM_ROW, 2], I32, kind="Internal").ap()

    with ExitStack() as whole:
        def sb(name, shape, dt=F32, scope=whole):
            return scope.enter_context(nc.sbuf_tensor(name, shape, dt))

        ps = whole.enter_context(nc.psum_tensor("banks", [P, 8, 512], F32))
        keep = {
            "ps": ps,
            "ident": sb("ident", [P, P]),
            "gates": sb("gates", [P, SEQ // P, TOPK]),
            "gate_of": sb("gate_of", [P, SEQ // P, E]),
            "item_row": sb("item_row", [1, 2 * ITEM_ROW], I32),
            "n_items": sb("n_items", [P, 1], I32),
        }
        with ExitStack() as scope:
            mixer(nc, scope, keep, x_rows, positions, norm1_g, w_in, b_in, attn_sinks, w_attn, pool_w[0],
                  pool_scale, w_pool, w_o, norm2_g, w_router[0], b_router, c_ident, c_before, c_swap,
                  c_masks, c_freq, c_fix, x2_dram, h2_dram, slot_dram, item_dram)
        with ExitStack() as scope:
            experts(nc, scope, keep, w_up, b_up[0], w_down, h2_dram, y_dram, slot_dram)
        with ExitStack() as scope:
            combine(nc, scope, keep, x2_dram, y_dram, b_down[0], normf_g, out_rows)


def mixer(nc, scope, keep, x_rows, positions, norm1_g, w_in, b_in, attn_sinks, w_attn, pool_w,
          pool_scale, w_pool, w_o, norm2_g, w_router, b_router, c_ident, c_before, c_swap, c_masks,
          c_freq, c_fix, x2_dram, h2_dram, slot_dram, item_dram):
    def sb(name, shape, dt=F32):
        return scope.enter_context(nc.sbuf_tensor(name, shape, dt))

    def sem(name):
        return scope.enter_context(nc.semaphore(name))

    ps, ident = keep["ps"], keep["ident"]
    gates, gate_of = keep["gates"], keep["gate_of"]
    item_row, n_items = keep["item_row"], keep["n_items"]

    before = sb("before", [P, P])
    ones = sb("ones", [P, P])
    swap = sb("swap", [P, P])
    masks = sb("masks", [P, 2, 2 * P])
    freq = sb("freq", [P, 1])
    fix = sb("fix", [P, 2, NG * HIST])
    g1_row, g2_row = sb("g1_row", [P, D]), sb("g2_row", [P, D])
    bv_row, br_row = sb("bv_row", [P, P]), sb("br_row", [P, E])
    sinks, sinks8 = sb("sinks", [P, HEADS]), sb("sinks8", [P, HEADS])
    bias_rows, bias = sb("bias_rows", [NB, P]), sb("bias", [P, NB])
    pool_mix = sb("pool_mix", [P, NG, P])
    router = sb("router", [P, KT, E])
    pos_i = sb("pos_i", [P, HALF], I32)
    cos, sin = sb("cos", [P, HALF]), sb("sin", [P, HALF])

    xs = sb("xs", [P, TT, D])
    rows = sb("rows", [P, TT, D])
    h_hi, h_lo = sb("h_hi", [P, KT, HALF], F32R), sb("h_lo", [P, KT, HALF], F32R)
    q = sb("q", [P, KT, HALF])
    k = sb("k", [P, KVH, P + HALF])
    v = sb("v", [P, TT + 1, P])
    u = sb("u", [P, NG, HIST + HALF])
    pooled = sb("pooled", [P, NG, HALF])
    gate = sb("gate", [P, 4, HALF])
    raw = sb("raw_m", [P, RAW, SLOT])
    w_hi, w_lo = sb("w_hi_m", [P, SPLIT, SLOT], F32R), sb("w_lo_m", [P, SPLIT, SLOT], F32R)

    flat = rows[:].rearrange("p t n -> p (t n)")
    merged = flat.rearrange("p (m n) -> p m n", n=HALF)
    scores = flat[:, 0:1024].rearrange("p (b n) -> p b n", b=2)
    probs = flat[:, 1024:2560].rearrange("p (b n) -> p b n", b=3)
    probs_t = flat[:, 2560:3584].rearrange("p (b n) -> p b n", b=2)
    wide = gate[:].rearrange("p a n -> p (a n)")
    win = [wide[:, 0:HIST + HALF], wide[:, 1024:1024 + HIST + HALF]]

    sumsq, rms, rstd = sb("sumsq", [P, TT]), sb("rms", [P, TT]), sb("rstd", [P, TT])
    smax, negmax = sb("smax", [P, 2, 2]), sb("negmax", [P, 2, 2])
    sdiff, sexp = sb("sdiff", [P, 2, 2]), sb("sexp", [P, 2, 2])
    psum_row, den, rden = sb("prob_sum", [P, 2, 2]), sb("den", [P, 2, 2]), sb("rden", [P, 3, 2])
    logits = sb("logits", [P, TT, E])
    top, top_i, top_f = sb("top", [P, 8]), sb("top_i", [P, 8], U32), sb("top_f", [P, 8])
    neg_top, etop, esum, resum = sb("neg_top", [P, 1]), sb("etop", [P, TOPK]), sb("esum", [P, 1]), sb("resum", [P, 1])
    onehot, chosen = sb("onehot", [P, TOPK, E]), sb("chosen", [P, E])
    e_row, base = sb("e_row", [P, E]), sb("base", [P, E])
    slot_of, picked = sb("slot_of", [P, E]), sb("picked", [P, TOPK, E])
    dest_f, dest = sb("dest_f", [P, TOPK]), sb("dest", [P, TT, TOPK], I32)
    codes = sb("codes", [P, SEQ // P, 2 * TOPK], I32)
    half_codes = sb("half_codes", [P, TT, 2 * TOPK], I32)
    free_slots = sb("free_slots", [P, 2 * E * SLOTS_PER_EXPERT // P], I32)
    NX = (ROUNDS - 1) * E
    over, order, one_x, x_expert, x_base, x_pick = (wide[:, NX * i:NX * i + NX] for i in range(6))
    count = sb("count", [P, E])
    part1 = sb("part1", [P, 1])
    extra_f, items_f = sb("extra_f", [P, 2]), sb("items_f", [P, 1])
    extra_i, first_i = sb("extra_i", [P, 2], I32), sb("first_i", [P, 2], I32)

    const_loaded, pos_loaded, x_loaded = sem("const_loaded"), sem("pos_loaded"), sem("x_loaded")
    raw_loaded = [sem(f"raw_loaded{r}") for r in range(RAW)]
    ready_const, zeroed, table_free = sem("ready_const"), sem("zeroed"), sem("table_free")
    bias_t, bias_done = sem("bias_t"), sem("bias_done")
    angles, cs_ready, sumsq_done, ms_done, rms_done = sem("angles"), sem("cs_ready"), sem("sumsq_done"), sem("ms_done"), sem("rms_done")
    rows_done, h2_rows_done = sem("rows_done"), sem("h2_rows_done")
    hi_done, lo_done = sem("hi_done"), sem("lo_done")
    xt_ready, h_hi_done, h_lo_done = sem("xt_ready"), sem("h_hi_done"), sem("h_lo_done")
    proj_ready, proj_evac, v_evac = sem("proj_ready"), sem("proj_evac"), sem("v_evac")
    rope_ready, rope_done = sem("rope_ready"), sem("rope_done")
    scored, max_done, exp_done = sem("scored"), sem("max_done"), sem("exp_done")
    rden_done, scaled, pt_ready, pt_evac = sem("rden_done"), sem("scaled"), sem("pt_ready"), sem("pt_evac")
    pv_ready, o_evac = sem("pv_ready"), sem("o_evac")
    mix_ready, mix_evac = sem("mix_ready"), sem("mix_evac")
    gate_mm, gate_done, br_ready, merged_done = sem("gate_mm"), sem("gate_done"), sem("br_ready"), sem("merged_done")
    out_ready, x2_done, x2_stored, h2_stored = sem("out_ready"), sem("x2_done"), sem("x2_stored"), sem("h2_stored")
    h2t_evac, logits_ready, top_done, etop_done = sem("h2t_evac"), sem("logits_ready"), sem("top_done"), sem("etop_done")
    chosen_done, rank_ready, dest_done, scattered = sem("chosen_done"), sem("rank_ready"), sem("dest_done"), sem("scattered")
    codes_done, hist_done = sem("codes_done"), sem("hist_done")
    items_done, items_stored, items_loaded = sem("items_done"), sem("items_stored"), sem("items_loaded")
    vstep, pstep = sem("vstep"), sem("pstep")

    NPE = len(TILES) - 1
    evac_no = {ti: sum(t != "v" for t in TILES[:ti + 1]) for ti in range(len(TILES))}
    tile_slot = {0: 0, 1: 0, 2: 1, **{3 + i: 2 + i // 2 for i in range(8)}, **{11 + i: 6 + i // 2 for i in range(4)}}
    slot_last = {s: max(t for t, at in tile_slot.items() if at == s) for s in range(PROJ_SLOTS)}

    def cols(w, c0, n):
        return w.rearrange("(k p) n -> p k n", p=P)[:, :, c0:c0 + n]

    def slot_view(t, r, n):
        return t[:, r, :].rearrange("p (k n) -> p k n", n=n)

    loads = []
    dst = [slot_view(raw, r, 256) for r in range(RAW)]
    for s in range(MIX_SLOTS):
        d, r = dst[s % RAW], s % RAW
        if s == 0:
            loads.append([(d[:, :, 64 * i:64 * i + 64], cols(w_in, O_K + 64 * (i // 2), 64)) for i in range(4)])
        elif s == 1:
            loads.append([(raw[:, r, 0:1024].rearrange("p (k n) -> p k n", n=P), cols(w_in, O_V, P))])
        elif s < 6:
            loads.append([(d, cols(w_in, 256 * (s - 2), 256))])
        elif s < PROJ_SLOTS:
            loads.append([(d, cols(w_in, O_U + 256 * (s - 6), 256))])
        elif s < OUT0:
            m, branch = divmod(s - GATE0, 2)
            if branch:
                loads.append([(raw[:, r, 0:1024].rearrange("p (k n) -> p k n", n=P), cols(w_attn, P * m, P)),
                              (raw[:, r, 1024:1536].rearrange("p (k n) -> p k n", n=P), cols(w_pool, P * m, P))])
            else:
                loads.append([(d[:, :, 0:P], cols(w_in, O_GA + P * m, P)), (d[:, :, P:2 * P], cols(w_in, O_GP + P * m, P))])
        else:
            n, kh = divmod(s - OUT0, 2)
            loads.append([(slot_view(raw, r, 512), cols(w_o, 512 * n, 512)[:, 4 * kh:4 * kh + 4, :])])
    arrived, per_half = {}, [0] * RAW
    for s in range(MIX_SLOTS):
        per_half[s % RAW] += 16 * len(loads[s])
        arrived[s] = per_half[s % RAW]
    split_slots = list(range(PROJ_SLOTS)) + [GATE0 + 2 * m for m in range(KT)]

    def raw_arrived(eng, hf, s):
        eng.wait_ge(raw_loaded[s % RAW], hf * per_half[s % RAW] + arrived[s])

    block = scope.enter_context(nc.Block())

    @block.sync
    def _(sp):
        for hf in range(2):
            sp.wait_ge(x2_stored, hf * 16 * TT)
            sp.wait_ge(h2_rows_done, hf * TT)
            for t in range(TT):
                sp.dma_start(xs[:, t, :], x_rows.rearrange("(h t p) n -> h t p n", p=P, t=TT)[hf, t]).then_inc(x_loaded, 16)
            sp.wait_ge(angles, hf)
            sp.dma_start(pos_i[:], positions.rearrange("a (h n) -> a h n", n=HALF)[:, bass.ds(hf, 1), :].rearrange("a h n -> a (h n)").to_broadcast([P, HALF])).then_inc(pos_loaded, 16)
            for s in range(MIX_SLOTS):
                last = s - RAW
                if last < 0:
                    sp.wait_ge(out_ready, hf * 2 * TT)
                elif last in split_slots:
                    sp.wait_ge(lo_done, hf * SPLITS + split_slots.index(last) + 1)
                else:
                    sp.wait_ge(br_ready, hf * KT + (last - GATE0) // 2 + 1)
                for to, src in loads[s]:
                    sp.dma_start(to, src).then_inc(raw_loaded[s % RAW], 16)
        sp.wait_ge(items_done, 1)
        sp.dma_start(item_dram[0:E, :], first_i[0:E, :]).then_inc(items_stored, 16)
        sp.dma_start(item_dram[E:ITEM_ROW, :], extra_i[0:ITEM_ROW - E, :]).then_inc(items_stored, 16)
        sp.wait_ge(items_stored, 32)
        sp.dma_start(item_row[:], item_dram.rearrange("(a i) c -> a (i c)", a=1)).then_inc(items_loaded, 16)
        sp.wait_ge(items_loaded, 16)

    def hi_part(act, hf, si):
        s = split_slots[si]
        raw_arrived(act, hf, s)
        if si >= SPLIT:
            if si - SPLIT < PROJ_SLOTS:
                act.wait_ge(proj_ready, hf * len(TILES) + slot_last[si - SPLIT] + 1)
            else:
                act.wait_ge(gate_mm, hf * 2 * KT + 2 * (si - SPLIT - PROJ_SLOTS) + 2)
        n = 1024 if s == 1 else SLOT
        nc.scalar.activation(w_hi[:, si % SPLIT, 0:n], raw[:, s % RAW, 0:n], ACT.Copy).then_inc(hi_done, 1)

    def lo_part(dve, hf, si):
        s = split_slots[si]
        dve.wait_ge(hi_done, hf * SPLITS + si + 1)
        n = 1024 if s == 1 else SLOT
        nc.vector.tensor_tensor(w_lo[:, si % SPLIT, 0:n], raw[:, s % RAW, 0:n],
                                w_hi[:, si % SPLIT, 0:n].bitcast(F32), ALU.subtract).then_inc(lo_done, 1)

    @block.scalar
    def _(act):
        consts = [(ident[:], c_ident), (before[:], c_before), (swap[:], c_swap), (masks[:], c_masks),
                  (freq[:], c_freq), (fix[:], c_fix),
                  (g1_row[:], norm1_g[0:1, :].to_broadcast([P, D])), (g2_row[:], norm2_g[0:1, :].to_broadcast([P, D])),
                  (bv_row[:], b_in[0:1, O_V:O_U].to_broadcast([P, P])), (br_row[:], b_router[0:1, :].to_broadcast([P, E])),
                  (sinks[:], attn_sinks[0:1, :].to_broadcast([P, HEADS])),
                  (pool_mix[:], pool_w.rearrange("g c d -> c g d")),
                  (router[:], w_router.rearrange("(k p) e -> p k e", p=P))]
        for kv in range(KVH):
            for half in range(2):
                consts.append((bias_rows[kv:kv + 1, 64 * half:64 * half + 64], b_in[0:1, O_K + 64 * kv:O_K + 64 * kv + 64]))
        for at, c0, n in ((B_Q, 0, 8), (B_U, O_U, NG), (B_GA, O_GA, 8), (B_GP, O_GP, 8)):
            consts.append((bias_rows[at:at + n, :], b_in[0, c0:c0 + n * P].rearrange("(r c) -> r c", c=P)))
        consts.append((bias_rows[B_PS:NB, :], pool_scale[0, :].rearrange("(r c) -> r c", c=P)))
        assert len(consts) == N_CONSTS
        for to, src in consts:
            act.dma_start(to, src).then_inc(const_loaded, 16)
        act.wait_ge(bias_done, 1)

        def row_stats(hf, second):
            uses = 2 * hf + second
            for t in range(TT):
                if second:
                    act.wait_ge(x2_done, hf * 2 * TT + 2 * TT)
                else:
                    act.wait_ge(x_loaded, 16 * TT * hf + 16 * TT)
                    act.wait_ge(h2_stored, hf * 16 * TT)
                nc.scalar.activation(rows[:, t, :], xs[:, t, :], ACT.Square, accum_out=sumsq[:, t:t + 1]).then_inc(sumsq_done, 1)
            act.wait_ge(ms_done, uses + 1)
            nc.scalar.activation(rms[:], rms[:], ACT.Sqrt).then_inc(rms_done, 1)

        for hf in range(2):
            act.wait_ge(angles, hf + 1)
            nc.scalar.activation(sin[:], gate[:, 2, :], ACT.Sin)
            nc.scalar.activation(cos[:], gate[:, 3, :], ACT.Sin).then_inc(cs_ready, 1)
            row_stats(hf, 0)
            hi_part(act, hf, 0)
            hi_part(act, hf, 1)
            for kt in range(KT):
                act.wait_ge(xt_ready, hf * 2 * KT + kt + 1)
                nc.scalar.activation(h_hi[:, kt, :], ps[:, kt % 2, :], ACT.Copy).then_inc(h_hi_done, 1)
            for ti, name in enumerate(TILES):
                act.wait_ge(proj_ready, hf * len(TILES) + ti + 1)
                if name != "v":
                    kind, i = name[0], int(name[1:])
                    to, b = {"k": (k[:, i % 2, P:], i), "q": (q[:, i, :], B_Q + i),
                             "u": (u[:, i % NG, HIST:], B_U + i)}[kind]
                    if name == "u0":
                        act.wait_ge(hist_done, hf)
                    nc.scalar.activation(to, ps[:, ti % 2, :], ACT.Identity, bias=bias[:, b:b + 1]).then_inc(proj_evac, 1)
                s = tile_slot[ti]
                if ti == slot_last[s]:
                    hi_part(act, hf, s + 2)
            for n in range(UNITS + 2):
                if n < UNITS:
                    b = n % 2
                    act.wait_ge(max_done, hf * UNITS + n + 1)
                    if n >= 3:
                        act.wait_ge(pt_ready, hf * UNITS + n - 2)
                    for hh in range(2):
                        nc.scalar.activation(probs[:, n % 3, 256 * hh:256 * hh + 256], scores[:, b, 256 * hh:256 * hh + 256],
                                             ACT.Exp, bias=negmax[:, b, hh:hh + 1], scale=HD ** -0.5,
                                             accum_out=psum_row[:, b, hh:hh + 1])
                    nc.scalar.activation(sexp[:, b, :], sdiff[:, b, :], ACT.Exp, scale=HD ** -0.5).then_inc(exp_done, 1)
                if n >= 2:
                    act.wait_ge(pt_ready, hf * UNITS + n - 1)
                    if n >= 4:
                        act.wait_ge(pv_ready, hf * UNITS + n - 3)
                    nc.scalar.activation(probs_t[:, n % 2, :], ps[:, (6, 2)[n % 2], :], ACT.Copy).then_inc(pt_evac, 1)
            for m in range(KT):
                for j, b in ((0, B_GA), (1, B_GP)):
                    act.wait_ge(gate_mm, hf * 2 * KT + 2 * m + j + 1)
                    if m >= 2:
                        act.wait_ge(merged_done, hf * KT + m - 1)
                    if m == 0 and j == 0:
                        act.wait_ge(hist_done, hf + 1)
                    nc.scalar.activation(gate[:, 2 * (m % 2) + j, :], ps[:, 4 * (m % 2) + j, :], ACT.Sigmoid,
                                         bias=bias[:, b + m:b + m + 1]).then_inc(gate_done, 1)
                if PROJ_SLOTS + m + 2 < SPLITS:
                    hi_part(act, hf, PROJ_SLOTS + m + 2)
            row_stats(hf, 1)
            for kt in range(KT):
                act.wait_ge(xt_ready, hf * 2 * KT + KT + kt + 1)
                nc.scalar.activation(q[:, kt, :], ps[:, kt % 2, :], ACT.Copy).then_inc(h2t_evac, 1)
            for t in range(TT):
                act.wait_ge(top_done, hf * TT + t + 1)
                nc.scalar.activation(etop[:], top[:, 0:TOPK], ACT.Exp, bias=neg_top[:, 0:1], accum_out=esum[:, 0:1]).then_inc(etop_done, 1)

    @block.tensor
    def _(pe):
        pe.wait_ge(const_loaded, 16 * N_CONSTS)
        nc.tensor.transpose(ps[:, 0, 0:NB], bias_rows[:], ident[0:NB, 0:NB]).then_inc(bias_t, 1)
        pe.wait_ge(bias_done, 1)
        pe.wait_ge(ready_const, 1)

        def transposes(hf, second):
            for kt in range(KT):
                if second:
                    if kt == 0:
                        pe.wait_ge(h2_rows_done, hf * TT + TT)
                    if kt >= 2:
                        pe.wait_ge(h2t_evac, hf * KT + kt - 1)
                else:
                    if kt == 0:
                        pe.wait_ge(rows_done, hf * TT + TT)
                    if kt >= 2:
                        pe.wait_ge(h_lo_done, hf * KT + kt - 1)
                for t in range(TT):
                    ins = nc.tensor.transpose(ps[:, kt % 2, P * t:P * t + P], rows[:, t, P * kt:P * kt + P], ident[:])
                ins.then_inc(xt_ready, 1)

        def three_pass(to, pairs):
            n = len(pairs)
            for i, (whi, wlo, mhi, mlo) in enumerate(pairs):
                nc.tensor.matmul(to, whi, mhi, start=i == 0, stop=False)
                nc.tensor.matmul(to, whi, mlo, start=False, stop=False)
                ins = nc.tensor.matmul(to, wlo, mhi, start=False, stop=i == n - 1)
            return ins

        for hf in range(2):
            transposes(hf, 0)
            pe.wait_ge(h_lo_done, hf * KT + KT)

            def rope(ri):
                ti = ROPED[ri]
                src = k[:, ti, P:] if ti < 2 else q[:, ti - 3, :]
                pe.wait_ge(proj_evac, hf * NPE + evac_no[ti])
                if ri >= 2:
                    pe.wait_ge(rope_done, hf * len(ROPED) + ri - 1)
                nc.tensor.matmul(ps[:, 2 + ri % 2, :], swap[:], src, start=True, stop=True).then_inc(rope_ready, 1)

            roped = 0
            for ti, name in enumerate(TILES):
                s = tile_slot[ti]
                pe.wait_ge(lo_done, hf * SPLITS + s + 1)
                if ti - 2 == 2:
                    pe.wait_ge(v_evac, hf + 1)
                elif ti >= 2:
                    pe.wait_ge(proj_evac, hf * NPE + evac_no[ti - 2])
                r = s % SPLIT
                if name == "v":
                    whi = w_hi[:, r, 0:1024].rearrange("p (k n) -> p k n", n=P)
                    wlo = w_lo[:, r, 0:1024].rearrange("p (k n) -> p k n", n=P)
                    for t in range(TT):
                        at = slice(P * t, P * t + P)
                        ins = three_pass(ps[:, ti % 2, at],
                                         [(h_hi[:, kt, at], h_lo[:, kt, at], whi[:, kt, :], wlo[:, kt, :]) for kt in range(KT)])
                else:
                    c = P * (ti - min(t for t, at in tile_slot.items() if at == s))
                    whi, wlo = slot_view(w_hi, r, 256), slot_view(w_lo, r, 256)
                    ins = three_pass(ps[:, ti % 2, :],
                                     [(whi[:, kt, c:c + P], wlo[:, kt, c:c + P], h_hi[:, kt, :], h_lo[:, kt, :]) for kt in range(KT)])
                ins.then_inc(proj_ready, 1)
                while roped < len(ROPED) and ROPED[roped] < ti:
                    rope(roped)
                    roped += 1
            pe.wait_ge(rope_done, hf * len(ROPED) + len(ROPED))
            pe.wait_ge(v_evac, hf + 1)
            pe.wait_ge(proj_evac, hf * NPE + NPE)
            for n in range(UNITS + 3):
                if n < UNITS:
                    b, p = divmod(n, HEADS // 2)
                    if n >= 2:
                        pe.wait_ge(max_done, hf * UNITS + n - 1)
                    for hh in range(2):
                        at = slice(64 * hh, 64 * hh + 64)
                        ins = nc.tensor.matmul(ps[:, (4, 0)[n % 2] + hh, 0:256], q[at, p, P * b:P * b + P],
                                               k[at, p // 4, P * b:P * b + 2 * P], start=True, stop=True)
                    ins.then_inc(scored, 1)
                if 2 <= n < UNITS + 2:
                    m = n - 2
                    pe.wait_ge(scaled, hf * UNITS + m + 1)
                    if m >= 2:
                        pe.wait_ge(pt_evac, hf * UNITS + m - 1)
                    for kk in range(2):
                        for hh in range(2):
                            c = P * (2 * kk + hh)
                            ins = nc.tensor.transpose(ps[:, (6, 2)[m % 2], c:c + P],
                                                      probs[:, m % 3, 256 * hh + P * kk:256 * hh + P * kk + P], ident[:])
                    ins.then_inc(pt_ready, 1)
                if n >= 3:
                    m = n - 3
                    b, p = divmod(m, HEADS // 2)
                    pe.wait_ge(pt_evac, hf * UNITS + m + 1)
                    if m >= 2:
                        pe.wait_ge(o_evac, hf * UNITS + m - 1)
                    for hh in range(2):
                        for kk in range(2):
                            c = P * (2 * kk + hh)
                            ins = nc.tensor.matmul(ps[64 * hh:64 * hh + 64, (7, 3)[m % 2], 0:P],
                                                   v[:, b + kk, 64 * (p // 4):64 * (p // 4) + 64],
                                                   probs_t[:, m % 2, c:c + P], start=kk == 0, stop=kk == 1)
                    ins.then_inc(pv_ready, 1)
            pe.wait_ge(hist_done, hf + 1)
            for g in range(NG):
                nc.tensor.matmul(ps[:, (0, 1, 4, 5)[g], :], pool_mix[:, g, :], pooled[:, g, :], start=True, stop=True).then_inc(mix_ready, 1)
            pe.wait_ge(mix_evac, hf * NG + NG)
            pe.wait_ge(o_evac, hf * UNITS + UNITS)
            for m in range(KT):
                si = PROJ_SLOTS + m
                bank = 4 * (m % 2)
                pe.wait_ge(lo_done, hf * SPLITS + si + 1)
                if m >= 2:
                    pe.wait_ge(merged_done, hf * KT + m - 1)
                whi, wlo = slot_view(w_hi, si % SPLIT, 256), slot_view(w_lo, si % SPLIT, 256)
                for j in range(2):
                    c = P * j
                    three_pass(ps[:, bank + j, :], [(whi[:, kt, c:c + P], wlo[:, kt, c:c + P], h_hi[:, kt, :], h_lo[:, kt, :])
                                                    for kt in range(KT)]).then_inc(gate_mm, 1)
                s = GATE0 + 2 * m + 1
                raw_arrived(pe, hf, s)
                wa = raw[:, s % RAW, :].rearrange("p (k n) -> p k n", n=P)
                for kt in range(KT):
                    nc.tensor.matmul(ps[:, bank + 2, :], wa[:, kt, :], q[:, kt, :], start=kt == 0, stop=kt == KT - 1)
                for g in range(NG):
                    ins = nc.tensor.matmul(ps[:, bank + 3, :], wa[:, KT + g, :], pooled[:, g, :], start=g == 0, stop=g == NG - 1)
                ins.then_inc(br_ready, 1)
            pe.wait_ge(merged_done, hf * KT + KT)
            for n in range(2):
                for kh in range(2):
                    raw_arrived(pe, hf, OUT0 + 2 * n + kh)
                for t in range(TT):
                    for kt in range(KT):
                        s = OUT0 + 2 * n + kt // 4
                        ins = nc.tensor.matmul(ps[:, n * TT + t, :], merged[:, kt, P * t:P * t + P],
                                               slot_view(raw, s % RAW, 512)[:, kt % 4, :], start=kt == 0, stop=kt == KT - 1)
                    ins.then_inc(out_ready, 1)
            pe.wait_ge(x2_done, hf * 2 * TT + 2 * TT)
            transposes(hf, 1)
            pe.wait_ge(h2t_evac, hf * KT + KT)
            for t in range(TT):
                for kt in range(KT):
                    ins = nc.tensor.matmul(ps[:, 2, E * t:E * t + E], q[:, kt, P * t:P * t + P], router[:, kt, :],
                                           start=kt == 0, stop=kt == KT - 1)
            ins.then_inc(logits_ready, 1)
            for t in range(TT):
                pe.wait_ge(chosen_done, hf * TT + t + 1)
                nc.tensor.matmul(ps[:, 3, 0:E], before[:], chosen[:], start=True, stop=True)
                nc.tensor.matmul(ps[:, 3, E:2 * E], ones[:], chosen[:], start=True, stop=True).then_inc(rank_ready, 1)

    @block.gpsimd
    def _(pool):
        pool.memset(ones[:], 1.0)
        pool.iota(e_row[:], pattern=[[1, E]], base=0, channel_multiplier=0, allow_small_or_imprecise_dtypes=True)
        pool.iota(base[:], pattern=[[SLOTS_PER_EXPERT, E]], base=0, channel_multiplier=0, allow_small_or_imprecise_dtypes=True)
        pool.iota(part1[:], pattern=[[0, 1]], base=1, channel_multiplier=1, allow_small_or_imprecise_dtypes=True)
        pool.iota(first_i[:, 0:1], pattern=[[0, 1]], base=0, channel_multiplier=1)
        pool.iota(first_i[:, 1:2], pattern=[[0, 1]], base=0, channel_multiplier=SLOTS_PER_EXPERT)
        codes4 = codes[:].rearrange("p t (k c) -> p t k c", c=2)
        pool.iota(codes4[:, :, :, 0], pattern=[[P, SEQ // P], [SEQ, TOPK]], base=0, channel_multiplier=1)
        pool.iota(codes4[:, :, :, 1], pattern=[[P, SEQ // P], [0, TOPK]], base=0, channel_multiplier=1)
        free2 = free_slots[:].rearrange("p (s c) -> p s c", c=2)
        pool.memset(free2[:, :, 0:1], FREE_CODE)
        pool.memset(free2[:, :, 1:2], 0)
        pool.memset(k[:, :, 0:P], 0.0)
        pool.memset(v[:, 0, :], 0.0)
        pool.memset(u[:, :, 0:HIST], 0.0).then_inc(ready_const, 1)
        pool.wait_ge(ready_const, 1)
        pool.dma_start(slot_dram.rearrange("(p s) c -> p (s c)", p=P), free_slots[:]).then_inc(table_free, 16)
        pool.wait_ge(const_loaded, 16 * N_CONSTS)
        for hf in range(2):
            st = Steps(pool, pstep, hf * MIX_POOL_STEPS)
            pool.wait_ge(scattered, hf * 16 * TT * TOPK)
            nc.gpsimd.tensor_copy(half_codes[:], codes[:, bass.ds(hf * TT, TT), :]).then_inc(codes_done, 1)
            pool.wait_ge(proj_evac, hf * NPE + NPE)
            pool.wait_ge(rope_done, hf * len(ROPED) + len(ROPED))
            pool.wait_ge(merged_done, hf * KT)
            for g, w in enumerate(POOL_WINDOWS):
                src, n = u[:, g, :], 1
                i = 0
                while n < w:
                    lo = 2 * n - 1
                    st.link(nc.gpsimd.tensor_tensor(win[i % 2][:, lo:], src[:, lo:], src[:, lo - n:HIST + HALF - n], ALU.add))
                    src, n, i = win[i % 2], 2 * n, i + 1
                st.link(nc.gpsimd.tensor_scalar(pooled[:, g, :], src[:, HIST:], 1.0 / w, None, ALU.mult))
                st.link(nc.gpsimd.tensor_tensor(pooled[:, g, 0:HIST], pooled[:, g, 0:HIST],
                                                fix[:, bass.ds(hf, 1), HIST * g:HIST * g + HIST].rearrange("p a n -> p (a n)"), ALU.mult))
                st.link(nc.gpsimd.tensor_tensor(pooled[:, g, :], pooled[:, g, :], u[:, g, HIST:], ALU.subtract))
            nc.gpsimd.tensor_copy(u[:, :, 0:HIST], u[:, :, HALF:HALF + HIST]).then_inc(hist_done, 1)
            for n in range(UNITS):
                pool.wait_ge(rden_done, hf * UNITS + n + 1)
                for hh in range(2):
                    pr = probs[:, n % 3, 256 * hh:256 * hh + 256]
                    ins = nc.gpsimd.tensor_scalar(pr, pr, rden[:, n % 3, hh:hh + 1], None, ALU.mult)
                ins.then_inc(scaled, 1)
            assert st.n == MIX_POOL_STEPS, st.n
            x2_half = x2_dram.rearrange("(h t p) n -> h t p n", p=P, t=TT)
            h2_half = h2_dram.rearrange("(h t p) n -> h t p n", p=P, t=TT)
            pool.wait_ge(x2_done, hf * 2 * TT + 2 * TT)
            for t in range(TT):
                pool.dma_start(x2_half[hf, t], xs[:, t, :]).then_inc(x2_stored, 16)
            for t in range(TT):
                pool.wait_ge(h2_rows_done, hf * TT + t + 1)
                pool.dma_start(h2_half[hf, t], rows[:, t, :]).then_inc(h2_stored, 16)
            pool.wait_ge(table_free, 16)
            pool.wait_ge(codes_done, hf + 1)
            for t in range(TT):
                pool.wait_ge(dest_done, hf * TT + t + 1)
                for c in range(TOPK):
                    pool.indirect_dma_start(slot_dram, bass.IndirectOffsetOnAxis(ap=dest[:, t, c:c + 1].bitcast(U32), axis=0),
                                            half_codes[:, t, 2 * c:2 * c + 2], None).then_inc(scattered, 16)
        pool.wait_ge(merged_done, 2 * KT)
        pool.memset(one_x, 1.0)
        pool.iota(x_expert, pattern=[[0, ROUNDS - 1], [1, E]], base=0, channel_multiplier=0, allow_small_or_imprecise_dtypes=True)
        pool.iota(x_base, pattern=[[ITEM, ROUNDS - 1], [SLOTS_PER_EXPERT, E]], base=ITEM, channel_multiplier=0, allow_small_or_imprecise_dtypes=True).then_inc(ready_const, 1)
        pool.wait_ge(scattered, 2 * 16 * TT * TOPK)
        pool.wait_ge(x2_stored, 2 * 16 * TT)
        pool.wait_ge(h2_stored, 2 * 16 * TT)

    @block.vector
    def _(dve):
        dve.wait_ge(bias_t, 1)
        nc.vector.tensor_copy(bias[:], ps[:, 0, 0:NB])
        nc.vector.tensor_scalar(sinks8[:], sinks[:], float(HD) ** 0.5, None, ALU.mult).then_inc(bias_done, 1)
        dve.wait_ge(bias_done, 1)
        dve.wait_ge(ready_const, 1)
        c1, c2, c3 = cut_pi()
        MAGIC = 1.5 * 2.0**23
        PI = float(np.float32(3.1415925))

        for hf in range(2):
            st = Steps(dve, vstep, hf * MIX_VECTOR_STEPS)

            def normalise(second, g_row, done):
                dve.wait_ge(sumsq_done, hf * 2 * TT + TT * second + TT)
                nc.vector.tensor_scalar(rms[:], sumsq[:], 1.0 / D, EPS, ALU.mult, ALU.add).then_inc(ms_done, 1)
                dve.wait_ge(rms_done, hf * 2 + second + 1)
                st.link(nc.vector.reciprocal(rstd[:], rms[:]))
                for t in range(TT):
                    nc.vector.scalar_tensor_tensor(rows[:, t, :], xs[:, t, :], rstd[:, t:t + 1], g_row[:], ALU.mult, ALU.mult).then_inc(done, 1)

            dve.wait_ge(pos_loaded, 16 * hf + 16)
            a, n_, s_, c_ = (gate[:, i, :] for i in range(4))
            st.link(nc.vector.tensor_scalar(a, pos_i[:], freq[:, 0:1], None, ALU.mult))
            st.link(nc.vector.tensor_scalar(n_, a, 1.0 / (2 * np.pi), MAGIC, ALU.mult, ALU.add))
            st.link(nc.vector.tensor_scalar(n_, n_, -MAGIC, None, ALU.add))
            for c in (c1, c2, c3):
                st.link(nc.vector.scalar_tensor_tensor(a, n_, -c, a, ALU.mult, ALU.add))
            nc.vector.tensor_scalar(s_, a, PI, -PI, ALU.min, ALU.max)
            st.link(nc.vector.tensor_scalar(c_, a, np.pi / 2, None, ALU.add))
            st.link(nc.vector.tensor_scalar(n_, c_, np.pi, -2 * np.pi, ALU.is_gt, ALU.mult))
            st.link(nc.vector.tensor_tensor(c_, c_, n_, ALU.add))
            nc.vector.tensor_scalar(c_, c_, PI, -PI, ALU.min, ALU.max).then_inc(angles, 1)

            normalise(0, g1_row, rows_done)
            lo_part(dve, hf, 0)
            lo_part(dve, hf, 1)
            for kt in range(KT):
                dve.wait_ge(h_hi_done, hf * KT + kt + 1)
                nc.vector.tensor_tensor(h_lo[:, kt, :], ps[:, kt % 2, :], h_hi[:, kt, :].bitcast(F32), ALU.subtract).then_inc(h_lo_done, 1)
            dve.wait_ge(cs_ready, hf + 1)
            for ti, name in enumerate(TILES):
                if name == "v":
                    dve.wait_ge(proj_ready, hf * len(TILES) + ti + 1)
                    nc.vector.tensor_tensor(v[:, 1:, :], ps[:, ti % 2, :].rearrange("p (t n) -> p t n", n=P),
                                            bv_row[:].unsqueeze(1).to_broadcast([P, TT, P]), ALU.add).then_inc(v_evac, 1)
                elif ti in ROPED:
                    ri = ROPED.index(ti)
                    qt = k[:, ti, P:] if ti < 2 else q[:, ti - 3, :]
                    dve.wait_ge(rope_ready, hf * len(ROPED) + ri + 1)
                    nc.vector.tensor_tensor(gate[:, 0, :], ps[:, 2 + ri % 2, :], sin[:], ALU.mult)
                    st.link(nc.vector.tensor_tensor(qt, qt, cos[:], ALU.mult))
                    nc.vector.tensor_tensor(qt, qt, gate[:, 0, :], ALU.add).then_inc(rope_done, 1)
                    dve.wait_ge(rope_done, hf * len(ROPED) + ri + 1)
                s = tile_slot[ti]
                if ti == slot_last[s]:
                    lo_part(dve, hf, s + 2)
            for n in range(UNITS + 3):
                if n < UNITS:
                    b, (blk, p) = n % 2, divmod(n, HEADS // 2)
                    dve.wait_ge(scored, hf * UNITS + n + 1)
                    if n >= 2:
                        dve.wait_ge(exp_done, hf * UNITS + n - 1)
                    mask = masks[:, min(blk, 1), :]
                    for hh in range(2):
                        at = slice(256 * hh, 256 * hh + 256)
                        ins = nc.vector.tensor_tensor_reduce(out=scores[:, b, at], in0=ps[:, (4, 0)[b] + hh, 0:256], in1=mask, scale=1.0,
                                                             scalar=-3e38, op0=ALU.add, op1=ALU.max, accum_out=smax[:, b, hh:hh + 1])
                    st.link(ins)
                    snk = sinks8[:, 2 * p:2 * p + 2]
                    st.link(nc.vector.tensor_tensor(smax[:, b, :], smax[:, b, :], snk, ALU.max))
                    nc.vector.tensor_scalar(negmax[:, b, :], smax[:, b, :], -(HD ** -0.5), None, ALU.mult)
                    nc.vector.tensor_tensor(sdiff[:, b, :], snk, smax[:, b, :], ALU.subtract).then_inc(max_done, 1)
                if 1 <= n <= UNITS:
                    m = n - 1
                    b = m % 2
                    dve.wait_ge(exp_done, hf * UNITS + m + 1)
                    st.link(nc.vector.tensor_tensor(den[:, b, :], psum_row[:, b, :], sexp[:, b, :], ALU.add))
                    if m >= 3:
                        dve.wait_ge(scaled, hf * UNITS + m - 2)
                    nc.vector.reciprocal(rden[:, m % 3, :], den[:, b, :]).then_inc(rden_done, 1)
                if n >= 3:
                    m = n - 3
                    blk, p = divmod(m, HEADS // 2)
                    dve.wait_ge(pv_ready, hf * UNITS + m + 1)
                    nc.vector.tensor_copy(q[:, p, P * blk:P * blk + P], ps[:, (7, 3)[m % 2], 0:P]).then_inc(o_evac, 1)
            nc.vector.tensor_copy(k[:, :, 0:P], k[:, :, HALF:])
            nc.vector.tensor_copy(masks[:, 0, :], masks[:, 1, :])
            nc.vector.tensor_copy(v[:, 0, :], v[:, TT, :])
            for g in range(NG):
                dve.wait_ge(mix_ready, hf * NG + g + 1)
                nc.vector.tensor_scalar(pooled[:, g, :], ps[:, (0, 1, 4, 5)[g], :], bias[:, B_PS + g:B_PS + g + 1], None, ALU.mult).then_inc(mix_evac, 1)
            for m in range(KT):
                bank, g2 = 4 * (m % 2), 2 * (m % 2)
                dve.wait_ge(gate_done, hf * 2 * KT + 2 * m + 2)
                dve.wait_ge(br_ready, hf * KT + m + 1)
                nc.vector.tensor_tensor(gate[:, g2, :], ps[:, bank + 2, :], gate[:, g2, :], ALU.mult)
                st.link(nc.vector.tensor_tensor(gate[:, g2 + 1, :], ps[:, bank + 3, :], gate[:, g2 + 1, :], ALU.mult))
                nc.vector.tensor_tensor(merged[:, m, :], gate[:, g2, :], gate[:, g2 + 1, :], ALU.add).then_inc(merged_done, 1)
                if PROJ_SLOTS + m + 2 < SPLITS:
                    lo_part(dve, hf, PROJ_SLOTS + m + 2)
            for n in range(2):
                for t in range(TT):
                    dve.wait_ge(out_ready, hf * 2 * TT + n * TT + t + 1)
                    part = xs[:, t, 512 * n:512 * n + 512]
                    nc.vector.tensor_tensor(part, ps[:, n * TT + t, :], part, ALU.add).then_inc(x2_done, 1)
            dve.wait_ge(x2_done, hf * 2 * TT + 2 * TT)
            normalise(1, g2_row, h2_rows_done)

            dve.wait_ge(logits_ready, hf + 1)
            st.link(nc.vector.tensor_tensor(logits[:], ps[:, 2, 0:TT * E].rearrange("p (t e) -> p t e", e=E),
                                            br_row[:].unsqueeze(1).to_broadcast([P, TT, E]), ALU.add))
            dve.wait_ge(scattered, hf * 16 * TT * TOPK)
            for t in range(TT):
                tile_at = bass.ds(hf * TT + t, 1)
                g_t = gates[:, tile_at, :].rearrange("p a k -> p (a k)")
                of_t = gate_of[:, tile_at, :].rearrange("p a e -> p (a e)")
                st.link(nc.vector.max(top[:], logits[:, t, :]))
                nc.vector.tensor_scalar(neg_top[:], top[:, 0:1], -1.0, None, ALU.mult).then_inc(top_done, 1)
                st.link(nc.vector.max_index(top_i[:], top[:], logits[:, t, :]))
                st.link(nc.vector.tensor_copy(top_f[:], top_i[:]))
                for c in range(TOPK):
                    ins = nc.vector.tensor_scalar(onehot[:, c, :], e_row[:], top_f[:, c:c + 1], None, ALU.is_equal)
                st.link(ins)
                nc.vector.reduce_sum(chosen[:], onehot[:].rearrange("p k e -> p e k"), AX_X).then_inc(chosen_done, 1)
                dve.wait_ge(etop_done, hf * TT + t + 1)
                st.link(nc.vector.reciprocal(resum[:], esum[:]))
                st.link(nc.vector.tensor_scalar(g_t, etop[:], resum[:, 0:1], None, ALU.mult))
                st.link(nc.vector.tensor_tensor(picked[:], onehot[:], g_t.unsqueeze(2).to_broadcast([P, TOPK, E]), ALU.mult))
                st.link(nc.vector.reduce_sum(of_t, picked[:].rearrange("p k e -> p e k"), AX_X))
                dve.wait_ge(rank_ready, hf * TT + t + 1)
                st.link(nc.vector.tensor_tensor(slot_of[:], ps[:, 3, 0:E], base[:], ALU.add))
                nc.vector.tensor_tensor(base[:], ps[:, 3, E:2 * E], base[:], ALU.add)
                st.link(nc.vector.tensor_tensor(picked[:], onehot[:], slot_of[:].unsqueeze(1).to_broadcast([P, TOPK, E]), ALU.mult))
                st.link(nc.vector.reduce_sum(dest_f[:], picked[:], AX_X))
                nc.vector.tensor_copy(dest[:, t, :], dest_f[:]).then_inc(dest_done, 1)
                dve.wait_ge(dest_done, hf * TT + t + 1)
            assert st.n == MIX_VECTOR_STEPS, st.n

        st = Steps(dve, vstep, 2 * MIX_VECTOR_STEPS)
        dve.wait_ge(ready_const, 2)
        st.link(nc.vector.scalar_tensor_tensor(count[:], e_row[:], float(-SLOTS_PER_EXPERT), base[:], ALU.mult, ALU.add))
        for r in range(1, ROUNDS):
            ins = nc.vector.tensor_scalar(over[:, E * (r - 1):E * r], count[:], float(ITEM * r), None, ALU.is_gt)
        st.link(ins)
        st.link(nc.vector.tensor_tensor_scan(order, one_x, over, 0.0, ALU.mult, ALU.add))
        st.link(nc.vector.tensor_scalar(items_f[:], order[:, NX - 1:NX], float(E), None, ALU.add))
        nc.vector.tensor_copy(n_items[:], items_f[:])
        st.link(nc.vector.tensor_scalar(x_pick, order, part1[:, 0:1], None, ALU.is_equal))
        st.link(nc.vector.tensor_tensor(x_pick, x_pick, over, ALU.mult))
        nc.vector.tensor_tensor(x_expert, x_expert, x_pick, ALU.mult)
        st.link(nc.vector.tensor_tensor(x_base, x_base, x_pick, ALU.mult))
        nc.vector.reduce_sum(extra_f[:, 0:1], x_expert, AX_X)
        st.link(nc.vector.reduce_sum(extra_f[:, 1:2], x_base, AX_X))
        nc.vector.tensor_copy(extra_i[:], extra_f[:]).then_inc(items_done, 1)


RAW_E, SPLIT_E, LEAD = 4, 4, 3


def experts(nc, scope, keep, w_up, b_up, w_down, h2_dram, y_dram, slot_dram):
    def sb(name, shape, dt=F32):
        return scope.enter_context(nc.sbuf_tensor(name, shape, dt))

    def sem(name):
        return scope.enter_context(nc.semaphore(name))

    ps, ident, item_row, n_items = keep["ps"], keep["ident"], keep["item_row"], keep["n_items"]
    raw = sb("raw_e", [P, RAW_E, SLOT])
    w_hi, w_lo = sb("w_hi_e", [P, SPLIT_E, SLOT], F32R), sb("w_lo_e", [P, SPLIT_E, SLOT], F32R)
    fetched = sb("fetched", [SUB, 2, 2], I32)
    in_work = sb("in_work", [SUB, 2, 2], I32)
    tokens = sb("tokens", [SUB, 2, D])
    xt_hi, xt_lo = sb("xt_hi", [P, KT, ITEM], F32R), sb("xt_lo", [P, KT, ITEM], F32R)
    a_hi, a_lo = sb("a_hi", [P, KT, ITEM], F32R), sb("a_lo", [P, KT, ITEM], F32R)
    glu, lin, sig = sb("glu", [P, 2, ITEM]), sb("lin", [P, 2, ITEM]), sb("sig", [P, 2, ITEM])
    act_out = sb("act_out", [P, 2, 2, ITEM])
    y = sb("y", [SUB, 2, D])
    bup_rows, bup_t = sb("bup_rows", [E, 2 * DFF]), sb("bup_t", [P, 2 * KT, E])
    bup = sb("bup", [P, 2, 2 * KT])

    raw_loaded = [sem(f"raw_loaded_e{r}") for r in range(RAW_E)]
    bup_loaded, bup_tr, bup_ready = sem("bup_loaded"), sem("bup_tr"), sem("bup_ready")
    fetch, copied, gathered, y_scattered = sem("fetch"), sem("copied"), sem("gathered"), sem("y_scattered")
    hi_done, lo_done, slot_used = sem("hi_done_e"), sem("lo_done_e"), sem("slot_used")
    xt_ready, xt_hi_done, xt_lo_done = sem("xt_ready_e"), sem("xt_hi_done"), sem("xt_lo_done")
    up_read, glu_done, sig_done, act_done, a_hi_done, a_lo_done = (
        sem("up_read"), sem("glu_done"), sem("sig_done"), sem("act_done"), sem("a_hi_done"), sem("a_lo_done"))
    bias_picked = sem("bias_picked")
    y_evac_s, y_evac_v = sem("y_evac_s"), sem("y_evac_v")
    vstep = sem("vstep_e")
    ticked = sem("ticked")

    XT = [(0, 0, 3), (1, 3, 3), (2, 6, 2)]
    QUARTERS = 4
    VSTEPS = QUARTERS

    block = scope.enter_context(nc.Block())

    def n_of(eng):
        return eng.value_load(n_items[0:1, 0:1], min_val=E, max_val=MAX_ITEMS)

    @block.sync
    def _(sp):
        sp.dma_start(bup_rows[:], b_up).then_inc(bup_loaded, 16)

        def load(s, e, item):
            r = s % RAW_E
            if s < UP_SLOTS:
                quarter, which = divmod(s, 2)
                src = w_up[e].rearrange("a (k p) n -> p (a k) n", p=P)[:, :, DFF * which + 256 * quarter:DFF * which + 256 * quarter + 256]
                to = raw[:, r, :].rearrange("p (k n) -> p k n", n=256)
            else:
                d = s - UP_SLOTS
                src = w_down[e].rearrange("a (k p) n -> p (a k) n", p=P)[:, 2 * d:2 * d + 2, :]
                to = raw[:, r, :].rearrange("p (k n) -> p k n", n=D)
            sp.dma_start(to, src).then_inc(raw_loaded[r], 16)

        n = n_of(sp)
        with sp.Fori(0, n) as item:
            e = sp.value_load(item_row[0:1, bass.ds(2 * item, 1)], min_val=0, max_val=E - 1)
            for s in range(ITEM_SLOTS):
                if s < RAW_E:
                    if s == 0:
                        sp.wait_ge(lo_done, item * ITEM_SLOTS)
                    else:
                        sp.wait_ge(lo_done, item * ITEM_SLOTS)
                else:
                    sp.wait_ge(lo_done, item * ITEM_SLOTS + s - RAW_E + 1)
                load(s, bass.ds(e, 1), item)
        for s in range(LEAD):
            sp.wait_ge(lo_done, n * ITEM_SLOTS)
            load(s, bass.ds(0, 1), 0)

    def hi_part(act, item, s, ahead):
        it = item + ahead if ahead else item
        act.wait_ge(raw_loaded[s % RAW_E], it * (16 * ITEM_SLOTS // RAW_E) + 16 * (s // RAW_E) + 16)
        if s >= SPLIT_E:
            act.wait_ge(slot_used, it * ITEM_SLOTS + s - SPLIT_E + 1)
        elif ahead:
            act.wait_ge(slot_used, item * ITEM_SLOTS + ITEM_SLOTS + s - SPLIT_E + 1)
        elif s == SPLIT_E - 1 and LEAD == SPLIT_E - 1:
            act.wait_ge(slot_used, item * ITEM_SLOTS)
        nc.scalar.activation(w_hi[:, s % SPLIT_E, :], raw[:, s % RAW_E, :], ACT.Copy).then_inc(hi_done, 1)

    def lo_part(dve, item, s, ahead):
        it = item + ahead if ahead else item
        dve.wait_ge(hi_done, it * ITEM_SLOTS + s + 1)
        nc.vector.tensor_tensor(w_lo[:, s % SPLIT_E, :], raw[:, s % RAW_E, :], w_hi[:, s % SPLIT_E, :].bitcast(F32),
                                ALU.subtract).then_inc(lo_done, 1)

    def xt_flat(t, k0, nk):
        return t[:, k0:k0 + nk, :].rearrange("p k n -> p (k n)")

    def xt_hi_part(act, item):
        for i, (bank, k0, nk) in enumerate(XT):
            act.wait_ge(xt_ready, item * 3 + i + 1)
            nc.scalar.activation(xt_flat(xt_hi, k0, nk), ps[:, bank, 0:nk * ITEM], ACT.Copy).then_inc(xt_hi_done, 1)

    def xt_lo_part(dve, item):
        for i, (bank, k0, nk) in enumerate(XT):
            dve.wait_ge(xt_hi_done, item * 3 + i + 1)
            nc.vector.tensor_tensor(xt_flat(xt_lo, k0, nk), ps[:, bank, 0:nk * ITEM], xt_flat(xt_hi, k0, nk).bitcast(F32),
                                    ALU.subtract).then_inc(xt_lo_done, 1)

    @block.scalar
    def _(act):
        n = n_of(act)
        for s in range(LEAD):
            hi_part(act, 0, s, 0)
        xt_hi_part(act, 0)
        with act.Fori(0, n) as item:
            for s in range(ITEM_SLOTS):
                hi_part(act, item, (s + LEAD) % ITEM_SLOTS, (s + LEAD) // ITEM_SLOTS)
                if s < UP_SLOTS and s % 2:
                    j = s // 2
                    act.wait_ge(glu_done, item * QUARTERS + j + 1)
                    nc.scalar.activation(sig[:], glu[:], ACT.Sigmoid, scale=ALPHA).then_inc(sig_done, 1)
                    act.wait_ge(act_done, item * QUARTERS + j + 1)
                    nc.scalar.activation(a_hi[:, 2 * j:2 * j + 2, :], act_out[:, j % 2], ACT.Copy).then_inc(a_hi_done, 1)
                if s == UP_SLOTS:
                    xt_hi_part(act, item + 1)
            act.wait_ge(slot_used, item * ITEM_SLOTS + ITEM_SLOTS)
            act.wait_ge(y_scattered, item * 32)
            for c in range(2):
                nc.scalar.activation(y[:, 0, 512 * c:512 * c + 512], ps[0:SUB, 4 + c, :], ACT.Copy).then_inc(y_evac_s, 1)

    @block.vector
    def _(dve):
        n = n_of(dve)
        dve.wait_ge(bup_tr, 1)
        nc.vector.tensor_copy(bup_t[:, 0:KT, :], ps[:, 0, 0:KT * E].rearrange("p (m e) -> p m e", e=E)).then_inc(bup_ready, 1)
        nc.vector.tensor_scalar(bup_t[:, KT:, :], ps[:, 0, KT * E:2 * KT * E].rearrange("p (m e) -> p m e", e=E), 1.0, None,
                                ALU.add).then_inc(bup_ready, 1)
        dve.wait_ge(bup_ready, 2)
        for s in range(LEAD):
            lo_part(dve, 0, s, 0)
        xt_lo_part(dve, 0)
        with dve.Fori(0, n) as item:
            st = Steps(dve, vstep, item * VSTEPS)
            e = dve.value_load(item_row[0:1, bass.ds(2 * item, 1)], min_val=0, max_val=E - 1)
            nc.vector.tensor_copy(bup[:, 0, :], bup_t[:, :, bass.ds(e, 1)].rearrange("p m a -> p (m a)")).then_inc(bias_picked, 1)
            dve.wait_ge(bias_picked, item + 1)
            for s in range(ITEM_SLOTS):
                lo_part(dve, item, (s + LEAD) % ITEM_SLOTS, (s + LEAD) // ITEM_SLOTS)
                if s < UP_SLOTS and s % 2:
                    j = s // 2
                    bank = 2 * (j % 2)
                    dve.wait_ge(slot_used, item * ITEM_SLOTS + s + 1)
                    for c in range(2):
                        ins = nc.vector.tensor_scalar(glu[:, c, :], ps[:, bank, ITEM * c:ITEM * c + ITEM],
                                                      bup[:, 0, 2 * j + c:2 * j + c + 1], LIMIT, ALU.add, ALU.min)
                    ins.then_inc(glu_done, 1)
                    for c in range(2):
                        ins = nc.vector.tensor_scalar(lin[:, c, :], ps[:, bank + 1, ITEM * c:ITEM * c + ITEM],
                                                      bup[:, 0, KT + 2 * j + c:KT + 2 * j + c + 1], LIMIT + 1, ALU.add, ALU.min)
                    ins.then_inc(up_read, 1)
                    dve.wait_ge(sig_done, item * QUARTERS + j + 1)
                    st.link(nc.vector.tensor_tensor(sig[:], glu[:], sig[:], ALU.mult))
                    nc.vector.scalar_tensor_tensor(act_out[:, j % 2].rearrange("p c n -> p (c n)"), lin[:].rearrange("p c n -> p (c n)"),
                                                   1.0 - LIMIT, sig[:].rearrange("p c n -> p (c n)"), ALU.max, ALU.mult).then_inc(act_done, 1)
                    dve.wait_ge(a_hi_done, item * QUARTERS + j + 1)
                    nc.vector.tensor_tensor(a_lo[:, 2 * j:2 * j + 2, :], act_out[:, j % 2], a_hi[:, 2 * j:2 * j + 2, :].bitcast(F32),
                                            ALU.subtract).then_inc(a_lo_done, 1)
                if s == UP_SLOTS:
                    xt_lo_part(dve, item + 1)
            dve.wait_ge(slot_used, item * ITEM_SLOTS + ITEM_SLOTS)
            dve.wait_ge(y_scattered, item * 32)
            for c in range(2):
                nc.vector.tensor_copy(y[:, 1, 512 * c:512 * c + 512], ps[0:SUB, 6 + c, :]).then_inc(y_evac_v, 1)
            assert st.n == VSTEPS, st.n

    @block.tensor
    def _(pe):
        pe.wait_ge(bup_loaded, 16)
        for m in range(2 * KT):
            ins = nc.tensor.transpose(ps[:, 0, E * m:E * m + E], bup_rows[:, P * m:P * m + P], ident[0:E, 0:E])
        ins.then_inc(bup_tr, 1)
        pe.wait_ge(bup_ready, 2)
        n = n_of(pe)

        def transposes(item):
            pe.wait_ge(gathered, item * 32 + 32)
            for i, (bank, k0, nk) in enumerate(XT):
                for kt in range(k0, k0 + nk):
                    for b in range(2):
                        c = ITEM * (kt - k0) + SUB * b
                        ins = nc.tensor.transpose(ps[:, bank, c:c + SUB], tokens[:, b, P * kt:P * kt + P], ident[0:SUB, 0:SUB])
                ins.then_inc(xt_ready, 1)

        transposes(0)
        with pe.Fori(0, n) as item:
            pe.wait_ge(xt_lo_done, item * 3 + 3)
            for s in range(UP_SLOTS):
                quarter, which = divmod(s, 2)
                r = s % SPLIT_E
                pe.wait_ge(lo_done, item * ITEM_SLOTS + s + 1)
                if quarter >= 2 and not which:
                    pe.wait_ge(up_read, item * QUARTERS + quarter - 1)
                bank = 2 * (quarter % 2) + which
                whi = w_hi[:, r, :].rearrange("p (k n) -> p k n", n=256)
                wlo = w_lo[:, r, :].rearrange("p (k n) -> p k n", n=256)
                for c in range(2):
                    to = ps[:, bank, ITEM * c:ITEM * c + ITEM]
                    at = slice(P * c, P * c + P)
                    for kt in range(KT):
                        nc.tensor.matmul(to, whi[:, kt, at], xt_hi[:, kt, :], start=kt == 0, stop=False)
                        nc.tensor.matmul(to, whi[:, kt, at], xt_lo[:, kt, :], start=False, stop=False)
                        ins = nc.tensor.matmul(to, wlo[:, kt, at], xt_hi[:, kt, :], start=False, stop=kt == KT - 1)
                ins.then_inc(slot_used, 1)
            pe.wait_ge(up_read, item * QUARTERS + QUARTERS)
            transposes(item + 1)
            for d in range(DOWN_SLOTS):
                s = UP_SLOTS + d
                r = s % SPLIT_E
                pe.wait_ge(lo_done, item * ITEM_SLOTS + s + 1)
                pe.wait_ge(a_lo_done, item * QUARTERS + d + 1)
                if d == 0:
                    pe.wait_ge(y_evac_s, item * 2)
                    pe.wait_ge(y_evac_v, item * 2)
                whi = w_hi[:, r, :].rearrange("p (k n) -> p k n", n=D)
                wlo = w_lo[:, r, :].rearrange("p (k n) -> p k n", n=D)
                for f in range(2):
                    ft = 2 * d + f
                    for b in range(2):
                        at = slice(SUB * b, SUB * b + SUB)
                        for a, w in ((a_hi, whi), (a_hi, wlo), (a_lo, whi)):
                            for c in range(2):
                                ins = nc.tensor.matmul(ps[0:SUB, 4 + 2 * b + c, :], a[:, ft, at], w[:, f, 512 * c:512 * c + 512],
                                                       start=ft == 0 and a is a_hi and w is whi, stop=ft == KT - 1 and a is a_lo)
                ins.then_inc(slot_used, 1)

    @block.gpsimd
    def _(pool):
        n = n_of(pool)
        def held(eng):
            eng.sem_inc(ticked, 1)

        def fetch_item(item):
            b0 = pool.value_load(item_row[0:1, bass.ds(2 * item + 1, 1)], min_val=0, max_val=E * SLOTS_PER_EXPERT - ITEM)
            for b in range(2):
                pool.dma_start(fetched[:, b, :], slot_dram[bass.ds(b0 + SUB * b, SUB), :]).then_inc(fetch, 16)
            pool.wait_ge(fetch, item * 32 + 32)
            pool.wait_ge(xt_ready, item * 3)
            held(pool)
            for b in range(2):
                pool.indirect_dma_start(tokens[:, b, :], None, h2_dram,
                                        bass.IndirectOffsetOnAxis(ap=fetched[:, b, 1:2].bitcast(U32), axis=0)).then_inc(gathered, 16)

        fetch_item(pool.snap(0))
        with pool.Fori(0, n) as item:
            pool.wait_ge(gathered, item * 32 + 32)
            held(pool)
            nc.gpsimd.tensor_copy(in_work[:], fetched[:]).then_inc(copied, 1)
            pool.wait_ge(copied, item + 1)
            fetch_item(item + 1)
            pool.wait_ge(y_evac_s, item * 2 + 2)
            pool.wait_ge(y_evac_v, item * 2 + 2)
            held(pool)
            for b in range(2):
                pool.indirect_dma_start(y_dram, bass.IndirectOffsetOnAxis(ap=in_work[:, b, 0:1].bitcast(U32), axis=0),
                                        y[:, b, :], None, bounds_check=NCODES - 1, oob_is_err=False).then_inc(y_scattered, 16)
            pool.wait_ge(y_scattered, item * 32 + 32)


def combine(nc, scope, keep, x2_dram, y_dram, b_down, normf_g, out_rows):
    def sb(name, shape, dt=F32):
        return scope.enter_context(nc.sbuf_tensor(name, shape, dt))

    def sem(name):
        return scope.enter_context(nc.semaphore(name))

    ps, ident, gates, gate_of = keep["ps"], keep["ident"], keep["gates"], keep["gate_of"]
    TILES_C = SEQ // P
    ys = sb("ys", [P, 2, TOPK, D])
    acc = sb("acc", [P, 2, D])
    junk = sb("junk", [P, D])
    bd, gf_row = sb("bd", [E, D]), sb("gf_row", [P, D])
    g_t = sb("g_t", [E, TILES_C, P])
    sumsq, ms, rms, rstd = sb("sumsq_c", [P, 2]), sb("ms_c", [P, 2]), sb("rms_c", [P, 2]), sb("rstd_c", [P, 2])

    loaded = [sem("loaded0"), sem("loaded1")]
    c_loaded, stored = sem("c_loaded"), [sem("stored0"), sem("stored1")]
    gt_ready, gt_done, bias_ready, added, squared, ms_done, rms_done, normed = (
        sem("gt_ready"), sem("gt_done"), sem("bias_ready"), sem("added"), sem("squared"), sem("ms_done_c"), sem("rms_done_c"), sem("normed"))
    vstep = sem("vstep_c")
    ticked = sem("ticked_c")
    VSTEPS = TOPK + 2
    y4 = y_dram.rearrange("(k t p) n -> t p k n", p=P, t=TILES_C)
    x8 = x2_dram.rearrange("(t p) n -> t p n", p=P)
    out8 = out_rows.rearrange("(t p) n -> t p n", p=P)
    block = scope.enter_context(nc.Block())

    @block.sync
    def _(sp):
        sp.dma_start(bd[:], b_down).then_inc(c_loaded, 16)
        sp.dma_start(gf_row[:], normf_g.rearrange("(a n) -> a n", a=1).to_broadcast([P, D])).then_inc(c_loaded, 16)
        with sp.Fori(0, TILES_C // 2) as i:
            for b in range(2):
                sp.wait_ge(stored[b], i * 16)
                for c in range(TOPK):
                    sp.dma_start(ys[:, b, c, :], y4[bass.ds(2 * i + b, 1), :, c, :].rearrange("a p n -> p (a n)")).then_inc(loaded[b], 16)
                sp.dma_start(acc[:, b, :], x8[bass.ds(2 * i + b, 1)].rearrange("a p n -> p (a n)")).then_inc(loaded[b], 16)

    @block.tensor
    def _(pe):
        for t in range(TILES_C):
            ins = nc.tensor.transpose(ps[0:E, t // 4, P * (t % 4):P * (t % 4) + P], gate_of[:, t, :], ident[:])
        ins.then_inc(gt_ready, 1)
        pe.wait_ge(gt_done, 1)
        pe.wait_ge(c_loaded, 32)
        for t in range(TILES_C):
            if t >= 2:
                pe.wait_ge(added, t - 1)
            for c in range(2):
                ins = nc.tensor.matmul(ps[:, 4 + 2 * (t % 2) + c, :], g_t[:, t, :], bd[:, 512 * c:512 * c + 512], start=True, stop=True)
            ins.then_inc(bias_ready, 1)

    @block.vector
    def _(dve):
        dve.wait_ge(gt_ready, 1)
        nc.vector.tensor_copy(g_t[:].rearrange("p t n -> p (t n)"), ps[0:E, 0:2, :].rearrange("p b n -> p (b n)")).then_inc(gt_done, 1)
        dve.wait_ge(c_loaded, 32)
        with dve.Fori(0, TILES_C // 2) as i:
            st = Steps(dve, vstep, i * 2 * VSTEPS)
            for b in range(2):
                g = gates[:, bass.ds(2 * i + b, 1), :].rearrange("p a k -> p (a k)")
                dve.wait_ge(loaded[b], i * 16 * (TOPK + 1) + 16 * (TOPK + 1))
                for c in range(TOPK):
                    st.link(nc.vector.scalar_tensor_tensor(acc[:, b, :], ys[:, b, c, :], g[:, c:c + 1], acc[:, b, :], ALU.mult, ALU.add))
                dve.wait_ge(bias_ready, 2 * i + b + 1)
                nc.vector.tensor_tensor(acc[:, b, :], ps[:, 4 + 2 * b:6 + 2 * b, :].rearrange("p a n -> p (a n)"), acc[:, b, :], ALU.add).then_inc(added, 1)
                dve.wait_ge(squared, 2 * i + b + 1)
                nc.vector.tensor_scalar(ms[:, b:b + 1], sumsq[:, b:b + 1], 1.0 / D, EPS, ALU.mult, ALU.add).then_inc(ms_done, 1)
                dve.wait_ge(rms_done, 2 * i + b + 1)
                st.link(nc.vector.reciprocal(rstd[:, b:b + 1], rms[:, b:b + 1]))
                st.link(nc.vector.scalar_tensor_tensor(acc[:, b, :], acc[:, b, :], rstd[:, b:b + 1], gf_row[:], ALU.mult, ALU.mult))
                dve.sem_inc(normed, 1)
            assert st.n == 2 * VSTEPS, st.n

    @block.scalar
    def _(act):
        with act.Fori(0, TILES_C // 2) as i:
            for b in range(2):
                act.wait_ge(added, 2 * i + b + 1)
                nc.scalar.activation(junk[:], acc[:, b, :], ACT.Square, accum_out=sumsq[:, b:b + 1]).then_inc(squared, 1)
                act.wait_ge(ms_done, 2 * i + b + 1)
                nc.scalar.activation(rms[:, b:b + 1], ms[:, b:b + 1], ACT.Sqrt).then_inc(rms_done, 1)

    @block.gpsimd
    def _(pool):
        with pool.Fori(0, TILES_C // 2) as i:
            for b in range(2):
                pool.wait_ge(normed, 2 * i + b + 1)
                pool.sem_inc(ticked, 1)
                pool.dma_start(out8[bass.ds(2 * i + b, 1)].rearrange("a p n -> p (a n)"), acc[:, b, :]).then_inc(stored[b], 16)
        pool.wait_ge(stored[0], 16 * (TILES_C // 2))
        pool.wait_ge(stored[1], 16 * (TILES_C // 2))


INPUTS = ["x", "positions", "norm1_g", "w_in", "b_in", "attn_sinks", "w_attn_br", "pool_w", "pool_scale", "w_pool_br",
          "w_out", "norm2_g", "w_router", "b_router", "w_up", "b_up", "w_down", "b_down", "normf_g"]


def kernel(**inputs):
    import concourse.bacc as bacc
    from concourse.bass_utils import run_bass_kernel_spmd

    nc = bacc.Bacc("TRN2", target_bir_lowering=False, num_devices=1)
    arrays = {f"in_{n}": np.ascontiguousarray(inputs[n]) for n in INPUTS}
    arrays.update({f"in_{n}": a for n, a in shape_constants().items()})
    args = [nc.dram_tensor(n, a.shape, mybir.dt.from_np(a.dtype), kind="ExternalInput").ap() for n, a in arrays.items()]
    out = nc.dram_tensor("out_0", [1, SEQ, D], F32, kind="ExternalOutput").ap()
    decoder_layer(nc, *args, out)
    return run_bass_kernel_spmd(nc, [arrays], core_ids=[0]).results[0]["out_0"]
```

```python
from contextlib import ExitStack

import numpy as np

import concourse.bass as bass
from concourse import mybir

F32 = mybir.dt.float32
F32R = mybir.dt.float32r
I32 = mybir.dt.int32
U32 = mybir.dt.uint32
ALU = mybir.AluOpType
ACT = mybir.ActivationFunctionType
AX_X = mybir.AxisListType.X

P = 128
D = 1024
SEQ = 1024
KT = D // P
HALF = 512
TT = HALF // P
HEADS, KVH, HD = 16, 2, 64
ROPE_DIM, ROPE_THETA = HD // 4, 500000.0
PW = D // 2
POOL_WINDOWS = (2, 4, 8, 16)
NG = len(POOL_WINDOWS)
HIST = 16
O_K = HEADS * HD
O_V = O_K + KVH * HD
O_U = O_V + KVH * HD
O_GA = O_U + PW
O_GP = O_GA + D
E, TOPK, DFF = 32, 4, 1024
EPS = 1e-5
ALPHA, LIMIT = 1.702, 7.0
NEG = -1e30

ITEM = 152
SUB = ITEM // 2
ROUNDS = -(-SEQ // ITEM)
SLOTS_PER_EXPERT = ROUNDS * ITEM
NCODES = SEQ * TOPK
MAX_ITEMS = E + NCODES // ITEM
ITEM_ROW = 64
FREE_CODE = 1 << 20

RAW = 4
SPLIT = 2
SLOT = 2048

PROJ_SLOTS = 8
GATE0 = PROJ_SLOTS
OUT0 = GATE0 + 2 * KT
MIX_SLOTS = OUT0 + 4
SPLITS = PROJ_SLOTS + KT
TILES = ["k0", "k1", "v"] + [f"q{i}" for i in range(8)] + [f"u{i}" for i in range(4)]
ROPED = [0, 1] + list(range(3, 11))
UNITS = TT * HEADS // 2
B_Q, B_U, B_GA, B_GP, B_PS, NB = 2, 10, 14, 22, 30, 34

UP_SLOTS, DOWN_SLOTS = 8, 4
ITEM_SLOTS = UP_SLOTS + DOWN_SLOTS


def rope_freqs():
    half = ROPE_DIM // 2
    f = np.power(np.float32(ROPE_THETA), -np.arange(half, dtype=np.float32) * np.float32(2.0 / ROPE_DIM))
    col = np.zeros((P, 1), np.float32)
    for h in range(P // HD):
        for j in range(ROPE_DIM):
            col[h * HD + j, 0] = f[j % half]
    return col


def shape_constants():
    half = ROPE_DIM // 2
    swap = np.zeros((P, P), np.float32)
    for h in range(P // HD):
        for j in range(half):
            swap[h * HD + j + half, h * HD + j] = -1.0
            swap[h * HD + j, h * HD + j + half] = 1.0
    q, k = np.arange(P)[:, None], np.arange(2 * P)[None, :]
    dist = q + P - k
    band = (dist >= 0) & (dist < P)
    masks = np.stack([np.where(band & (k >= P), 0.0, NEG), np.where(band, 0.0, NEG)], 1).astype(np.float32)
    fix = np.ones((P, 2, NG, HIST), np.float32)
    for g, w in enumerate(POOL_WINDOWS):
        fix[:, 0, g, :] = w / np.minimum(np.arange(1, HIST + 1), w)
    return {
        "c_ident": np.eye(P, dtype=np.float32),
        "c_before": np.triu(np.ones((P, P), np.float32), 1),
        "c_swap": swap,
        "c_masks": masks,
        "c_freq": rope_freqs(),
        "c_fix": fix.reshape(P, 2, NG * HIST),
    }


def cut_pi():
    two_pi, parts = 2 * np.pi, []
    for _ in range(2):
        m, e = np.frexp(two_pi)
        part = float(np.floor(m * 256) / 256 * 2.0**e)
        parts.append(part)
        two_pi -= part
    return parts + [float(np.float32(two_pi))]


class Steps:

    def __init__(self, eng, sem, base=0):
        self.eng, self.sem, self.base, self.n = eng, sem, base, 0

    def done(self, ins):
        self.n += 1
        ins.then_inc(self.sem, 1)
        return self.n

    def wait(self, n=None):
        self.eng.wait_ge(self.sem, self.base + (self.n if n is None else n))

    def link(self, ins):
        self.done(ins)
        self.wait()


N_CONSTS = 22
MIX_VECTOR_STEPS = 170
MIX_POOL_STEPS = 22


def decoder_layer(nc, x, positions, norm1_g, w_in, b_in, attn_sinks, w_attn_br, pool_w, pool_scale,
                  w_pool_br, w_out, norm2_g, w_router, b_router, w_up, b_up, w_down, b_down, normf_g,
                  c_ident, c_before, c_swap, c_masks, c_freq, c_fix, out):
    x_rows = x[0]
    out_rows = out[0]
    w_in, w_attn, w_pool, w_o = w_in[0], w_attn_br[0], w_pool_br[0], w_out[0]
    w_up, w_down = w_up[0], w_down[0]

    x2_dram = nc.dram_tensor("x2_rows", [SEQ, D], F32, kind="Internal").ap()
    h2_dram = nc.dram_tensor("h2_rows", [SEQ, D], F32, kind="Internal").ap()
    y_dram = nc.dram_tensor("y_rows", [NCODES, D], F32, kind="Internal").ap()
    slot_dram = nc.dram_tensor("slot_entries", [E * SLOTS_PER_EXPERT, 2], I32, kind="Internal").ap()
    item_dram = nc.dram_tensor("item_entries", [ITEM_ROW, 2], I32, kind="Internal").ap()

    with ExitStack() as whole:
        def sb(name, shape, dt=F32, scope=whole):
            return scope.enter_context(nc.sbuf_tensor(name, shape, dt))

        ps = whole.enter_context(nc.psum_tensor("banks", [P, 8, 512], F32))
        keep = {
            "ps": ps,
            "ident": sb("ident", [P, P]),
            "gates": sb("gates", [P, SEQ // P, TOPK]),
            "gate_of": sb("gate_of", [P, SEQ // P, E]),
            "item_row": sb("item_row", [1, 2 * ITEM_ROW], I32),
            "n_items": sb("n_items", [P, 1], I32),
        }
        with ExitStack() as scope:
            mixer(nc, scope, keep, x_rows, positions, norm1_g, w_in, b_in, attn_sinks, w_attn, pool_w[0],
                  pool_scale, w_pool, w_o, norm2_g, w_router[0], b_router, c_ident, c_before, c_swap,
                  c_masks, c_freq, c_fix, x2_dram, h2_dram, slot_dram, item_dram)
        with ExitStack() as scope:
            experts(nc, scope, keep, w_up, b_up[0], w_down, h2_dram, y_dram, slot_dram)
        with ExitStack() as scope:
            combine(nc, scope, keep, x2_dram, y_dram, b_down[0], normf_g, out_rows)


def mixer(nc, scope, keep, x_rows, positions, norm1_g, w_in, b_in, attn_sinks, w_attn, pool_w,
          pool_scale, w_pool, w_o, norm2_g, w_router, b_router, c_ident, c_before, c_swap, c_masks,
          c_freq, c_fix, x2_dram, h2_dram, slot_dram, item_dram):
    def sb(name, shape, dt=F32):
        return scope.enter_context(nc.sbuf_tensor(name, shape, dt))

    def sem(name):
        return scope.enter_context(nc.semaphore(name))

    ps, ident = keep["ps"], keep["ident"]
    gates, gate_of = keep["gates"], keep["gate_of"]
    item_row, n_items = keep["item_row"], keep["n_items"]

    before = sb("before", [P, P])
    ones = sb("ones", [P, P])
    swap = sb("swap", [P, P])
    masks = sb("masks", [P, 2, 2 * P])
    freq = sb("freq", [P, 1])
    fix = sb("fix", [P, 2, NG * HIST])
    g1_row, g2_row = sb("g1_row", [P, D]), sb("g2_row", [P, D])
    bv_row, br_row = sb("bv_row", [P, P]), sb("br_row", [P, E])
    sinks, sinks8 = sb("sinks", [P, HEADS]), sb("sinks8", [P, HEADS])
    bias_rows, bias = sb("bias_rows", [NB, P]), sb("bias", [P, NB])
    pool_mix = sb("pool_mix", [P, NG, P])
    router = sb("router", [P, KT, E])
    pos_i = sb("pos_i", [P, HALF], I32)
    cos, sin = sb("cos", [P, HALF]), sb("sin", [P, HALF])

    xs = sb("xs", [P, TT, D])
    rows = sb("rows", [P, TT, D])
    h_hi, h_lo = sb("h_hi", [P, KT, HALF], F32R), sb("h_lo", [P, KT, HALF], F32R)
    q = sb("q", [P, KT, HALF])
    k = sb("k", [P, KVH, P + HALF])
    v = sb("v", [P, TT + 1, P])
    u = sb("u", [P, NG, HIST + HALF])
    pooled = sb("pooled", [P, NG, HALF])
    gate = sb("gate", [P, 4, HALF])
    raw = sb("raw_m", [P, RAW, SLOT])
    w_hi, w_lo = sb("w_hi_m", [P, SPLIT, SLOT], F32R), sb("w_lo_m", [P, SPLIT, SLOT], F32R)

    flat = rows[:].rearrange("p t n -> p (t n)")
    merged = flat.rearrange("p (m n) -> p m n", n=HALF)
    scores = flat[:, 0:1024].rearrange("p (b n) -> p b n", b=2)
    probs = flat[:, 1024:2560].rearrange("p (b n) -> p b n", b=3)
    probs_t = flat[:, 2560:3584].rearrange("p (b n) -> p b n", b=2)
    wide = gate[:].rearrange("p a n -> p (a n)")
    win = [wide[:, 0:HIST + HALF], wide[:, 1024:1024 + HIST + HALF]]

    sumsq, rms, rstd = sb("sumsq", [P, TT]), sb("rms", [P, TT]), sb("rstd", [P, TT])
    smax, negmax = sb("smax", [P, 2, 2]), sb("negmax", [P, 2, 2])
    sdiff, sexp = sb("sdiff", [P, 2, 2]), sb("sexp", [P, 2, 2])
    psum_row, den, rden = sb("prob_sum", [P, 2, 2]), sb("den", [P, 2, 2]), sb("rden", [P, 3, 2])
    logits = sb("logits", [P, TT, E])
    top, top_i, top_f = sb("top", [P, 8]), sb("top_i", [P, 8], U32), sb("top_f", [P, 8])
    neg_top, etop, esum, resum = sb("neg_top", [P, 1]), sb("etop", [P, TOPK]), sb("esum", [P, 1]), sb("resum", [P, 1])
    onehot, chosen = sb("onehot", [P, TOPK, E]), sb("chosen", [P, E])
    e_row, base = sb("e_row", [P, E]), sb("base", [P, E])
    slot_of, picked = sb("slot_of", [P, E]), sb("picked", [P, TOPK, E])
    dest_f, dest = sb("dest_f", [P, TOPK]), sb("dest", [P, TT, TOPK], I32)
    codes = sb("codes", [P, SEQ // P, 2 * TOPK], I32)
    half_codes = sb("half_codes", [P, TT, 2 * TOPK], I32)
    free_slots = sb("free_slots", [P, 2 * E * SLOTS_PER_EXPERT // P], I32)
    NX = (ROUNDS - 1) * E
    over, order, one_x, x_expert, x_base, x_pick = (wide[:, NX * i:NX * i + NX] for i in range(6))
    count = sb("count", [P, E])
    part1 = sb("part1", [P, 1])
    extra_f, items_f = sb("extra_f", [P, 2]), sb("items_f", [P, 1])
    extra_i, first_i = sb("extra_i", [P, 2], I32), sb("first_i", [P, 2], I32)

    const_loaded, pos_loaded, x_loaded = sem("const_loaded"), sem("pos_loaded"), sem("x_loaded")
    raw_loaded = [sem(f"raw_loaded{r}") for r in range(RAW)]
    ready_const, zeroed, table_free = sem("ready_const"), sem("zeroed"), sem("table_free")
    bias_t, bias_done = sem("bias_t"), sem("bias_done")
    angles, cs_ready, sumsq_done, ms_done, rms_done = sem("angles"), sem("cs_ready"), sem("sumsq_done"), sem("ms_done"), sem("rms_done")
    rows_done, h2_rows_done = sem("rows_done"), sem("h2_rows_done")
    hi_done, lo_done = sem("hi_done"), sem("lo_done")
    xt_ready, h_hi_done, h_lo_done = sem("xt_ready"), sem("h_hi_done"), sem("h_lo_done")
    proj_ready, proj_evac, v_evac = sem("proj_ready"), sem("proj_evac"), sem("v_evac")
    rope_ready, rope_done = sem("rope_ready"), sem("rope_done")
    scored, max_done, exp_done = sem("scored"), sem("max_done"), sem("exp_done")
    rden_done, scaled, pt_ready, pt_evac = sem("rden_done"), sem("scaled"), sem("pt_ready"), sem("pt_evac")
    pv_ready, o_evac = sem("pv_ready"), sem("o_evac")
    mix_ready, mix_evac = sem("mix_ready"), sem("mix_evac")
    gate_mm, gate_done, br_ready, merged_done = sem("gate_mm"), sem("gate_done"), sem("br_ready"), sem("merged_done")
    out_ready, x2_done, x2_stored, h2_stored = sem("out_ready"), sem("x2_done"), sem("x2_stored"), sem("h2_stored")
    h2t_evac, logits_ready, top_done, etop_done = sem("h2t_evac"), sem("logits_ready"), sem("top_done"), sem("etop_done")
    chosen_done, rank_ready, dest_done, scattered = sem("chosen_done"), sem("rank_ready"), sem("dest_done"), sem("scattered")
    codes_done, hist_done = sem("codes_done"), sem("hist_done")
    items_done, items_stored, items_loaded = sem("items_done"), sem("items_stored"), sem("items_loaded")
    vstep, pstep = sem("vstep"), sem("pstep")

    NPE = len(TILES) - 1
    evac_no = {ti: sum(t != "v" for t in TILES[:ti + 1]) for ti in range(len(TILES))}
    tile_slot = {0: 0, 1: 0, 2: 1, **{3 + i: 2 + i // 2 for i in range(8)}, **{11 + i: 6 + i // 2 for i in range(4)}}
    slot_last = {s: max(t for t, at in tile_slot.items() if at == s) for s in range(PROJ_SLOTS)}

    def cols(w, c0, n):
        return w.rearrange("(k p) n -> p k n", p=P)[:, :, c0:c0 + n]

    def slot_view(t, r, n):
        return t[:, r, :].rearrange("p (k n) -> p k n", n=n)

    loads = []
    dst = [slot_view(raw, r, 256) for r in range(RAW)]
    for s in range(MIX_SLOTS):
        d, r = dst[s % RAW], s % RAW
        if s == 0:
            loads.append([(d[:, :, 64 * i:64 * i + 64], cols(w_in, O_K + 64 * (i // 2), 64)) for i in range(4)])
        elif s == 1:
            loads.append([(raw[:, r, 0:1024].rearrange("p (k n) -> p k n", n=P), cols(w_in, O_V, P))])
        elif s < 6:
            loads.append([(d, cols(w_in, 256 * (s - 2), 256))])
        elif s < PROJ_SLOTS:
            loads.append([(d, cols(w_in, O_U + 256 * (s - 6), 256))])
        elif s < OUT0:
            m, branch = divmod(s - GATE0, 2)
            if branch:
                loads.append([(raw[:, r, 0:1024].rearrange("p (k n) -> p k n", n=P), cols(w_attn, P * m, P)),
                              (raw[:, r, 1024:1536].rearrange("p (k n) -> p k n", n=P), cols(w_pool, P * m, P))])
            else:
                loads.append([(d[:, :, 0:P], cols(w_in, O_GA + P * m, P)), (d[:, :, P:2 * P], cols(w_in, O_GP + P * m, P))])
        else:
            n, kh = divmod(s - OUT0, 2)
            loads.append([(slot_view(raw, r, 512), cols(w_o, 512 * n, 512)[:, 4 * kh:4 * kh + 4, :])])
    arrived, per_half = {}, [0] * RAW
    for s in range(MIX_SLOTS):
        per_half[s % RAW] += 16 * len(loads[s])
        arrived[s] = per_half[s % RAW]
    split_slots = list(range(PROJ_SLOTS)) + [GATE0 + 2 * m for m in range(KT)]

    def raw_arrived(eng, hf, s):
        eng.wait_ge(raw_loaded[s % RAW], hf * per_half[s % RAW] + arrived[s])

    block = scope.enter_context(nc.Block())

    @block.sync
    def _(sp):
        for hf in range(2):
            sp.wait_ge(x2_stored, hf * 16 * TT)
            sp.wait_ge(h2_rows_done, hf * TT)
            for t in range(TT):
                sp.dma_start(xs[:, t, :], x_rows.rearrange("(h t p) n -> h t p n", p=P, t=TT)[hf, t]).then_inc(x_loaded, 16)
            sp.wait_ge(angles, hf)
            sp.dma_start(pos_i[:], positions.rearrange("a (h n) -> a h n", n=HALF)[:, bass.ds(hf, 1), :].rearrange("a h n -> a (h n)").to_broadcast([P, HALF])).then_inc(pos_loaded, 16)
            for s in range(MIX_SLOTS):
                last = s - RAW
                if last < 0:
                    sp.wait_ge(out_ready, hf * 2 * TT)
                elif last in split_slots:
                    sp.wait_ge(lo_done, hf * SPLITS + split_slots.index(last) + 1)
                else:
                    sp.wait_ge(br_ready, hf * KT + (last - GATE0) // 2 + 1)
                for to, src in loads[s]:
                    sp.dma_start(to, src).then_inc(raw_loaded[s % RAW], 16)
        sp.wait_ge(items_done, 1)
        sp.dma_start(item_dram[0:E, :], first_i[0:E, :]).then_inc(items_stored, 16)
        sp.dma_start(item_dram[E:ITEM_ROW, :], extra_i[0:ITEM_ROW - E, :]).then_inc(items_stored, 16)
        sp.wait_ge(items_stored, 32)
        sp.dma_start(item_row[:], item_dram.rearrange("(a i) c -> a (i c)", a=1)).then_inc(items_loaded, 16)
        sp.wait_ge(items_loaded, 16)

    def hi_part(act, hf, si):
        s = split_slots[si]
        raw_arrived(act, hf, s)
        if si >= SPLIT:
            if si - SPLIT < PROJ_SLOTS:
                act.wait_ge(proj_ready, hf * len(TILES) + slot_last[si - SPLIT] + 1)
            else:
                act.wait_ge(gate_mm, hf * 2 * KT + 2 * (si - SPLIT - PROJ_SLOTS) + 2)
        n = 1024 if s == 1 else SLOT
        nc.scalar.activation(w_hi[:, si % SPLIT, 0:n], raw[:, s % RAW, 0:n], ACT.Copy).then_inc(hi_done, 1)

    def lo_part(dve, hf, si):
        s = split_slots[si]
        dve.wait_ge(hi_done, hf * SPLITS + si + 1)
        n = 1024 if s == 1 else SLOT
        nc.vector.tensor_tensor(w_lo[:, si % SPLIT, 0:n], raw[:, s % RAW, 0:n],
                                w_hi[:, si % SPLIT, 0:n].bitcast(F32), ALU.subtract).then_inc(lo_done, 1)

    @block.scalar
    def _(act):
        consts = [(ident[:], c_ident), (before[:], c_before), (swap[:], c_swap), (masks[:], c_masks),
                  (freq[:], c_freq), (fix[:], c_fix),
                  (g1_row[:], norm1_g[0:1, :].to_broadcast([P, D])), (g2_row[:], norm2_g[0:1, :].to_broadcast([P, D])),
                  (bv_row[:], b_in[0:1, O_V:O_U].to_broadcast([P, P])), (br_row[:], b_router[0:1, :].to_broadcast([P, E])),
                  (sinks[:], attn_sinks[0:1, :].to_broadcast([P, HEADS])),
                  (pool_mix[:], pool_w.rearrange("g c d -> c g d")),
                  (router[:], w_router.rearrange("(k p) e -> p k e", p=P))]
        for kv in range(KVH):
            for half in range(2):
                consts.append((bias_rows[kv:kv + 1, 64 * half:64 * half + 64], b_in[0:1, O_K + 64 * kv:O_K + 64 * kv + 64]))
        for at, c0, n in ((B_Q, 0, 8), (B_U, O_U, NG), (B_GA, O_GA, 8), (B_GP, O_GP, 8)):
            consts.append((bias_rows[at:at + n, :], b_in[0, c0:c0 + n * P].rearrange("(r c) -> r c", c=P)))
        consts.append((bias_rows[B_PS:NB, :], pool_scale[0, :].rearrange("(r c) -> r c", c=P)))
        assert len(consts) == N_CONSTS
        for to, src in consts:
            act.dma_start(to, src).then_inc(const_loaded, 16)
        act.wait_ge(bias_done, 1)

        def row_stats(hf, second):
            uses = 2 * hf + second
            for t in range(TT):
                if second:
                    act.wait_ge(x2_done, hf * 2 * TT + 2 * TT)
                else:
                    act.wait_ge(x_loaded, 16 * TT * hf + 16 * TT)
                    act.wait_ge(h2_stored, hf * 16 * TT)
                nc.scalar.activation(rows[:, t, :], xs[:, t, :], ACT.Square, accum_out=sumsq[:, t:t + 1]).then_inc(sumsq_done, 1)
            act.wait_ge(ms_done, uses + 1)
            nc.scalar.activation(rms[:], rms[:], ACT.Sqrt).then_inc(rms_done, 1)

        for hf in range(2):
            act.wait_ge(angles, hf + 1)
            nc.scalar.activation(sin[:], gate[:, 2, :], ACT.Sin)
            nc.scalar.activation(cos[:], gate[:, 3, :], ACT.Sin).then_inc(cs_ready, 1)
            row_stats(hf, 0)
            hi_part(act, hf, 0)
            hi_part(act, hf, 1)
            for kt in range(KT):
                act.wait_ge(xt_ready, hf * 2 * KT + kt + 1)
                nc.scalar.activation(h_hi[:, kt, :], ps[:, kt % 2, :], ACT.Copy).then_inc(h_hi_done, 1)
            for ti, name in enumerate(TILES):
                act.wait_ge(proj_ready, hf * len(TILES) + ti + 1)
                if name != "v":
                    kind, i = name[0], int(name[1:])
                    to, b = {"k": (k[:, i % 2, P:], i), "q": (q[:, i, :], B_Q + i),
                             "u": (u[:, i % NG, HIST:], B_U + i)}[kind]
                    if name == "u0":
                        act.wait_ge(hist_done, hf)
                    nc.scalar.activation(to, ps[:, ti % 2, :], ACT.Identity, bias=bias[:, b:b + 1]).then_inc(proj_evac, 1)
                s = tile_slot[ti]
                if ti == slot_last[s]:
                    hi_part(act, hf, s + 2)
            for n in range(UNITS + 2):
                if n < UNITS:
                    b = n % 2
                    act.wait_ge(max_done, hf * UNITS + n + 1)
                    if n >= 3:
                        act.wait_ge(pt_ready, hf * UNITS + n - 2)
                    for hh in range(2):
                        nc.scalar.activation(probs[:, n % 3, 256 * hh:256 * hh + 256], scores[:, b, 256 * hh:256 * hh + 256],
                                             ACT.Exp, bias=negmax[:, b, hh:hh + 1], scale=HD ** -0.5,
                                             accum_out=psum_row[:, b, hh:hh + 1])
                    nc.scalar.activation(sexp[:, b, :], sdiff[:, b, :], ACT.Exp, scale=HD ** -0.5).then_inc(exp_done, 1)
                if n >= 2:
                    act.wait_ge(pt_ready, hf * UNITS + n - 1)
                    if n >= 4:
                        act.wait_ge(pv_ready, hf * UNITS + n - 3)
                    nc.scalar.activation(probs_t[:, n % 2, :], ps[:, (6, 2)[n % 2], :], ACT.Copy).then_inc(pt_evac, 1)
            for m in range(KT):
                for j, b in ((0, B_GA), (1, B_GP)):
                    act.wait_ge(gate_mm, hf * 2 * KT + 2 * m + j + 1)
                    if m >= 2:
                        act.wait_ge(merged_done, hf * KT + m - 1)
                    if m == 0 and j == 0:
                        act.wait_ge(hist_done, hf + 1)
                    nc.scalar.activation(gate[:, 2 * (m % 2) + j, :], ps[:, 4 * (m % 2) + j, :], ACT.Sigmoid,
                                         bias=bias[:, b + m:b + m + 1]).then_inc(gate_done, 1)
                if PROJ_SLOTS + m + 2 < SPLITS:
                    hi_part(act, hf, PROJ_SLOTS + m + 2)
            row_stats(hf, 1)
            for kt in range(KT):
                act.wait_ge(xt_ready, hf * 2 * KT + KT + kt + 1)
                nc.scalar.activation(q[:, kt, :], ps[:, kt % 2, :], ACT.Copy).then_inc(h2t_evac, 1)
            for t in range(TT):
                act.wait_ge(top_done, hf * TT + t + 1)
                nc.scalar.activation(etop[:], top[:, 0:TOPK], ACT.Exp, bias=neg_top[:, 0:1], accum_out=esum[:, 0:1]).then_inc(etop_done, 1)

    @block.tensor
    def _(pe):
        pe.wait_ge(const_loaded, 16 * N_CONSTS)
        nc.tensor.transpose(ps[:, 0, 0:NB], bias_rows[:], ident[0:NB, 0:NB]).then_inc(bias_t, 1)
        pe.wait_ge(bias_done, 1)
        pe.wait_ge(ready_const, 1)

        def transposes(hf, second):
            for kt in range(KT):
                if second:
                    if kt == 0:
                        pe.wait_ge(h2_rows_done, hf * TT + TT)
                    if kt >= 2:
                        pe.wait_ge(h2t_evac, hf * KT + kt - 1)
                else:
                    if kt == 0:
                        pe.wait_ge(rows_done, hf * TT + TT)
                    if kt >= 2:
                        pe.wait_ge(h_lo_done, hf * KT + kt - 1)
                for t in range(TT):
                    ins = nc.tensor.transpose(ps[:, kt % 2, P * t:P * t + P], rows[:, t, P * kt:P * kt + P], ident[:])
                ins.then_inc(xt_ready, 1)

        def three_pass(to, pairs):
            n = len(pairs)
            for i, (whi, wlo, mhi, mlo) in enumerate(pairs):
                nc.tensor.matmul(to, whi, mhi, start=i == 0, stop=False)
                nc.tensor.matmul(to, whi, mlo, start=False, stop=False)
                ins = nc.tensor.matmul(to, wlo, mhi, start=False, stop=i == n - 1)
            return ins

        for hf in range(2):
            transposes(hf, 0)
            pe.wait_ge(h_lo_done, hf * KT + KT)

            def rope(ri):
                ti = ROPED[ri]
                src = k[:, ti, P:] if ti < 2 else q[:, ti - 3, :]
                pe.wait_ge(proj_evac, hf * NPE + evac_no[ti])
                if ri >= 2:
                    pe.wait_ge(rope_done, hf * len(ROPED) + ri - 1)
                nc.tensor.matmul(ps[:, 2 + ri % 2, :], swap[:], src, start=True, stop=True).then_inc(rope_ready, 1)

            roped = 0
            for ti, name in enumerate(TILES):
                s = tile_slot[ti]
                pe.wait_ge(lo_done, hf * SPLITS + s + 1)
                if ti - 2 == 2:
                    pe.wait_ge(v_evac, hf + 1)
                elif ti >= 2:
                    pe.wait_ge(proj_evac, hf * NPE + evac_no[ti - 2])
                r = s % SPLIT
                if name == "v":
                    whi = w_hi[:, r, 0:1024].rearrange("p (k n) -> p k n", n=P)
                    wlo = w_lo[:, r, 0:1024].rearrange("p (k n) -> p k n", n=P)
                    for t in range(TT):
                        at = slice(P * t, P * t + P)
                        ins = three_pass(ps[:, ti % 2, at],
                                         [(h_hi[:, kt, at], h_lo[:, kt, at], whi[:, kt, :], wlo[:, kt, :]) for kt in range(KT)])
                else:
                    c = P * (ti - min(t for t, at in tile_slot.items() if at == s))
                    whi, wlo = slot_view(w_hi, r, 256), slot_view(w_lo, r, 256)
                    ins = three_pass(ps[:, ti % 2, :],
                                     [(whi[:, kt, c:c + P], wlo[:, kt, c:c + P], h_hi[:, kt, :], h_lo[:, kt, :]) for kt in range(KT)])
                ins.then_inc(proj_ready, 1)
                while roped < len(ROPED) and ROPED[roped] < ti:
                    rope(roped)
                    roped += 1
            pe.wait_ge(rope_done, hf * len(ROPED) + len(ROPED))
            pe.wait_ge(v_evac, hf + 1)
            pe.wait_ge(proj_evac, hf * NPE + NPE)
            for n in range(UNITS + 3):
                if n < UNITS:
                    b, p = divmod(n, HEADS // 2)
                    if n >= 2:
                        pe.wait_ge(max_done, hf * UNITS + n - 1)
                    for hh in range(2):
                        at = slice(64 * hh, 64 * hh + 64)
                        ins = nc.tensor.matmul(ps[:, (4, 0)[n % 2] + hh, 0:256], q[at, p, P * b:P * b + P],
                                               k[at, p // 4, P * b:P * b + 2 * P], start=True, stop=True)
                    ins.then_inc(scored, 1)
                if 2 <= n < UNITS + 2:
                    m = n - 2
                    pe.wait_ge(scaled, hf * UNITS + m + 1)
                    if m >= 2:
                        pe.wait_ge(pt_evac, hf * UNITS + m - 1)
                    for kk in range(2):
                        for hh in range(2):
                            c = P * (2 * kk + hh)
                            ins = nc.tensor.transpose(ps[:, (6, 2)[m % 2], c:c + P],
                                                      probs[:, m % 3, 256 * hh + P * kk:256 * hh + P * kk + P], ident[:])
                    ins.then_inc(pt_ready, 1)
                if n >= 3:
                    m = n - 3
                    b, p = divmod(m, HEADS // 2)
                    pe.wait_ge(pt_evac, hf * UNITS + m + 1)
                    if m >= 2:
                        pe.wait_ge(o_evac, hf * UNITS + m - 1)
                    for hh in range(2):
                        for kk in range(2):
                            c = P * (2 * kk + hh)
                            ins = nc.tensor.matmul(ps[64 * hh:64 * hh + 64, (7, 3)[m % 2], 0:P],
                                                   v[:, b + kk, 64 * (p // 4):64 * (p // 4) + 64],
                                                   probs_t[:, m % 2, c:c + P], start=kk == 0, stop=kk == 1)
                    ins.then_inc(pv_ready, 1)
            pe.wait_ge(hist_done, hf + 1)
            for g in range(NG):
                nc.tensor.matmul(ps[:, (0, 1, 4, 5)[g], :], pool_mix[:, g, :], pooled[:, g, :], start=True, stop=True).then_inc(mix_ready, 1)
            pe.wait_ge(mix_evac, hf * NG + NG)
            pe.wait_ge(o_evac, hf * UNITS + UNITS)
            for m in range(KT):
                si = PROJ_SLOTS + m
                bank = 4 * (m % 2)
                pe.wait_ge(lo_done, hf * SPLITS + si + 1)
                if m >= 2:
                    pe.wait_ge(merged_done, hf * KT + m - 1)
                whi, wlo = slot_view(w_hi, si % SPLIT, 256), slot_view(w_lo, si % SPLIT, 256)
                for j in range(2):
                    c = P * j
                    three_pass(ps[:, bank + j, :], [(whi[:, kt, c:c + P], wlo[:, kt, c:c + P], h_hi[:, kt, :], h_lo[:, kt, :])
                                                    for kt in range(KT)]).then_inc(gate_mm, 1)
                s = GATE0 + 2 * m + 1
                raw_arrived(pe, hf, s)
                wa = raw[:, s % RAW, :].rearrange("p (k n) -> p k n", n=P)
                for kt in range(KT):
                    nc.tensor.matmul(ps[:, bank + 2, :], wa[:, kt, :], q[:, kt, :], start=kt == 0, stop=kt == KT - 1)
                for g in range(NG):
                    ins = nc.tensor.matmul(ps[:, bank + 3, :], wa[:, KT + g, :], pooled[:, g, :], start=g == 0, stop=g == NG - 1)
                ins.then_inc(br_ready, 1)
            pe.wait_ge(merged_done, hf * KT + KT)
            for n in range(2):
                for kh in range(2):
                    raw_arrived(pe, hf, OUT0 + 2 * n + kh)
                for t in range(TT):
                    for kt in range(KT):
                        s = OUT0 + 2 * n + kt // 4
                        ins = nc.tensor.matmul(ps[:, n * TT + t, :], merged[:, kt, P * t:P * t + P],
                                               slot_view(raw, s % RAW, 512)[:, kt % 4, :], start=kt == 0, stop=kt == KT - 1)
                    ins.then_inc(out_ready, 1)
            pe.wait_ge(x2_done, hf * 2 * TT + 2 * TT)
            transposes(hf, 1)
            pe.wait_ge(h2t_evac, hf * KT + KT)
            for t in range(TT):
                for kt in range(KT):
                    ins = nc.tensor.matmul(ps[:, 2, E * t:E * t + E], q[:, kt, P * t:P * t + P], router[:, kt, :],
                                           start=kt == 0, stop=kt == KT - 1)
            ins.then_inc(logits_ready, 1)
            for t in range(TT):
                pe.wait_ge(chosen_done, hf * TT + t + 1)
                nc.tensor.matmul(ps[:, 3, 0:E], before[:], chosen[:], start=True, stop=True)
                nc.tensor.matmul(ps[:, 3, E:2 * E], ones[:], chosen[:], start=True, stop=True).then_inc(rank_ready, 1)

    @block.gpsimd
    def _(pool):
        pool.memset(ones[:], 1.0)
        pool.iota(e_row[:], pattern=[[1, E]], base=0, channel_multiplier=0, allow_small_or_imprecise_dtypes=True)
        pool.iota(base[:], pattern=[[SLOTS_PER_EXPERT, E]], base=0, channel_multiplier=0, allow_small_or_imprecise_dtypes=True)
        pool.iota(part1[:], pattern=[[0, 1]], base=1, channel_multiplier=1, allow_small_or_imprecise_dtypes=True)
        pool.iota(first_i[:, 0:1], pattern=[[0, 1]], base=0, channel_multiplier=1)
        pool.iota(first_i[:, 1:2], pattern=[[0, 1]], base=0, channel_multiplier=SLOTS_PER_EXPERT)
        codes4 = codes[:].rearrange("p t (k c) -> p t k c", c=2)
        pool.iota(codes4[:, :, :, 0], pattern=[[P, SEQ // P], [SEQ, TOPK]], base=0, channel_multiplier=1)
        pool.iota(codes4[:, :, :, 1], pattern=[[P, SEQ // P], [0, TOPK]], base=0, channel_multiplier=1)
        free2 = free_slots[:].rearrange("p (s c) -> p s c", c=2)
        pool.memset(free2[:, :, 0:1], FREE_CODE)
        pool.memset(free2[:, :, 1:2], 0)
        pool.memset(k[:, :, 0:P], 0.0)
        pool.memset(v[:, 0, :], 0.0)
        pool.memset(u[:, :, 0:HIST], 0.0).then_inc(ready_const, 1)
        pool.wait_ge(ready_const, 1)
        pool.dma_start(slot_dram.rearrange("(p s) c -> p (s c)", p=P), free_slots[:]).then_inc(table_free, 16)
        pool.wait_ge(const_loaded, 16 * N_CONSTS)
        for hf in range(2):
            st = Steps(pool, pstep, hf * MIX_POOL_STEPS)
            pool.wait_ge(scattered, hf * 16 * TT * TOPK)
            nc.gpsimd.tensor_copy(half_codes[:], codes[:, bass.ds(hf * TT, TT), :]).then_inc(codes_done, 1)
            pool.wait_ge(proj_evac, hf * NPE + NPE)
            pool.wait_ge(rope_done, hf * len(ROPED) + len(ROPED))
            pool.wait_ge(merged_done, hf * KT)
            for g, w in enumerate(POOL_WINDOWS):
                src, n = u[:, g, :], 1
                i = 0
                while n < w:
                    lo = 2 * n - 1
                    st.link(nc.gpsimd.tensor_tensor(win[i % 2][:, lo:], src[:, lo:], src[:, lo - n:HIST + HALF - n], ALU.add))
                    src, n, i = win[i % 2], 2 * n, i + 1
                st.link(nc.gpsimd.tensor_scalar(pooled[:, g, :], src[:, HIST:], 1.0 / w, None, ALU.mult))
                st.link(nc.gpsimd.tensor_tensor(pooled[:, g, 0:HIST], pooled[:, g, 0:HIST],
                                                fix[:, bass.ds(hf, 1), HIST * g:HIST * g + HIST].rearrange("p a n -> p (a n)"), ALU.mult))
                st.link(nc.gpsimd.tensor_tensor(pooled[:, g, :], pooled[:, g, :], u[:, g, HIST:], ALU.subtract))
            nc.gpsimd.tensor_copy(u[:, :, 0:HIST], u[:, :, HALF:HALF + HIST]).then_inc(hist_done, 1)
            for n in range(UNITS):
                pool.wait_ge(rden_done, hf * UNITS + n + 1)
                for hh in range(2):
                    pr = probs[:, n % 3, 256 * hh:256 * hh + 256]
                    ins = nc.gpsimd.tensor_scalar(pr, pr, rden[:, n % 3, hh:hh + 1], None, ALU.mult)
                ins.then_inc(scaled, 1)
            assert st.n == MIX_POOL_STEPS, st.n
            x2_half = x2_dram.rearrange("(h t p) n -> h t p n", p=P, t=TT)
            h2_half = h2_dram.rearrange("(h t p) n -> h t p n", p=P, t=TT)
            pool.wait_ge(x2_done, hf * 2 * TT + 2 * TT)
            for t in range(TT):
                pool.dma_start(x2_half[hf, t], xs[:, t, :]).then_inc(x2_stored, 16)
            for t in range(TT):
                pool.wait_ge(h2_rows_done, hf * TT + t + 1)
                pool.dma_start(h2_half[hf, t], rows[:, t, :]).then_inc(h2_stored, 16)
            pool.wait_ge(table_free, 16)
            pool.wait_ge(codes_done, hf + 1)
            for t in range(TT):
                pool.wait_ge(dest_done, hf * TT + t + 1)
                for c in range(TOPK):
                    pool.indirect_dma_start(slot_dram, bass.IndirectOffsetOnAxis(ap=dest[:, t, c:c + 1].bitcast(U32), axis=0),
                                            half_codes[:, t, 2 * c:2 * c + 2], None).then_inc(scattered, 16)
        pool.wait_ge(merged_done, 2 * KT)
        pool.memset(one_x, 1.0)
        pool.iota(x_expert, pattern=[[0, ROUNDS - 1], [1, E]], base=0, channel_multiplier=0, allow_small_or_imprecise_dtypes=True)
        pool.iota(x_base, pattern=[[ITEM, ROUNDS - 1], [SLOTS_PER_EXPERT, E]], base=ITEM, channel_multiplier=0, allow_small_or_imprecise_dtypes=True).then_inc(ready_const, 1)
        pool.wait_ge(scattered, 2 * 16 * TT * TOPK)
        pool.wait_ge(x2_stored, 2 * 16 * TT)
        pool.wait_ge(h2_stored, 2 * 16 * TT)

    @block.vector
    def _(dve):
        dve.wait_ge(bias_t, 1)
        nc.vector.tensor_copy(bias[:], ps[:, 0, 0:NB])
        nc.vector.tensor_scalar(sinks8[:], sinks[:], float(HD) ** 0.5, None, ALU.mult).then_inc(bias_done, 1)
        dve.wait_ge(bias_done, 1)
        dve.wait_ge(ready_const, 1)
        c1, c2, c3 = cut_pi()
        MAGIC = 1.5 * 2.0**23
        PI = float(np.float32(3.1415925))

        for hf in range(2):
            st = Steps(dve, vstep, hf * MIX_VECTOR_STEPS)

            def normalise(second, g_row, done):
                dve.wait_ge(sumsq_done, hf * 2 * TT + TT * second + TT)
                nc.vector.tensor_scalar(rms[:], sumsq[:], 1.0 / D, EPS, ALU.mult, ALU.add).then_inc(ms_done, 1)
                dve.wait_ge(rms_done, hf * 2 + second + 1)
                st.link(nc.vector.reciprocal(rstd[:], rms[:]))
                for t in range(TT):
                    nc.vector.scalar_tensor_tensor(rows[:, t, :], xs[:, t, :], rstd[:, t:t + 1], g_row[:], ALU.mult, ALU.mult).then_inc(done, 1)

            dve.wait_ge(pos_loaded, 16 * hf + 16)
            a, n_, s_, c_ = (gate[:, i, :] for i in range(4))
            st.link(nc.vector.tensor_scalar(a, pos_i[:], freq[:, 0:1], None, ALU.mult))
            st.link(nc.vector.tensor_scalar(n_, a, 1.0 / (2 * np.pi), MAGIC, ALU.mult, ALU.add))
            st.link(nc.vector.tensor_scalar(n_, n_, -MAGIC, None, ALU.add))
            for c in (c1, c2, c3):
                st.link(nc.vector.scalar_tensor_tensor(a, n_, -c, a, ALU.mult, ALU.add))
            nc.vector.tensor_scalar(s_, a, PI, -PI, ALU.min, ALU.max)
            st.link(nc.vector.tensor_scalar(c_, a, np.pi / 2, None, ALU.add))
            st.link(nc.vector.tensor_scalar(n_, c_, np.pi, -2 * np.pi, ALU.is_gt, ALU.mult))
            st.link(nc.vector.tensor_tensor(c_, c_, n_, ALU.add))
            nc.vector.tensor_scalar(c_, c_, PI, -PI, ALU.min, ALU.max).then_inc(angles, 1)

            normalise(0, g1_row, rows_done)
            lo_part(dve, hf, 0)
            lo_part(dve, hf, 1)
            for kt in range(KT):
                dve.wait_ge(h_hi_done, hf * KT + kt + 1)
                nc.vector.tensor_tensor(h_lo[:, kt, :], ps[:, kt % 2, :], h_hi[:, kt, :].bitcast(F32), ALU.subtract).then_inc(h_lo_done, 1)
            dve.wait_ge(cs_ready, hf + 1)
            for ti, name in enumerate(TILES):
                if name == "v":
                    dve.wait_ge(proj_ready, hf * len(TILES) + ti + 1)
                    nc.vector.tensor_tensor(v[:, 1:, :], ps[:, ti % 2, :].rearrange("p (t n) -> p t n", n=P),
                                            bv_row[:].unsqueeze(1).to_broadcast([P, TT, P]), ALU.add).then_inc(v_evac, 1)
                elif ti in ROPED:
                    ri = ROPED.index(ti)
                    qt = k[:, ti, P:] if ti < 2 else q[:, ti - 3, :]
                    dve.wait_ge(rope_ready, hf * len(ROPED) + ri + 1)
                    nc.vector.tensor_tensor(gate[:, 0, :], ps[:, 2 + ri % 2, :], sin[:], ALU.mult)
                    st.link(nc.vector.tensor_tensor(qt, qt, cos[:], ALU.mult))
                    nc.vector.tensor_tensor(qt, qt, gate[:, 0, :], ALU.add).then_inc(rope_done, 1)
                    dve.wait_ge(rope_done, hf * len(ROPED) + ri + 1)
                s = tile_slot[ti]
                if ti == slot_last[s]:
                    lo_part(dve, hf, s + 2)
            for n in range(UNITS + 3):
                if n < UNITS:
                    b, (blk, p) = n % 2, divmod(n, HEADS // 2)
                    dve.wait_ge(scored, hf * UNITS + n + 1)
                    if n >= 2:
                        dve.wait_ge(exp_done, hf * UNITS + n - 1)
                    mask = masks[:, min(blk, 1), :]
                    for hh in range(2):
                        at = slice(256 * hh, 256 * hh + 256)
                        ins = nc.vector.tensor_tensor_reduce(out=scores[:, b, at], in0=ps[:, (4, 0)[b] + hh, 0:256], in1=mask, scale=1.0,
                                                             scalar=-3e38, op0=ALU.add, op1=ALU.max, accum_out=smax[:, b, hh:hh + 1])
                    st.link(ins)
                    snk = sinks8[:, 2 * p:2 * p + 2]
                    st.link(nc.vector.tensor_tensor(smax[:, b, :], smax[:, b, :], snk, ALU.max))
                    nc.vector.tensor_scalar(negmax[:, b, :], smax[:, b, :], -(HD ** -0.5), None, ALU.mult)
                    nc.vector.tensor_tensor(sdiff[:, b, :], snk, smax[:, b, :], ALU.subtract).then_inc(max_done, 1)
                if 1 <= n <= UNITS:
                    m = n - 1
                    b = m % 2
                    dve.wait_ge(exp_done, hf * UNITS + m + 1)
                    st.link(nc.vector.tensor_tensor(den[:, b, :], psum_row[:, b, :], sexp[:, b, :], ALU.add))
                    if m >= 3:
                        dve.wait_ge(scaled, hf * UNITS + m - 2)
                    nc.vector.reciprocal(rden[:, m % 3, :], den[:, b, :]).then_inc(rden_done, 1)
                if n >= 3:
                    m = n - 3
                    blk, p = divmod(m, HEADS // 2)
                    dve.wait_ge(pv_ready, hf * UNITS + m + 1)
                    nc.vector.tensor_copy(q[:, p, P * blk:P * blk + P], ps[:, (7, 3)[m % 2], 0:P]).then_inc(o_evac, 1)
            nc.vector.tensor_copy(k[:, :, 0:P], k[:, :, HALF:])
            nc.vector.tensor_copy(masks[:, 0, :], masks[:, 1, :])
            nc.vector.tensor_copy(v[:, 0, :], v[:, TT, :])
            for g in range(NG):
                dve.wait_ge(mix_ready, hf * NG + g + 1)
                nc.vector.tensor_scalar(pooled[:, g, :], ps[:, (0, 1, 4, 5)[g], :], bias[:, B_PS + g:B_PS + g + 1], None, ALU.mult).then_inc(mix_evac, 1)
            for m in range(KT):
                bank, g2 = 4 * (m % 2), 2 * (m % 2)
                dve.wait_ge(gate_done, hf * 2 * KT + 2 * m + 2)
                dve.wait_ge(br_ready, hf * KT + m + 1)
                nc.vector.tensor_tensor(gate[:, g2, :], ps[:, bank + 2, :], gate[:, g2, :], ALU.mult)
                st.link(nc.vector.tensor_tensor(gate[:, g2 + 1, :], ps[:, bank + 3, :], gate[:, g2 + 1, :], ALU.mult))
                nc.vector.tensor_tensor(merged[:, m, :], gate[:, g2, :], gate[:, g2 + 1, :], ALU.add).then_inc(merged_done, 1)
                if PROJ_SLOTS + m + 2 < SPLITS:
                    lo_part(dve, hf, PROJ_SLOTS + m + 2)
            for n in range(2):
                for t in range(TT):
                    dve.wait_ge(out_ready, hf * 2 * TT + n * TT + t + 1)
                    part = xs[:, t, 512 * n:512 * n + 512]
                    nc.vector.tensor_tensor(part, ps[:, n * TT + t, :], part, ALU.add).then_inc(x2_done, 1)
            dve.wait_ge(x2_done, hf * 2 * TT + 2 * TT)
            normalise(1, g2_row, h2_rows_done)

            dve.wait_ge(logits_ready, hf + 1)
            st.link(nc.vector.tensor_tensor(logits[:], ps[:, 2, 0:TT * E].rearrange("p (t e) -> p t e", e=E),
                                            br_row[:].unsqueeze(1).to_broadcast([P, TT, E]), ALU.add))
            dve.wait_ge(scattered, hf * 16 * TT * TOPK)
            for t in range(TT):
                tile_at = bass.ds(hf * TT + t, 1)
                g_t = gates[:, tile_at, :].rearrange("p a k -> p (a k)")
                of_t = gate_of[:, tile_at, :].rearrange("p a e -> p (a e)")
                st.link(nc.vector.max(top[:], logits[:, t, :]))
                nc.vector.tensor_scalar(neg_top[:], top[:, 0:1], -1.0, None, ALU.mult).then_inc(top_done, 1)
                st.link(nc.vector.max_index(top_i[:], top[:], logits[:, t, :]))
                st.link(nc.vector.tensor_copy(top_f[:], top_i[:]))
                for c in range(TOPK):
                    ins = nc.vector.tensor_scalar(onehot[:, c, :], e_row[:], top_f[:, c:c + 1], None, ALU.is_equal)
                st.link(ins)
                nc.vector.reduce_sum(chosen[:], onehot[:].rearrange("p k e -> p e k"), AX_X).then_inc(chosen_done, 1)
                dve.wait_ge(etop_done, hf * TT + t + 1)
                st.link(nc.vector.reciprocal(resum[:], esum[:]))
                st.link(nc.vector.tensor_scalar(g_t, etop[:], resum[:, 0:1], None, ALU.mult))
                st.link(nc.vector.tensor_tensor(picked[:], onehot[:], g_t.unsqueeze(2).to_broadcast([P, TOPK, E]), ALU.mult))
                st.link(nc.vector.reduce_sum(of_t, picked[:].rearrange("p k e -> p e k"), AX_X))
                dve.wait_ge(rank_ready, hf * TT + t + 1)
                st.link(nc.vector.tensor_tensor(slot_of[:], ps[:, 3, 0:E], base[:], ALU.add))
                nc.vector.tensor_tensor(base[:], ps[:, 3, E:2 * E], base[:], ALU.add)
                st.link(nc.vector.tensor_tensor(picked[:], onehot[:], slot_of[:].unsqueeze(1).to_broadcast([P, TOPK, E]), ALU.mult))
                st.link(nc.vector.reduce_sum(dest_f[:], picked[:], AX_X))
                nc.vector.tensor_copy(dest[:, t, :], dest_f[:]).then_inc(dest_done, 1)
                dve.wait_ge(dest_done, hf * TT + t + 1)
            assert st.n == MIX_VECTOR_STEPS, st.n

        st = Steps(dve, vstep, 2 * MIX_VECTOR_STEPS)
        dve.wait_ge(ready_const, 2)
        st.link(nc.vector.scalar_tensor_tensor(count[:], e_row[:], float(-SLOTS_PER_EXPERT), base[:], ALU.mult, ALU.add))
        for r in range(1, ROUNDS):
            ins = nc.vector.tensor_scalar(over[:, E * (r - 1):E * r], count[:], float(ITEM * r), None, ALU.is_gt)
        st.link(ins)
        st.link(nc.vector.tensor_tensor_scan(order, one_x, over, 0.0, ALU.mult, ALU.add))
        st.link(nc.vector.tensor_scalar(items_f[:], order[:, NX - 1:NX], float(E), None, ALU.add))
        nc.vector.tensor_copy(n_items[:], items_f[:])
        st.link(nc.vector.tensor_scalar(x_pick, order, part1[:, 0:1], None, ALU.is_equal))
        st.link(nc.vector.tensor_tensor(x_pick, x_pick, over, ALU.mult))
        nc.vector.tensor_tensor(x_expert, x_expert, x_pick, ALU.mult)
        st.link(nc.vector.tensor_tensor(x_base, x_base, x_pick, ALU.mult))
        nc.vector.reduce_sum(extra_f[:, 0:1], x_expert, AX_X)
        st.link(nc.vector.reduce_sum(extra_f[:, 1:2], x_base, AX_X))
        nc.vector.tensor_copy(extra_i[:], extra_f[:]).then_inc(items_done, 1)


def experts(nc, scope, keep, w_up, b_up, w_down, h2_dram, y_dram, slot_dram):
    def sb(name, shape, dt=F32):
        return scope.enter_context(nc.sbuf_tensor(name, shape, dt))

    def sem(name):
        return scope.enter_context(nc.semaphore(name))

    ps, ident, item_row, n_items = keep["ps"], keep["ident"], keep["item_row"], keep["n_items"]
    raw = sb("raw_e", [P, ITEM_SLOTS, SLOT])
    fetched = sb("fetched", [SUB, 2, 2], I32)
    in_work = sb("in_work", [SUB, 2, 2], I32)
    tokens = sb("tokens", [SUB, 2, D])
    xt = sb("xt", [P, KT, ITEM])
    act = sb("act", [P, KT, ITEM])
    glu, lin, sig = sb("glu", [P, 2, 2, ITEM]), sb("lin", [P, 2, 2, ITEM]), sb("sig", [P, 2, 2, ITEM])
    yt = sb("yt", [P, KT, ITEM])
    y = sb("y", [SUB, 2, D])
    bup_rows, bup_t = sb("bup_rows", [E, 2 * DFF]), sb("bup_t", [P, 2 * KT, E])
    bup = sb("bup", [P, 2 * KT])

    raw_loaded = [sem(f"raw_loaded_e{r}") for r in range(ITEM_SLOTS)]
    bup_loaded, bup_tr, bup_ready = sem("bup_loaded"), sem("bup_tr"), sem("bup_ready")
    fetch, copied, gathered, y_scattered = sem("fetch"), sem("copied"), sem("gathered"), sem("y_scattered")
    slot_used, xt_ready, xt_done = sem("slot_used"), sem("xt_ready"), sem("xt_done")
    up_read, glu_done, sig_done, act_done = sem("up_read"), sem("glu_done"), sem("sig_done"), sem("act_done")
    yt_done, y_ready, y_done = sem("yt_done"), sem("y_ready"), sem("y_done")
    bias_picked, ticked, y_free, vstep = sem("bias_picked"), sem("ticked"), sem("y_free"), sem("vstep_e")

    XT = [(0, 0, 3), (1, 3, 3), (1, 6, 2)]
    QUARTERS = 4
    VSTEPS = QUARTERS

    block = scope.enter_context(nc.Block())

    def n_of(eng):
        return eng.value_load(n_items[0:1, 0:1], min_val=E, max_val=MAX_ITEMS)

    @block.sync
    def _(sp):
        n = n_of(sp)
        sp.dma_start(bup_rows[:], b_up).then_inc(bup_loaded, 16)
        with sp.Fori(0, n) as item:
            e = sp.value_load(item_row[0:1, bass.ds(2 * item, 1)], min_val=0, max_val=E - 1)
            for s in range(ITEM_SLOTS):
                if s < UP_SLOTS:
                    quarter, which = divmod(s, 2)
                    w, c0 = w_up, DFF * which + 256 * quarter
                else:
                    w, c0 = w_down, 256 * (s - UP_SLOTS)
                sp.wait_ge(slot_used, item * ITEM_SLOTS + s + 1)
                sp.dma_start(raw[:, s, :].rearrange("p (k n) -> p k n", n=256),
                             w[bass.ds(e, 1)].rearrange("a (k p) n -> p (a k) n", p=P)[:, :, c0:c0 + 256]).then_inc(raw_loaded[s], 16)

    @block.scalar
    def _(se):
        def xt_part(item, i):
            bank, k0, nk = XT[i]
            se.wait_ge(xt_ready, item * len(XT) + i + 1)
            nc.scalar.activation(xt[:, k0:k0 + nk, :].rearrange("p k n -> p (k n)"), ps[:, bank, 0:nk * ITEM], ACT.Copy).then_inc(xt_done, 1)

        n = n_of(se)
        for i in range(len(XT)):
            xt_part(0, i)
        with se.Fori(0, n) as item:
            for j in range(QUARTERS):
                se.wait_ge(glu_done, item * QUARTERS + j + 1)
                nc.scalar.activation(sig[:, j % 2], glu[:, j % 2], ACT.Sigmoid, scale=ALPHA).then_inc(sig_done, 1)
            xt_part(item + 1, 0)
            xt_part(item + 1, 1)
            for d in range(DOWN_SLOTS):
                se.wait_ge(slot_used, (item + 1) * ITEM_SLOTS + UP_SLOTS + d + 1)
                nc.scalar.activation(yt[:, 2 * d:2 * d + 2, :].rearrange("p k n -> p (k n)"), ps[:, 3 - d % 2, 0:2 * ITEM], ACT.Copy).then_inc(yt_done, 1)
            xt_part(item + 1, 2)

    @block.vector
    def _(dve):
        dve.sem_inc(y_done, 2)
        n = n_of(dve)
        dve.wait_ge(bup_tr, 1)
        nc.vector.tensor_copy(bup_t[:, 0:KT, :], ps[:, 0, 0:KT * E].rearrange("p (m e) -> p m e", e=E))
        nc.vector.tensor_scalar(bup_t[:, KT:, :], ps[:, 0, KT * E:2 * KT * E].rearrange("p (m e) -> p m e", e=E), 1.0, None,
                                ALU.add).then_inc(bup_ready, 1)
        dve.wait_ge(bup_ready, 1)
        with dve.Fori(0, n) as item:
            st = Steps(dve, vstep, item * VSTEPS)
            e = dve.value_load(item_row[0:1, bass.ds(2 * item, 1)], min_val=0, max_val=E - 1)
            nc.vector.tensor_copy(bup[:], bup_t[:, :, bass.ds(e, 1)].rearrange("p m a -> p (m a)")).then_inc(bias_picked, 1)
            dve.wait_ge(bias_picked, item + 1)
            for j in range(QUARTERS):
                bank, b = 2 * (j % 2), j % 2
                for which, to, clamp, done in ((0, glu, LIMIT, glu_done), (1, lin, LIMIT + 1, up_read)):
                    dve.wait_ge(slot_used, (item + 1) * ITEM_SLOTS + 2 * j + which + 1)
                    for c in range(2):
                        col = KT * which + 2 * j + c
                        ins = nc.vector.tensor_scalar(to[:, b, c, :], ps[:, bank + which, ITEM * c:ITEM * c + ITEM],
                                                      bup[:, col:col + 1], clamp, ALU.add, ALU.min)
                    ins.then_inc(done, 1)
                dve.wait_ge(sig_done, item * QUARTERS + j + 1)
                st.link(nc.vector.tensor_tensor(sig[:, b], glu[:, b], sig[:, b], ALU.mult))
                dve.wait_ge(up_read, item * QUARTERS + j + 1)
                nc.vector.scalar_tensor_tensor(act[:, 2 * j:2 * j + 2, :].rearrange("p c n -> p (c n)"), lin[:, b].rearrange("p c n -> p (c n)"),
                                               1.0 - LIMIT, sig[:, b].rearrange("p c n -> p (c n)"), ALU.max, ALU.mult).then_inc(act_done, 1)
            dve.wait_ge(y_free, item + 1)
            for half in range(2):
                dve.wait_ge(y_ready, item * 2 + half + 1)
                for b in range(2):
                    ins = nc.vector.tensor_copy(y[:, b, 512 * half:512 * half + 512], ps[0:SUB, 4 + 2 * b + half, :])
                ins.then_inc(y_done, 1)

    @block.tensor
    def _(pe):
        pe.sem_inc(slot_used, ITEM_SLOTS)
        pe.wait_ge(bup_loaded, 16)
        for m in range(2 * KT):
            ins = nc.tensor.transpose(ps[:, 0, E * m:E * m + E], bup_rows[:, P * m:P * m + P], ident[0:E, 0:E])
        ins.then_inc(bup_tr, 1)
        pe.wait_ge(bup_ready, 1)
        n = n_of(pe)

        def transposes(item, i):
            bank, k0, nk = XT[i]
            if i == 0:
                pe.wait_ge(gathered, item * 32 + 32)
            if i == 2:
                pe.wait_ge(xt_done, item * len(XT) + 2)
            for kt in range(k0, k0 + nk):
                for b in range(2):
                    c = ITEM * (kt - k0) + SUB * b
                    ins = nc.tensor.transpose(ps[:, bank, c:c + SUB], tokens[:, b, P * kt:P * kt + P], ident[0:SUB, 0:SUB])
            ins.then_inc(xt_ready, 1)

        def y_transposes(item, d):
            pe.wait_ge(yt_done, item * DOWN_SLOTS + d + 1)
            for m in (2 * d, 2 * d + 1):
                for b in range(2):
                    ins = nc.tensor.transpose(ps[0:SUB, 4 + 2 * b + m // 4, P * (m % 4):P * (m % 4) + P],
                                              yt[:, m, SUB * b:SUB * b + SUB], ident[:])
            if d % 2:
                ins.then_inc(y_ready, 1)

        for i in range(len(XT)):
            transposes(0, i)
        with pe.Fori(0, n) as item:
            for s in range(ITEM_SLOTS):
                up = s < UP_SLOTS
                d = s - UP_SLOTS
                pe.wait_ge(raw_loaded[s], item * 16 + 16)
                if s == 0:
                    pe.wait_ge(xt_done, item * len(XT) + len(XT))
                if up:
                    quarter, which = divmod(s, 2)
                    bank = 2 * (quarter % 2) + which
                    if quarter >= 2 and not which:
                        pe.wait_ge(up_read, item * QUARTERS + quarter - 1)
                else:
                    bank = 3 - d % 2
                    if d == 0:
                        pe.wait_ge(up_read, item * QUARTERS + QUARTERS)
                        transposes(item + 1, 0)
                        transposes(item + 1, 1)
                        pe.wait_ge(act_done, item * QUARTERS + QUARTERS - 1)
                    if d >= 2:
                        pe.wait_ge(yt_done, item * DOWN_SLOTS + d - 1)
                w = raw[:, s, :].rearrange("p (k n) -> p k n", n=256)
                x = xt if up else act
                for c in range(2):
                    for kt in range(KT):
                        if s == UP_SLOTS and c == 0 and kt == KT - 2:
                            pe.wait_ge(act_done, item * QUARTERS + QUARTERS)
                        ins = nc.tensor.matmul(ps[:, bank, ITEM * c:ITEM * c + ITEM], w[:, kt, P * c:P * c + P], x[:, kt, :],
                                               start=kt == 0, stop=kt == KT - 1)
                ins.then_inc(slot_used, 1)
                if d == 1:
                    pe.wait_ge(y_done, item * 2 + 2)
                if d >= 1:
                    y_transposes(item, d - 1)
            transposes(item + 1, 2)
            y_transposes(item, DOWN_SLOTS - 1)

    @block.gpsimd
    def _(pool):
        pool.sem_inc(y_free, 1)
        n = n_of(pool)

        def held(eng):
            eng.sem_inc(ticked, 1)

        def fetch_item(item, first=False):
            b0 = pool.value_load(item_row[0:1, bass.ds(2 * item + 1, 1)], min_val=0, max_val=E * SLOTS_PER_EXPERT - ITEM)
            for b in range(2):
                pool.dma_start(fetched[:, b, :], slot_dram[bass.ds(b0 + SUB * b, SUB), :]).then_inc(fetch, 16)
            pool.wait_ge(fetch, item * 32 + 32)
            if not first:
                pool.wait_ge(xt_ready, item * len(XT))
            held(pool)
            for b in range(2):
                pool.indirect_dma_start(tokens[:, b, :], None, h2_dram,
                                        bass.IndirectOffsetOnAxis(ap=fetched[:, b, 1:2].bitcast(U32), axis=0)).then_inc(gathered, 16)

        fetch_item(0, first=True)
        with pool.Fori(0, n) as item:
            pool.wait_ge(gathered, item * 32 + 32)
            held(pool)
            nc.gpsimd.tensor_copy(in_work[:], fetched[:]).then_inc(copied, 1)
            pool.wait_ge(copied, item + 1)
            fetch_item(item + 1)
            pool.wait_ge(y_done, item * 2 + 4)
            held(pool)
            for b in range(2):
                pool.indirect_dma_start(y_dram, bass.IndirectOffsetOnAxis(ap=in_work[:, b, 0:1].bitcast(U32), axis=0),
                                        y[:, b, :], None, bounds_check=NCODES - 1, oob_is_err=False).then_inc(y_scattered, 16)
            pool.wait_ge(y_scattered, item * 32 + 32)
            pool.sem_inc(y_free, 1)


def combine(nc, scope, keep, x2_dram, y_dram, b_down, normf_g, out_rows):
    def sb(name, shape, dt=F32):
        return scope.enter_context(nc.sbuf_tensor(name, shape, dt))

    def sem(name):
        return scope.enter_context(nc.semaphore(name))

    ps, ident, gates, gate_of = keep["ps"], keep["ident"], keep["gates"], keep["gate_of"]
    TILES_C = SEQ // P
    ys = sb("ys", [P, 2, TOPK, D])
    acc = sb("acc", [P, 2, D])
    junk = sb("junk", [P, D])
    bd, gf_row = sb("bd", [E, D]), sb("gf_row", [P, D])
    g_t = sb("g_t", [E, TILES_C, P])
    sumsq, ms, rms, rstd = sb("sumsq_c", [P, 2]), sb("ms_c", [P, 2]), sb("rms_c", [P, 2]), sb("rstd_c", [P, 2])

    loaded = [sem("loaded0"), sem("loaded1")]
    c_loaded, stored = sem("c_loaded"), [sem("stored0"), sem("stored1")]
    gt_ready, gt_done, bias_ready, added, squared, ms_done, rms_done, normed = (
        sem("gt_ready"), sem("gt_done"), sem("bias_ready"), sem("added"), sem("squared"), sem("ms_done_c"), sem("rms_done_c"), sem("normed"))
    vstep = sem("vstep_c")
    VSTEPS = TOPK + 2
    y4 = y_dram.rearrange("(k t p) n -> t p k n", p=P, t=TILES_C)
    x8 = x2_dram.rearrange("(t p) n -> t p n", p=P)
    out8 = out_rows.rearrange("(t p) n -> t p n", p=P)
    block = scope.enter_context(nc.Block())

    @block.sync
    def _(sp):
        sp.dma_start(bd[:], b_down).then_inc(c_loaded, 16)
        sp.dma_start(gf_row[:], normf_g.rearrange("(a n) -> a n", a=1).to_broadcast([P, D])).then_inc(c_loaded, 16)
        with sp.Fori(0, TILES_C // 2) as i:
            for b in range(2):
                sp.wait_ge(stored[b], i * 16 + 16)
                for c in range(TOPK):
                    sp.dma_start(ys[:, b, c, :], y4[bass.ds(2 * i + b, 1), :, c, :].rearrange("a p n -> p (a n)")).then_inc(loaded[b], 16)
                sp.dma_start(acc[:, b, :], x8[bass.ds(2 * i + b, 1)].rearrange("a p n -> p (a n)")).then_inc(loaded[b], 16)

    @block.tensor
    def _(pe):
        for t in range(TILES_C):
            ins = nc.tensor.transpose(ps[0:E, t // 4, P * (t % 4):P * (t % 4) + P], gate_of[:, t, :], ident[:])
        ins.then_inc(gt_ready, 1)
        pe.wait_ge(gt_done, 1)
        pe.wait_ge(c_loaded, 32)
        for t in range(TILES_C):
            if t >= 2:
                pe.wait_ge(added, t - 1)
            for c in range(2):
                ins = nc.tensor.matmul(ps[:, 4 + 2 * (t % 2) + c, :], g_t[:, t, :], bd[:, 512 * c:512 * c + 512], start=True, stop=True)
            ins.then_inc(bias_ready, 1)

    @block.vector
    def _(dve):
        dve.wait_ge(gt_ready, 1)
        nc.vector.tensor_copy(g_t[:].rearrange("p t n -> p (t n)"), ps[0:E, 0:2, :].rearrange("p b n -> p (b n)")).then_inc(gt_done, 1)
        dve.wait_ge(c_loaded, 32)
        with dve.Fori(0, TILES_C // 2) as i:
            st = Steps(dve, vstep, i * 2 * VSTEPS)
            for b in range(2):
                g = gates[:, bass.ds(2 * i + b, 1), :].rearrange("p a k -> p (a k)")
                dve.wait_ge(loaded[b], i * 16 * (TOPK + 1) + 16 * (TOPK + 1))
                for c in range(TOPK):
                    st.link(nc.vector.scalar_tensor_tensor(acc[:, b, :], ys[:, b, c, :], g[:, c:c + 1], acc[:, b, :], ALU.mult, ALU.add))
                dve.wait_ge(bias_ready, 2 * i + b + 1)
                nc.vector.tensor_tensor(acc[:, b, :], ps[:, 4 + 2 * b:6 + 2 * b, :].rearrange("p a n -> p (a n)"), acc[:, b, :], ALU.add).then_inc(added, 1)
                dve.wait_ge(squared, 2 * i + b + 1)
                nc.vector.tensor_scalar(ms[:, b:b + 1], sumsq[:, b:b + 1], 1.0 / D, EPS, ALU.mult, ALU.add).then_inc(ms_done, 1)
                dve.wait_ge(rms_done, 2 * i + b + 1)
                st.link(nc.vector.reciprocal(rstd[:, b:b + 1], rms[:, b:b + 1]))
                st.link(nc.vector.scalar_tensor_tensor(acc[:, b, :], acc[:, b, :], rstd[:, b:b + 1], gf_row[:], ALU.mult, ALU.mult))
                dve.sem_inc(normed, 1)
            assert st.n == 2 * VSTEPS, st.n

    @block.scalar
    def _(act):
        for b in range(2):
            act.sem_inc(stored[b], 16)
        with act.Fori(0, TILES_C // 2) as i:
            for b in range(2):
                act.wait_ge(added, 2 * i + b + 1)
                nc.scalar.activation(junk[:], acc[:, b, :], ACT.Square, accum_out=sumsq[:, b:b + 1]).then_inc(squared, 1)
                act.wait_ge(ms_done, 2 * i + b + 1)
                nc.scalar.activation(rms[:, b:b + 1], ms[:, b:b + 1], ACT.Sqrt).then_inc(rms_done, 1)
                act.wait_ge(normed, 2 * i + b + 1)
                act.dma_start(out8[bass.ds(2 * i + b, 1)].rearrange("a p n -> p (a n)"), acc[:, b, :]).then_inc(stored[b], 16)
        for b in range(2):
            act.wait_ge(stored[b], 16 * (TILES_C // 2) + 16)


INPUTS = ["x", "positions", "norm1_g", "w_in", "b_in", "attn_sinks", "w_attn_br", "pool_w", "pool_scale", "w_pool_br",
          "w_out", "norm2_g", "w_router", "b_router", "w_up", "b_up", "w_down", "b_down", "normf_g"]


def kernel(**inputs):
    import concourse.bacc as bacc
    from concourse.bass_utils import run_bass_kernel_spmd

    nc = bacc.Bacc("TRN2", target_bir_lowering=False, num_devices=1)
    arrays = {f"in_{n}": np.ascontiguousarray(inputs[n]) for n in INPUTS}
    arrays.update({f"in_{n}": a for n, a in shape_constants().items()})
    args = [nc.dram_tensor(n, a.shape, mybir.dt.from_np(a.dtype), kind="ExternalInput").ap() for n, a in arrays.items()]
    out = nc.dram_tensor("out_0", [1, SEQ, D], F32, kind="ExternalOutput").ap()
    decoder_layer(nc, *args, out)
    return run_bass_kernel_spmd(nc, [arrays], core_ids=[0]).results[0]["out_0"]
```

```python
from contextlib import ExitStack

import numpy as np

import concourse.bass as bass
from concourse import mybir

F32 = mybir.dt.float32
F32R = mybir.dt.float32r
I32 = mybir.dt.int32
U32 = mybir.dt.uint32
ALU = mybir.AluOpType
ACT = mybir.ActivationFunctionType
AX_X = mybir.AxisListType.X

P = 128
D = 1024
SEQ = 1024
KT = D // P
HALF = 512
TT = HALF // P
HEADS, KVH, HD = 16, 2, 64
ROPE_DIM, ROPE_THETA = HD // 4, 500000.0
PW = D // 2
POOL_WINDOWS = (2, 4, 8, 16)
NG = len(POOL_WINDOWS)
HIST = 16
O_K = HEADS * HD
O_V = O_K + KVH * HD
O_U = O_V + KVH * HD
O_GA = O_U + PW
O_GP = O_GA + D
E, TOPK, DFF = 32, 4, 1024
EPS = 1e-5
ALPHA, LIMIT = 1.702, 7.0
NEG = -1e30

ITEM = 168
WIDTHS = (88, 104, 112, 120, 128, 136, 144, 152, 168)
SUB = ITEM // 2
ROUNDS = -(-SEQ // ITEM)
SLOTS_PER_EXPERT = ROUNDS * ITEM
NCODES = SEQ * TOPK
MAX_ITEMS = E + NCODES // ITEM
ITEM_ROW = 64
FREE_CODE = 1 << 20

RAW = 4
SPLIT = 2
SLOT = 2048

PROJ_SLOTS = 8
GATE0 = PROJ_SLOTS
OUT0 = GATE0 + 2 * KT
MIX_SLOTS = OUT0 + 4
SPLITS = PROJ_SLOTS + KT + 4
TILES = ["k0", "k1", "v"] + [f"q{i}" for i in range(8)] + [f"u{i}" for i in range(4)]
ROPED = [0, 1] + list(range(3, 11))
UNITS = TT * HEADS // 2
B_Q, B_U, B_GA, B_GP, B_PS, NB = 2, 10, 14, 22, 30, 34

UP_SLOTS, DOWN_SLOTS = 8, 4
ITEM_SLOTS = UP_SLOTS + DOWN_SLOTS


def rope_freqs():
    half = ROPE_DIM // 2
    f = np.power(np.float32(ROPE_THETA), -np.arange(half, dtype=np.float32) * np.float32(2.0 / ROPE_DIM))
    col = np.zeros((P, 1), np.float32)
    for h in range(P // HD):
        for j in range(ROPE_DIM):
            col[h * HD + j, 0] = f[j % half]
    return col


def shape_constants():
    half = ROPE_DIM // 2
    swap = np.zeros((P, P), np.float32)
    for h in range(P // HD):
        for j in range(half):
            swap[h * HD + j + half, h * HD + j] = -1.0
            swap[h * HD + j, h * HD + j + half] = 1.0
    q, k = np.arange(P)[:, None], np.arange(2 * P)[None, :]
    dist = q + P - k
    band = (dist >= 0) & (dist < P)
    masks = np.stack([np.where(band & (k >= P), 0.0, NEG), np.where(band, 0.0, NEG)], 1).astype(np.float32)
    fix = np.ones((P, 2, NG, HIST), np.float32)
    for g, w in enumerate(POOL_WINDOWS):
        fix[:, 0, g, :] = w / np.minimum(np.arange(1, HIST + 1), w)
    return {
        "c_ident": np.eye(P, dtype=np.float32),
        "c_before": np.triu(np.ones((P, P), np.float32), 1),
        "c_swap": swap,
        "c_masks": masks,
        "c_freq": rope_freqs(),
        "c_fix": fix.reshape(P, 2, NG * HIST),
    }


def cut_pi():
    two_pi, parts = 2 * np.pi, []
    for _ in range(2):
        m, e = np.frexp(two_pi)
        part = float(np.floor(m * 256) / 256 * 2.0**e)
        parts.append(part)
        two_pi -= part
    return parts + [float(np.float32(two_pi))]


class Steps:

    def __init__(self, eng, sem, base=0):
        self.eng, self.sem, self.base, self.n = eng, sem, base, 0

    def done(self, ins):
        self.n += 1
        ins.then_inc(self.sem, 1)
        return self.n

    def wait(self, n=None):
        self.eng.wait_ge(self.sem, self.base + (self.n if n is None else n))

    def link(self, ins):
        self.done(ins)
        self.wait()


N_CONSTS = 19
ROUTE_AT = 1
MIX_POOL_STEPS = 22


def decoder_layer(nc, x, positions, norm1_g, w_in, b_in, attn_sinks, w_attn_br, pool_w, pool_scale,
                  w_pool_br, w_out, norm2_g, w_router, b_router, w_up, b_up, w_down, b_down, normf_g,
                  c_ident, c_before, c_swap, c_masks, c_freq, c_fix, out):
    x_rows = x[0]
    out_rows = out[0]
    w_in, w_attn, w_pool, w_o = w_in[0], w_attn_br[0], w_pool_br[0], w_out[0]
    w_up, w_down = w_up[0], w_down[0]

    x2_dram = nc.dram_tensor("x2_rows", [SEQ, D], F32, kind="Internal").ap()
    h2_dram = nc.dram_tensor("h2_rows", [SEQ, D], F32, kind="Internal").ap()
    y_dram = nc.dram_tensor("y_rows", [NCODES, D], F32, kind="Internal").ap()
    slot_dram = nc.dram_tensor("slot_entries", [E * SLOTS_PER_EXPERT, 2], I32, kind="Internal").ap()
    item_dram = nc.dram_tensor("item_entries", [ITEM_ROW, 3], I32, kind="Internal").ap()

    with ExitStack() as whole:
        def sb(name, shape, dt=F32, scope=whole):
            return scope.enter_context(nc.sbuf_tensor(name, shape, dt))

        ps = whole.enter_context(nc.psum_tensor("banks", [P, 8, 512], F32))
        keep = {
            "ps": ps,
            "ident": sb("ident", [P, P]),
            "gates": sb("gates", [P, SEQ // P, TOPK]),
            "gate_of": sb("gate_of", [P, SEQ // P, E]),
            "item_row": sb("item_row", [1, 3 * ITEM_ROW], I32),
            "n_items": sb("n_items", [P, 1], I32),
        }
        with ExitStack() as scope:
            mixer(nc, scope, keep, x_rows, positions, norm1_g, w_in, b_in, attn_sinks, w_attn, pool_w[0],
                  pool_scale, w_pool, w_o, norm2_g, w_router[0], b_router, c_ident, c_before, c_swap,
                  c_masks, c_freq, c_fix, x2_dram, h2_dram, slot_dram, item_dram)
        x2 = sb("x2", [P, SEQ // P, D])
        with ExitStack() as scope:
            experts(nc, scope, keep, w_up, b_up[0], w_down, h2_dram, y_dram, slot_dram, x2_dram, x2)
        with ExitStack() as scope:
            combine(nc, scope, keep, x2, y_dram, b_down[0], normf_g, out_rows)


def mixer(nc, scope, keep, x_rows, positions, norm1_g, w_in, b_in, attn_sinks, w_attn, pool_w,
          pool_scale, w_pool, w_o, norm2_g, w_router, b_router, c_ident, c_before, c_swap, c_masks,
          c_freq, c_fix, x2_dram, h2_dram, slot_dram, item_dram):
    def sb(name, shape, dt=F32):
        return scope.enter_context(nc.sbuf_tensor(name, shape, dt))

    def sem(name):
        return scope.enter_context(nc.semaphore(name))

    ps, ident = keep["ps"], keep["ident"]
    gates, gate_of = keep["gates"], keep["gate_of"]
    item_row, n_items = keep["item_row"], keep["n_items"]

    before = sb("before", [P, P])
    ones = sb("ones", [P, P])
    swap = sb("swap", [P, P])
    masks = sb("masks", [P, 2, 2 * P])
    freq = sb("freq", [P, 1])
    fix = sb("fix", [P, 2, NG * HIST])
    g1_row, g2_row = sb("g1_row", [P, D]), sb("g2_row", [P, D])
    bv_row, br_row = sb("bv_row", [P, P]), sb("br_row", [P, E])
    sinks, sinks8 = sb("sinks", [P, HEADS]), sb("sinks8", [P, HEADS])
    bias_rows, bias = sb("bias_rows", [NB, P]), sb("bias", [P, NB])
    pool_mix = sb("pool_mix", [P, NG, P])
    router = sb("router", [P, KT, E])
    pos_i = sb("pos_i", [P, HALF], I32)
    cos, sin = sb("cos", [P, HALF]), sb("sin", [P, HALF])

    xs = sb("xs", [P, TT, D])
    rows = sb("rows", [P, TT, D])
    h_hi, h_lo = sb("h_hi", [P, KT, HALF], F32R), sb("h_lo", [P, KT, HALF], F32R)
    q = sb("q", [P, KT, HALF])
    k = sb("k", [P, KVH, P + HALF])
    v = sb("v", [P, TT + 1, P])
    u = sb("u", [P, NG, HIST + HALF])
    pooled = sb("pooled", [P, NG, HALF])
    gate = sb("gate", [P, 4, HALF])
    raw = sb("raw_m", [P, RAW, SLOT])
    w_hi, w_lo = sb("w_hi_m", [P, SPLIT, SLOT], F32R), sb("w_lo_m", [P, SPLIT, SLOT], F32R)

    h2 = q[:].rearrange("p k n -> p (k n)").rearrange("p (t n) -> p t n", n=D)
    flat = rows[:].rearrange("p t n -> p (t n)")
    merged = flat.rearrange("p (m n) -> p m n", n=HALF)
    scores = flat[:, 0:1024].rearrange("p (b n) -> p b n", b=2)
    probs = flat[:, 1024:3072].rearrange("p (b n) -> p b n", b=4)
    probs_t = flat[:, 3072:4096].rearrange("p (b n) -> p b n", b=2)
    h2_t = raw[:, 2:4, :].rearrange("p s n -> p (s n)").rearrange("p (k n) -> p k n", n=HALF)
    squares = gate[:].rearrange("p (b a) n -> p b (a n)", b=2)
    v_t = gate[:, 1, :]
    wide = gate[:].rearrange("p a n -> p (a n)")
    win = [wide[:, 0:HIST + HALF], wide[:, HIST + HALF:2 * (HIST + HALF)]]
    diag = [wide[:, 2 * (HIST + HALF) + 2 * P * i:][:, 0:2 * P] for i in range(3)]

    sumsq, rms, rstd = sb("sumsq", [P, TT]), sb("rms", [P, TT]), sb("rstd", [P, TT])
    smax, negmax = sb("smax", [P, 2, 2]), sb("negmax", [P, 2, 2])
    sdiff, sexp = sb("sdiff", [P, 2, 2]), sb("sexp", [P, 2, 2])
    psum_row, den, rden = sb("prob_sum", [P, 2, 2]), sb("den", [P, 2, 2]), sb("rden", [P, 2, 2])
    logits = sb("logits", [P, TT, E])
    top, top_i, top_f = sb("top", [P, TT, 8]), sb("top_i", [P, TT, 8], U32), sb("top_f", [P, TT, TOPK])
    top_rel, etop, esum, resum = sb("top_rel", [P, TT, TOPK]), sb("etop", [P, TT, TOPK]), sb("esum", [P, TT]), sb("resum", [P, TT])
    onehot, chosen = sb("onehot", [P, TT * TOPK, E]), sb("chosen", [P, TT, E])
    e_row, base = sb("e_row", [P, E]), sb("base", [P, E])
    slot_of = sb("slot_of", [P, TT, E])
    picked = gate[:, 3, :].rearrange("p (c e) -> p c e", e=E)
    dest_f, dest = sb("dest_f", [P, TT * TOPK]), sb("dest", [P, TT, TOPK], I32)
    codes = sb("codes", [P, SEQ // P, 2 * TOPK], I32)
    half_codes = sb("half_codes", [P, TT, 2 * TOPK], I32)
    free_slots = pooled[:].rearrange("p g n -> p (g n)").bitcast(I32)[:, 0:2 * E * SLOTS_PER_EXPERT // P]
    NX = (ROUNDS - 1) * E
    over, order, one_x, x_expert, x_base, x_pick, x_count = (wide[:, NX * i:NX * i + NX] for i in range(7))
    count = sb("count", [P, E])
    part1 = sb("part1", [P, 1])
    extra_f, items_f = sb("extra_f", [P, 3]), sb("items_f", [P, 1])
    extra_i, first_i = sb("extra_i", [P, 3], I32), sb("first_i", [P, 3], I32)
    first_n = sb("first_n", [P, 1])

    early_loaded, const_loaded, pos_loaded = sem("early_loaded"), sem("const_loaded"), sem("pos_loaded")
    x_loaded = [sem(f"x_loaded{t}") for t in range(TT)]
    x2_stored = [sem(f"x2_stored{t}") for t in range(TT)]
    raw_loaded = [sem(f"raw_loaded{r}") for r in range(RAW)]
    ready_const, table_free = sem("ready_const"), sem("table_free")
    bias_t, bias_done = sem("bias_t"), sem("bias_done")
    angles, cs_ready, sumsq_done, ms_done, rms_done = sem("angles"), sem("cs_ready"), sem("sumsq_done"), sem("ms_done"), sem("rms_done")
    rows_done, h2_rows_done = sem("rows_done"), sem("h2_rows_done")
    hi_done, lo_done = sem("hi_done"), sem("lo_done")
    xt_ready, h_hi_done, h_lo_done = sem("xt_ready"), sem("h_hi_done"), sem("h_lo_done")
    proj_ready, proj_evac, v_evac = sem("proj_ready"), sem("proj_evac"), sem("v_evac")
    v_ready = sem("v_ready")
    rope_ready, rope_done = sem("rope_ready"), sem("rope_done")
    scored, max_done, exp_done = sem("scored"), sem("max_done"), sem("exp_done")
    diag_done, pt_ready, pt_evac = sem("diag_done"), sem("pt_ready"), sem("pt_evac")
    pv_ready, o_evac = sem("pv_ready"), sem("o_evac")
    mix_ready, mix_evac = sem("mix_ready"), sem("mix_evac")
    gate_mm, gate_done, br_ready, merged_done = sem("gate_mm"), sem("gate_done"), sem("br_ready"), sem("merged_done")
    m_hi_done, m_lo_done, out_half_used = sem("m_hi_done"), sem("m_lo_done"), sem("out_half_used")
    out_ready, x2_done, h2_stored = sem("out_ready"), sem("x2_done"), sem("h2_stored")
    h2t_evac, logits_ready, top_done, etop_done = sem("h2t_evac"), sem("logits_ready"), sem("top_done"), sem("etop_done")
    chosen_done, rank_ready, dest_done, scattered = sem("chosen_done"), sem("rank_ready"), sem("dest_done"), sem("scattered")
    logits_read = sem("logits_read")
    codes_done, hist_done = sem("codes_done"), sem("hist_done")
    items_done, items_stored, items_loaded = sem("items_done"), sem("items_stored"), sem("items_loaded")
    vstep, pstep = sem("vstep"), sem("pstep")

    NPE = len(TILES)
    tile_slot = {0: 0, 1: 0, 2: 1, **{3 + i: 2 + i // 2 for i in range(8)}, **{11 + i: 6 + i // 2 for i in range(4)}}
    slot_last = {s: max(t for t, at in tile_slot.items() if at == s) for s in range(PROJ_SLOTS)}

    def cols(w, c0, n):
        return w.rearrange("(k p) n -> p k n", p=P)[:, :, c0:c0 + n]

    def slot_view(t, r, n):
        return t[:, r, :].rearrange("p (k n) -> p k n", n=n)

    loads = []
    dst = [slot_view(raw, r, 256) for r in range(RAW)]
    for s in range(MIX_SLOTS):
        d, r = dst[s % RAW], s % RAW
        if s == 0:
            loads.append([(d[:, :, 64 * i:64 * i + 64], cols(w_in, O_K + 64 * (i // 2), 64)) for i in range(4)])
        elif s == 1:
            loads.append([(raw[:, r, 0:1024].rearrange("p (k n) -> p k n", n=P), cols(w_in, O_V, P))])
        elif s < 6:
            loads.append([(d, cols(w_in, 256 * (s - 2), 256))])
        elif s < PROJ_SLOTS:
            loads.append([(d, cols(w_in, O_U + 256 * (s - 6), 256))])
        elif s < OUT0:
            m, branch = divmod(s - GATE0, 2)
            if branch:
                loads.append([(raw[:, r, 0:1024].rearrange("p (k n) -> p k n", n=P), cols(w_attn, P * m, P)),
                              (raw[:, r, 1024:1536].rearrange("p (k n) -> p k n", n=P), cols(w_pool, P * m, P))])
            else:
                loads.append([(d[:, :, 0:P], cols(w_in, O_GA + P * m, P)), (d[:, :, P:2 * P], cols(w_in, O_GP + P * m, P))])
        else:
            n, kh = divmod(s - OUT0, 2)
            loads.append([(slot_view(raw, r, 512), cols(w_o, 512 * n, 512)[:, 4 * kh:4 * kh + 4, :])])
    arrived, per_half = {}, [0] * RAW
    for s in range(MIX_SLOTS):
        per_half[s % RAW] += 16 * len(loads[s])
        arrived[s] = per_half[s % RAW]
    split_slots = list(range(PROJ_SLOTS)) + [GATE0 + 2 * m for m in range(KT)] + list(range(OUT0, MIX_SLOTS))

    def raw_arrived(eng, hf, s):
        eng.wait_ge(raw_loaded[s % RAW], hf * per_half[s % RAW] + arrived[s])

    block = scope.enter_context(nc.Block())

    def load_constants(sp):
        consts = [(before[:], c_before), (swap[:], c_swap), (masks[:], c_masks), (fix[:], c_fix), (g2_row[:], norm2_g[0:1, :].to_broadcast([P, D])),
                  (bv_row[:], b_in[0:1, O_V:O_U].to_broadcast([P, P])), (br_row[:], b_router[0:1, :].to_broadcast([P, E])),
                  (sinks[:], attn_sinks[0:1, :].to_broadcast([P, HEADS])),
                  (pool_mix[:], pool_w.rearrange("g c d -> c g d")),
                  (router[:], w_router.rearrange("(k p) e -> p k e", p=P))]
        for kv in range(KVH):
            for half in range(2):
                consts.append((bias_rows[kv:kv + 1, 64 * half:64 * half + 64], b_in[0:1, O_K + 64 * kv:O_K + 64 * kv + 64]))
        for at, c0, n in ((B_Q, 0, 8), (B_U, O_U, NG), (B_GA, O_GA, 8), (B_GP, O_GP, 8)):
            consts.append((bias_rows[at:at + n, :], b_in[0, c0:c0 + n * P].rearrange("(r c) -> r c", c=P)))
        consts.append((bias_rows[B_PS:NB, :], pool_scale[0, :].rearrange("(r c) -> r c", c=P)))
        assert len(consts) == N_CONSTS
        for to, src in consts:
            sp.dma_start(to, src).then_inc(const_loaded, 16)

    def load_positions(sp, hf):
        sp.dma_start(pos_i[:], positions[:, HALF * hf:HALF * hf + HALF].to_broadcast([P, HALF])).then_inc(pos_loaded, 16)

    @block.sync
    def _(sp):
        for hf in range(2):
            for t in range(TT):
                if hf:
                    sp.wait_ge(x2_stored[t], hf * 16)
                    sp.wait_ge(h2_rows_done, (hf - 1) * TT + t + 1)
                sp.dma_start(xs[:, t, :], x_rows.rearrange("(h t p) n -> h t p n", p=P, t=TT)[hf, t]).then_inc(x_loaded[t], 16)
            if hf == 0:
                load_positions(sp, 0)
            for s in range(MIX_SLOTS):
                if s == GATE0 and hf == 0:
                    sp.wait_ge(angles, 1)
                    load_positions(sp, 1)
                last = s - RAW
                if last < 0:
                    sp.wait_ge(out_ready, hf * 2 * TT)
                    if s == 2:
                        sp.wait_ge(logits_ready, hf)
                elif last in split_slots:
                    sp.wait_ge(lo_done, hf * SPLITS + split_slots.index(last) + 1)
                else:
                    sp.wait_ge(br_ready, hf * KT + (last - GATE0) // 2 + 1)
                for to, src in loads[s]:
                    sp.dma_start(to, src).then_inc(raw_loaded[s % RAW], 16)
                if s == 1 and hf == 0:
                    load_constants(sp)
        sp.wait_ge(items_done, 1)
        sp.dma_start(item_dram[0:E, :], first_i[0:E, :]).then_inc(items_stored, 16)
        sp.dma_start(item_dram[E:ITEM_ROW, :], extra_i[0:ITEM_ROW - E, :]).then_inc(items_stored, 16)
        sp.wait_ge(items_stored, 32)
        sp.dma_start(item_row[:], item_dram.rearrange("(a i) c -> a (i c)", a=1)).then_inc(items_loaded, 16)
        sp.wait_ge(items_loaded, 16)

    def hi_part(act, hf, si):
        s = split_slots[si]
        raw_arrived(act, hf, s)
        if si >= SPLIT:
            if si - SPLIT < PROJ_SLOTS:
                act.wait_ge(proj_ready, hf * len(TILES) + slot_last[si - SPLIT] + 1)
            elif si - SPLIT < PROJ_SLOTS + KT:
                act.wait_ge(gate_mm, hf * 2 * KT + 2 * (si - SPLIT - PROJ_SLOTS) + 2)
            elif si == SPLITS - 2:
                act.wait_ge(out_half_used, hf * 2 + 1)
            else:
                act.wait_ge(out_ready, hf * 2 * TT + TT)
        n = 1024 if s == 1 else SLOT
        nc.scalar.activation(w_hi[:, si % SPLIT, 0:n], raw[:, s % RAW, 0:n], ACT.Copy).then_inc(hi_done, 1)

    def lo_part(dve, hf, si):
        s = split_slots[si]
        dve.wait_ge(hi_done, hf * SPLITS + si + 1)
        n = 1024 if s == 1 else SLOT
        nc.vector.tensor_tensor(w_lo[:, si % SPLIT, 0:n], raw[:, s % RAW, 0:n],
                                w_hi[:, si % SPLIT, 0:n].bitcast(F32), ALU.subtract).then_inc(lo_done, 1)

    @block.scalar
    def _(act):
        for to, src in ((g1_row[:], norm1_g[0:1, :].to_broadcast([P, D])), (ident[:], c_ident), (freq[:], c_freq)):
            act.dma_start(to, src).then_inc(early_loaded, 16)
        def row_stats(hf, second):
            first = (2 * hf + second) * TT
            for t in range(TT + 1):
                if t < TT:
                    if second:
                        act.wait_ge(x2_done, hf * 2 * TT + TT + t + 1)
                    else:
                        act.wait_ge(x_loaded[t], 16 * hf + 16)
                    nc.scalar.activation(squares[:, t % 2, :], xs[:, t, :], ACT.Square, accum_out=sumsq[:, t:t + 1]).then_inc(sumsq_done, 1)
                if t >= 1:
                    act.wait_ge(ms_done, first + t)
                    nc.scalar.activation(rms[:, t - 1:t], rms[:, t - 1:t], ACT.Sqrt).then_inc(rms_done, 1)

        def sines(hf):
            act.wait_ge(angles, hf + 1)
            nc.scalar.activation(sin[:], gate[:, 2, :], ACT.Sin)
            nc.scalar.activation(cos[:], gate[:, 3, :], ACT.Sin).then_inc(cs_ready, 1)
            act.wait_ge(cs_ready, hf + 1)

        def merged_hi(hf, m):
            if m == 0:
                act.wait_ge(gate_mm, hf * 2 * KT + 2 * KT)
            act.wait_ge(merged_done, hf * KT + m + 1)
            nc.scalar.activation(h_hi[:, m, :], merged[:, m, :], ACT.Copy).then_inc(m_hi_done, 1)

        def top_exp(hf):
            act.wait_ge(top_done, hf + 1)
            nc.scalar.activation(etop[:], top_rel[:], ACT.Exp).then_inc(etop_done, 1)

        row_stats(0, 0)
        for hf in range(2):
            hi_part(act, hf, 0)
            act.wait_ge(h2_stored, hf * 16 * TT)
            for kt in range(KT):
                act.wait_ge(xt_ready, hf * 2 * KT + kt + 1)
                nc.scalar.activation(h_hi[:, kt, :], ps[:, kt, :], ACT.Copy).then_inc(h_hi_done, 1)
            hi_part(act, hf, 1)
            if hf == 0:
                sines(0)
                act.wait_ge(bias_done, 1)
            for ti, name in enumerate(TILES):
                act.wait_ge(proj_ready, hf * len(TILES) + ti + 1)
                if name == "v":
                    nc.scalar.activation(v_t, ps[:, ti % 2, :], ACT.Copy).then_inc(proj_evac, 1)
                else:
                    kind, i = name[0], int(name[1:])
                    to, b = {"k": (k[:, i % 2, P:], i), "q": (q[:, i, :], B_Q + i),
                             "u": (u[:, i % NG, HIST:], B_U + i)}[kind]
                    if name == "u0":
                        act.wait_ge(hist_done, hf)
                    nc.scalar.activation(to, ps[:, ti % 2, :], ACT.Identity, bias=bias[:, b:b + 1]).then_inc(proj_evac, 1)
                s = tile_slot[ti]
                if ti == slot_last[s]:
                    hi_part(act, hf, s + 2)
                if hf and ti == ROUTE_AT + 1:
                    top_exp(hf - 1)
            for n in range(UNITS + 3):
                if n < UNITS:
                    b = n % 2
                    act.wait_ge(max_done, hf * UNITS + n + 1)
                    if n >= 4:
                        act.wait_ge(pt_ready, hf * UNITS + n - 3)
                    for hh in range(2):
                        nc.scalar.activation(probs[:, n % 4, 256 * hh:256 * hh + 256], scores[:, b, 256 * hh:256 * hh + 256],
                                             ACT.Exp, bias=negmax[:, b, hh:hh + 1], scale=HD ** -0.5,
                                             accum_out=psum_row[:, b, hh:hh + 1])
                    nc.scalar.activation(sexp[:, b, :], sdiff[:, b, :], ACT.Exp, scale=HD ** -0.5).then_inc(exp_done, 1)
                if n >= 3:
                    m = n - 3
                    act.wait_ge(pt_ready, hf * UNITS + m + 1)
                    if m >= 2:
                        act.wait_ge(pv_ready, hf * UNITS + m - 1)
                    nc.scalar.activation(probs_t[:, m % 2, :], ps[:, (6, 2)[m % 2], :], ACT.Copy).then_inc(pt_evac, 1)
            for m in range(KT):
                for j, b in ((0, B_GA), (1, B_GP)):
                    act.wait_ge(gate_mm, hf * 2 * KT + 2 * m + j + 1)
                    if m >= 2:
                        act.wait_ge(merged_done, hf * KT + m - 1)
                    if m == 0 and j == 0:
                        act.wait_ge(hist_done, hf + 1)
                    nc.scalar.activation(gate[:, 2 * (m % 2) + j, :], ps[:, 4 * (m % 2) + j, :], ACT.Sigmoid,
                                         bias=bias[:, b + m:b + m + 1]).then_inc(gate_done, 1)
                if m == KT - 1:
                    for done in range(KT - 1):
                        merged_hi(hf, done)
                hi_part(act, hf, PROJ_SLOTS + m + 2)
            merged_hi(hf, KT - 1)
            hi_part(act, hf, SPLITS - 2)
            hi_part(act, hf, SPLITS - 1)
            if hf == 0:
                sines(1)
            row_stats(hf, 1)
            for kt in range(KT):
                act.wait_ge(xt_ready, hf * 2 * KT + KT + kt + 1)
                nc.scalar.activation(h2_t[:, kt, :], ps[:, kt, :], ACT.Copy).then_inc(h2t_evac, 1)
            if hf == 0:
                row_stats(1, 0)
        top_exp(1)

    @block.tensor
    def _(pe):
        def transposes(hf, second):
            for t in range(TT):
                pe.wait_ge(h2_rows_done if second else rows_done, hf * TT + t + 1)
                for kt in range(KT):
                    ins = nc.tensor.transpose(ps[:, kt, P * t:P * t + P], (h2 if second else rows)[:, t, P * kt:P * kt + P], ident[:])
                    if t == TT - 1:
                        ins.then_inc(xt_ready, 1)

        def three_pass(to, pairs, first=True, last=True, ready=None):
            n = len(pairs)
            for i, (whi, wlo, mhi, mlo) in enumerate(pairs):
                if ready is not None:
                    ready(i)
                nc.tensor.matmul(to, whi, mhi, start=first and i == 0, stop=False)
                nc.tensor.matmul(to, whi, mlo, start=False, stop=False)
                ins = nc.tensor.matmul(to, wlo, mhi, start=False, stop=last and i == n - 1)
            return ins

        def ranks(hf):
            pe.wait_ge(chosen_done, hf + 1)
            for t in range(TT + 1):
                at = ps[:, 7, E * t:E * t + E]
                if t < TT:
                    nc.tensor.matmul(at, before[:], chosen[:, t, :], start=True, stop=t == 0)
                for past in range(t):
                    ins = nc.tensor.matmul(at, ones[:], chosen[:, past, :], start=t == TT and past == 0, stop=past == t - 1)
            ins.then_inc(rank_ready, 1)

        pe.wait_ge(early_loaded, 48)
        transposes(0, 0)
        pe.wait_ge(const_loaded, 16 * N_CONSTS)
        pe.wait_ge(ready_const, 1)
        for hf in range(2):

            def rope(ri):
                ti = ROPED[ri]
                src = k[:, ti, P:] if ti < 2 else q[:, ti - 3, :]
                pe.wait_ge(proj_evac, hf * NPE + ti + 1)
                if ri >= 2:
                    pe.wait_ge(rope_done, hf * len(ROPED) + ri - 1)
                nc.tensor.matmul(ps[:, 2 + ri % 2, :], swap[:], src, start=True, stop=True).then_inc(rope_ready, 1)

            roped = 0
            for ti, name in enumerate(TILES):
                s = tile_slot[ti]
                pe.wait_ge(lo_done, hf * SPLITS + s + 1)
                if ti >= 2:
                    pe.wait_ge(proj_evac, hf * NPE + ti - 1)
                r = s % SPLIT
                if name == "v":
                    whi = w_hi[:, r, 0:1024].rearrange("p (k n) -> p k n", n=P)
                    wlo = w_lo[:, r, 0:1024].rearrange("p (k n) -> p k n", n=P)
                    ins = three_pass(ps[:, ti % 2, :], [(whi[:, kt, :], wlo[:, kt, :], h_hi[:, kt, :], h_lo[:, kt, :]) for kt in range(KT)])
                else:
                    c = P * (ti - min(t for t, at in tile_slot.items() if at == s))
                    whi, wlo = slot_view(w_hi, r, 256), slot_view(w_lo, r, 256)
                    ins = three_pass(ps[:, ti % 2, :],
                                     [(whi[:, kt, c:c + P], wlo[:, kt, c:c + P], h_hi[:, kt, :], h_lo[:, kt, :]) for kt in range(KT)],
                                     ready=(lambda kt: pe.wait_ge(h_lo_done, hf * KT + kt + 1)) if ti == 0 else None)
                ins.then_inc(proj_ready, 1)
                if hf == 0 and ti == 0:
                    nc.tensor.transpose(ps[:, 2, 0:NB], bias_rows[:], ident[0:NB, 0:NB]).then_inc(bias_t, 1)
                while roped < len(ROPED) and ROPED[roped] < ti:
                    rope(roped)
                    roped += 1
                if ti == TILES.index("v") + 1:
                    pe.wait_ge(proj_evac, hf * NPE + ti)
                    for t in range(TT):
                        ins = nc.tensor.transpose(ps[:, 4, P * t:P * t + P], v_t[:, P * t:P * t + P], ident[:])
                    ins.then_inc(v_ready, 1)
                if hf and ti == ROUTE_AT + 2:
                    ranks(hf - 1)
            pe.wait_ge(rope_done, hf * len(ROPED) + len(ROPED))
            pe.wait_ge(v_evac, hf + 1)
            pe.wait_ge(proj_evac, hf * NPE + NPE)
            for n in range(UNITS + 4):
                if n < UNITS:
                    b, p = divmod(n, HEADS // 2)
                    if n >= 2:
                        pe.wait_ge(max_done, hf * UNITS + n - 1)
                    for hh in range(2):
                        at = slice(64 * hh, 64 * hh + 64)
                        ins = nc.tensor.matmul(ps[:, (4, 0)[n % 2] + hh, 0:256], q[at, p, P * b:P * b + P],
                                               k[at, p // 4, P * b:P * b + 2 * P], start=True, stop=True)
                    ins.then_inc(scored, 1)
                if 3 <= n < UNITS + 3:
                    m = n - 3
                    pe.wait_ge(diag_done, hf * UNITS + m + 1)
                    if m >= 2:
                        pe.wait_ge(pt_evac, hf * UNITS + m - 1)
                    for kk in range(2):
                        for hh in range(2):
                            c = P * (2 * kk + hh)
                            ins = nc.tensor.matmul(ps[:, (6, 2)[m % 2], c:c + P],
                                                   probs[:, m % 4, 256 * hh + P * kk:256 * hh + P * kk + P],
                                                   diag[m % 3][:, P * hh:P * hh + P], start=True, stop=True)
                    ins.then_inc(pt_ready, 1)
                if n >= 4:
                    m = n - 4
                    b, p = divmod(m, HEADS // 2)
                    pe.wait_ge(pt_evac, hf * UNITS + m + 1)
                    if m >= 2:
                        pe.wait_ge(o_evac, hf * UNITS + m - 1)
                    for hh in range(2):
                        for kk in range(2):
                            c = P * (2 * kk + hh)
                            ins = nc.tensor.matmul(ps[64 * hh:64 * hh + 64, (7, 3)[m % 2], 0:P],
                                                   v[:, b + kk, 64 * (p // 4):64 * (p // 4) + 64],
                                                   probs_t[:, m % 2, c:c + P], start=kk == 0, stop=kk == 1)
                    ins.then_inc(pv_ready, 1)
            pe.wait_ge(hist_done, hf + 1)
            for g in range(NG):
                nc.tensor.matmul(ps[:, (0, 1, 4, 5)[g], :], pool_mix[:, g, :], pooled[:, g, :], start=True, stop=True).then_inc(mix_ready, 1)
            pe.wait_ge(mix_evac, hf * NG + NG)
            pe.wait_ge(o_evac, hf * UNITS + UNITS)
            for m in range(KT):
                si = PROJ_SLOTS + m
                bank = 4 * (m % 2)
                pe.wait_ge(lo_done, hf * SPLITS + si + 1)
                if m >= 2:
                    pe.wait_ge(merged_done, hf * KT + m - 1)
                whi, wlo = slot_view(w_hi, si % SPLIT, 256), slot_view(w_lo, si % SPLIT, 256)
                for j in range(2):
                    c = P * j
                    three_pass(ps[:, bank + j, :], [(whi[:, kt, c:c + P], wlo[:, kt, c:c + P], h_hi[:, kt, :], h_lo[:, kt, :])
                                                    for kt in range(KT)]).then_inc(gate_mm, 1)
                s = GATE0 + 2 * m + 1
                raw_arrived(pe, hf, s)
                wa = raw[:, s % RAW, :].rearrange("p (k n) -> p k n", n=P)
                for kt in range(KT):
                    nc.tensor.matmul(ps[:, bank + 2, :], wa[:, kt, :], q[:, kt, :], start=kt == 0, stop=kt == KT - 1)
                for g in range(NG):
                    ins = nc.tensor.matmul(ps[:, bank + 3, :], wa[:, KT + g, :], pooled[:, g, :], start=g == 0, stop=g == NG - 1)
                ins.then_inc(br_ready, 1)
            pe.wait_ge(merged_done, hf * KT + KT - 1)
            for n in range(2):
                for kh in range(2):
                    si = PROJ_SLOTS + KT + 2 * n + kh
                    pe.wait_ge(lo_done, hf * SPLITS + si + 1)
                    pe.wait_ge(m_lo_done, hf * KT + 4 * kh + 4)
                    if n == 1:
                        pe.wait_ge(merged_done, hf * KT + KT)
                    whi, wlo = slot_view(w_hi, si % SPLIT, 512), slot_view(w_lo, si % SPLIT, 512)
                    for t in range(TT):
                        at = slice(P * t, P * t + P)
                        ins = three_pass(ps[:, n * TT + t, :],
                                         [(h_hi[:, 4 * kh + i, at], h_lo[:, 4 * kh + i, at], whi[:, i, :], wlo[:, i, :]) for i in range(4)],
                                         first=kh == 0, last=kh == 1)
                        if kh:
                            ins.then_inc(out_ready, 1)
                    if not kh:
                        ins.then_inc(out_half_used, 1)
            pe.wait_ge(x2_done, hf * 2 * TT + 2 * TT)
            transposes(hf, 1)
            for t in range(TT):
                for kt in range(KT):
                    if t == 0:
                        pe.wait_ge(h2t_evac, hf * KT + kt + 1)
                    ins = nc.tensor.matmul(ps[:, 0, E * t:E * t + E], h2_t[:, kt, P * t:P * t + P], router[:, kt, :],
                                           start=kt == 0, stop=kt == KT - 1)
            ins.then_inc(logits_ready, 1)
            if hf == 0:
                pe.wait_ge(logits_read, 1)
                transposes(1, 0)
        pe.wait_ge(h2t_evac, 2 * KT)
        ranks(1)

    @block.gpsimd
    def _(pool):
        pool.memset(ones[:], 1.0)
        pool.iota(e_row[:], pattern=[[1, E]], base=0, channel_multiplier=0, allow_small_or_imprecise_dtypes=True)
        pool.iota(base[:], pattern=[[SLOTS_PER_EXPERT, E]], base=0, channel_multiplier=0, allow_small_or_imprecise_dtypes=True)
        pool.iota(part1[:], pattern=[[0, 1]], base=1, channel_multiplier=1, allow_small_or_imprecise_dtypes=True)
        pool.iota(first_i[:, 0:1], pattern=[[0, 1]], base=0, channel_multiplier=1)
        pool.iota(first_i[:, 1:2], pattern=[[0, 1]], base=0, channel_multiplier=SLOTS_PER_EXPERT)
        codes4 = codes[:].rearrange("p t (k c) -> p t k c", c=2)
        pool.iota(codes4[:, :, :, 0], pattern=[[P, SEQ // P], [SEQ, TOPK]], base=0, channel_multiplier=1)
        pool.iota(codes4[:, :, :, 1], pattern=[[P, SEQ // P], [0, TOPK]], base=0, channel_multiplier=1)
        free2 = free_slots.rearrange("p (s c) -> p s c", c=2)
        pool.memset(free2[:, :, 0:1], FREE_CODE)
        pool.memset(free2[:, :, 1:2], 0)
        pool.memset(k[:, :, 0:P], 0.0)
        pool.memset(v[:, 0, :], 0.0)
        pool.memset(u[:, :, 0:HIST], 0.0).then_inc(ready_const, 1)
        pool.wait_ge(ready_const, 1)
        pool.dma_start(slot_dram.rearrange("(p s) c -> p (s c)", p=P), free_slots).then_inc(table_free, 16)
        pool.wait_ge(table_free, 16)
        pool.wait_ge(const_loaded, 16 * N_CONSTS)
        for hf in range(2):
            st = Steps(pool, pstep, hf * MIX_POOL_STEPS)
            pool.wait_ge(scattered, hf * 16 * TT * TOPK)
            nc.gpsimd.tensor_copy(half_codes[:], codes[:, bass.ds(hf * TT, TT), :]).then_inc(codes_done, 1)
            pool.wait_ge(proj_evac, hf * NPE + NPE)
            pool.wait_ge(rope_done, hf * len(ROPED) + len(ROPED))
            pool.wait_ge(merged_done, hf * KT)
            for g, w in enumerate(POOL_WINDOWS):
                src, n = u[:, g, :], 1
                i = 0
                while n < w:
                    lo = 2 * n - 1
                    st.link(nc.gpsimd.tensor_tensor(win[i % 2][:, lo:], src[:, lo:], src[:, lo - n:HIST + HALF - n], ALU.add))
                    src, n, i = win[i % 2], 2 * n, i + 1
                st.link(nc.gpsimd.tensor_scalar(pooled[:, g, :], src[:, HIST:], 1.0 / w, None, ALU.mult))
                st.link(nc.gpsimd.tensor_tensor(pooled[:, g, 0:HIST], pooled[:, g, 0:HIST],
                                                fix[:, bass.ds(hf, 1), HIST * g:HIST * g + HIST].rearrange("p a n -> p (a n)"), ALU.mult))
                st.link(nc.gpsimd.tensor_tensor(pooled[:, g, :], pooled[:, g, :], u[:, g, HIST:], ALU.subtract))
            nc.gpsimd.tensor_copy(u[:, :, 0:HIST], u[:, :, HALF:HALF + HIST]).then_inc(hist_done, 1)
            assert st.n == MIX_POOL_STEPS, st.n
            x2_half = x2_dram.rearrange("(h t p) n -> h t p n", p=P, t=TT)
            h2_half = h2_dram.rearrange("(h t p) n -> h t p n", p=P, t=TT)
            for t in range(TT):
                pool.wait_ge(x2_done, hf * 2 * TT + TT + t + 1)
                pool.dma_start(x2_half[hf, t], xs[:, t, :]).then_inc(x2_stored[t], 16)
                pool.wait_ge(h2_rows_done, hf * TT + t + 1)
                pool.dma_start(h2_half[hf, t], h2[:, t, :]).then_inc(h2_stored, 16)
            pool.wait_ge(codes_done, hf + 1)
            if hf:
                pool.wait_ge(h2_rows_done, 2 * TT)
                pool.memset(one_x, 1.0)
                pool.iota(x_expert, pattern=[[0, ROUNDS - 1], [1, E]], base=0, channel_multiplier=0, allow_small_or_imprecise_dtypes=True)
                pool.iota(x_base, pattern=[[ITEM, ROUNDS - 1], [SLOTS_PER_EXPERT, E]], base=ITEM, channel_multiplier=0, allow_small_or_imprecise_dtypes=True).then_inc(ready_const, 1)
            pool.wait_ge(dest_done, hf + 1)
            for t in range(TT):
                for c in range(TOPK):
                    pool.indirect_dma_start(slot_dram, bass.IndirectOffsetOnAxis(ap=dest[:, t, c:c + 1].bitcast(U32), axis=0),
                                            half_codes[:, t, 2 * c:2 * c + 2], None).then_inc(scattered, 16)
        pool.wait_ge(scattered, 2 * 16 * TT * TOPK)
        for t in range(TT):
            pool.wait_ge(x2_stored[t], 2 * 16)
        pool.wait_ge(h2_stored, 2 * 16 * TT)

    @block.vector
    def _(dve):
        c1, c2, c3 = cut_pi()
        MAGIC = 1.5 * 2.0**23
        PI = float(np.float32(3.1415925))
        st = Steps(dve, vstep)

        def mean(hf, second, t):
            dve.wait_ge(sumsq_done, (2 * hf + second) * TT + t + 1)
            nc.vector.tensor_scalar(rms[:, t:t + 1], sumsq[:, t:t + 1], 1.0 / D, EPS, ALU.mult, ALU.add).then_inc(ms_done, 1)

        def normalise(hf, second, t):
            dve.wait_ge(rms_done, (2 * hf + second) * TT + t + 1)
            st.link(nc.vector.reciprocal(rstd[:, t:t + 1], rms[:, t:t + 1]))
            to, g_row, done = (h2, g2_row, h2_rows_done) if second else (rows, g1_row, rows_done)
            nc.vector.scalar_tensor_tensor(to[:, t, :], xs[:, t, :], rstd[:, t:t + 1], g_row[:], ALU.mult, ALU.mult).then_inc(done, 1)

        def normalise_x(hf):
            for t in range(TT + 1):
                if t < TT:
                    mean(hf, 0, t)
                if t >= 1:
                    normalise(hf, 0, t - 1)

        def find_angles(hf):
            dve.wait_ge(pos_loaded, 16 * hf + 16)
            a, n_, s_, c_ = (gate[:, i, :] for i in range(4))
            st.link(nc.vector.tensor_scalar(a, pos_i[:], freq[:, 0:1], None, ALU.mult))
            st.link(nc.vector.tensor_scalar(n_, a, 1.0 / (2 * np.pi), MAGIC, ALU.mult, ALU.add))
            st.link(nc.vector.tensor_scalar(n_, n_, -MAGIC, None, ALU.add))
            for c in (c1, c2, c3):
                st.link(nc.vector.scalar_tensor_tensor(a, n_, -c, a, ALU.mult, ALU.add))
            nc.vector.tensor_scalar(s_, a, PI, -PI, ALU.min, ALU.max)
            st.link(nc.vector.tensor_scalar(c_, a, np.pi / 2, None, ALU.add))
            st.link(nc.vector.tensor_scalar(n_, c_, np.pi, -2 * np.pi, ALU.is_gt, ALU.mult))
            st.link(nc.vector.tensor_tensor(c_, c_, n_, ALU.add))
            nc.vector.tensor_scalar(c_, c_, PI, -PI, ALU.min, ALU.max).then_inc(angles, 1)

        def merged_lo(hf, m):
            dve.wait_ge(m_hi_done, hf * KT + m + 1)
            nc.vector.tensor_tensor(h_lo[:, m, :], merged[:, m, :], h_hi[:, m, :].bitcast(F32), ALU.subtract).then_inc(m_lo_done, 1)

        def read_logits(hf):
            dve.wait_ge(logits_ready, hf + 1)
            nc.vector.tensor_tensor(logits[:], ps[:, 0, 0:TT * E].rearrange("p (t e) -> p t e", e=E),
                                    br_row[:].unsqueeze(1).to_broadcast([P, TT, E]), ALU.add).then_inc(logits_read, 1)
            dve.wait_ge(logits_read, hf + 1)

        def choose(hf):
            for t in range(TT):
                ins = nc.vector.max(top[:, t, :], logits[:, t, :])
            st.link(ins)
            nc.vector.tensor_tensor(top_rel[:], top[:, :, 0:TOPK], top[:, :, 0:1].to_broadcast([P, TT, TOPK]), ALU.subtract).then_inc(top_done, 1)
            for t in range(TT):
                ins = nc.vector.max_index(top_i[:, t, :], top[:, t, :], logits[:, t, :])
            st.link(ins)
            st.link(nc.vector.tensor_copy(top_f[:], top_i[:, :, 0:TOPK]))
            st.link(nc.vector.tensor_tensor(onehot[:], e_row[:].unsqueeze(1).to_broadcast([P, TT * TOPK, E]),
                                            top_f[:].rearrange("p t k -> p (t k)").unsqueeze(2).to_broadcast([P, TT * TOPK, E]), ALU.is_equal))
            nc.vector.reduce_sum(chosen[:], onehot[:].rearrange("p (t k) e -> p t e k", k=TOPK), AX_X).then_inc(chosen_done, 1)

        def place(hf):
            dve.wait_ge(rank_ready, hf + 1)
            st.link(nc.vector.tensor_tensor(slot_of[:], ps[:, 7, 0:TT * E].rearrange("p (t e) -> p t e", e=E),
                                            base[:].unsqueeze(1).to_broadcast([P, TT, E]), ALU.add))
            nc.vector.tensor_tensor(base[:], ps[:, 7, TT * E:TT * E + E], base[:], ALU.add)
            for t in range(TT):
                at = slice(TOPK * t, TOPK * t + TOPK)
                ins = nc.vector.tensor_tensor(picked[:, at, :], onehot[:, at, :], slot_of[:, t:t + 1, :].to_broadcast([P, TOPK, E]), ALU.mult)
            st.link(ins)
            st.link(nc.vector.reduce_sum(dest_f[:], picked, AX_X))
            dve.wait_ge(scattered, hf * 16 * TT * TOPK)
            nc.vector.tensor_copy(dest[:].rearrange("p t k -> p (t k)"), dest_f[:]).then_inc(dest_done, 1)
            dve.wait_ge(etop_done, hf + 1)
            st.link(nc.vector.reduce_sum(esum[:], etop[:], AX_X))
            st.link(nc.vector.reciprocal(resum[:], esum[:]))
            g_half = gates[:, TT * hf:TT * hf + TT, :]
            st.link(nc.vector.tensor_tensor(g_half, etop[:], resum[:].unsqueeze(2).to_broadcast([P, TT, TOPK]), ALU.mult))
            st.link(nc.vector.tensor_tensor(picked, onehot[:], g_half.rearrange("p t k -> p (t k)").unsqueeze(2).to_broadcast([P, TT * TOPK, E]), ALU.mult))
            st.link(nc.vector.reduce_sum(gate_of[:, TT * hf:TT * hf + TT, :], picked.rearrange("p (t k) e -> p t e k", k=TOPK), AX_X))

        dve.wait_ge(early_loaded, 48)
        normalise_x(0)
        for hf in range(2):
            lo_part(dve, hf, 0)
            for kt in range(KT):
                dve.wait_ge(h_hi_done, hf * KT + kt + 1)
                nc.vector.tensor_tensor(h_lo[:, kt, :], ps[:, kt, :], h_hi[:, kt, :].bitcast(F32), ALU.subtract).then_inc(h_lo_done, 1)
            lo_part(dve, hf, 1)
            if hf == 0:
                find_angles(0)
                dve.wait_ge(bias_t, 1)
                nc.vector.tensor_copy(bias[:], ps[:, 2, 0:NB])
                nc.vector.tensor_scalar(sinks8[:], sinks[:], float(HD) ** 0.5, None, ALU.mult).then_inc(bias_done, 1)
                dve.wait_ge(bias_done, 1)
                dve.wait_ge(ready_const, 1)
            dve.wait_ge(cs_ready, hf + 1)
            for ti, name in enumerate(TILES):
                s = tile_slot[ti]
                if ti == slot_last[s]:
                    lo_part(dve, hf, s + 2)
                if name == "v":
                    dve.wait_ge(v_ready, hf + 1)
                    nc.vector.tensor_tensor(v[:, 1:, :], ps[:, 4, :].rearrange("p (t n) -> p t n", n=P),
                                            bv_row[:].unsqueeze(1).to_broadcast([P, TT, P]), ALU.add).then_inc(v_evac, 1)
                elif ti in ROPED:
                    ri = ROPED.index(ti)
                    qt = k[:, ti, P:] if ti < 2 else q[:, ti - 3, :]
                    dve.wait_ge(rope_ready, hf * len(ROPED) + ri + 1)
                    nc.vector.tensor_tensor(gate[:, 0, :], ps[:, 2 + ri % 2, :], sin[:], ALU.mult)
                    st.link(nc.vector.tensor_tensor(qt, qt, cos[:], ALU.mult))
                    nc.vector.tensor_tensor(qt, qt, gate[:, 0, :], ALU.add).then_inc(rope_done, 1)
                    dve.wait_ge(rope_done, hf * len(ROPED) + ri + 1)
                if hf and ti == ROUTE_AT:
                    choose(hf - 1)
                if hf and ti == ROUTE_AT + 3:
                    place(hf - 1)
            for n in range(UNITS + 4):
                if n < UNITS:
                    b, (blk, p) = n % 2, divmod(n, HEADS // 2)
                    dve.wait_ge(scored, hf * UNITS + n + 1)
                    if n >= 2:
                        dve.wait_ge(exp_done, hf * UNITS + n - 1)
                    mask = masks[:, min(blk, 1), :]
                    for hh in range(2):
                        at = slice(256 * hh, 256 * hh + 256)
                        ins = nc.vector.tensor_tensor_reduce(out=scores[:, b, at], in0=ps[:, (4, 0)[b] + hh, 0:256], in1=mask, scale=1.0,
                                                             scalar=-3e38, op0=ALU.add, op1=ALU.max, accum_out=smax[:, b, hh:hh + 1])
                    st.link(ins)
                    snk = sinks8[:, 2 * p:2 * p + 2]
                    st.link(nc.vector.tensor_tensor(smax[:, b, :], smax[:, b, :], snk, ALU.max))
                    nc.vector.tensor_scalar(negmax[:, b, :], smax[:, b, :], -(HD ** -0.5), None, ALU.mult)
                    nc.vector.tensor_tensor(sdiff[:, b, :], snk, smax[:, b, :], ALU.subtract).then_inc(max_done, 1)
                if 1 <= n <= UNITS:
                    m = n - 1
                    b = m % 2
                    dve.wait_ge(exp_done, hf * UNITS + m + 1)
                    st.link(nc.vector.tensor_tensor(den[:, b, :], psum_row[:, b, :], sexp[:, b, :], ALU.add))
                    st.link(nc.vector.reciprocal(rden[:, b, :], den[:, b, :]))
                    if m >= 3:
                        dve.wait_ge(pt_ready, hf * UNITS + m - 2)
                    for hh in range(2):
                        ins = nc.vector.tensor_scalar(diag[m % 3][:, P * hh:P * hh + P], ident[:], rden[:, b, hh:hh + 1], None, ALU.mult)
                    ins.then_inc(diag_done, 1)
                if n >= 4:
                    m = n - 4
                    blk, p = divmod(m, HEADS // 2)
                    dve.wait_ge(pv_ready, hf * UNITS + m + 1)
                    nc.vector.tensor_copy(q[:, p, P * blk:P * blk + P], ps[:, (7, 3)[m % 2], 0:P]).then_inc(o_evac, 1)
            nc.vector.tensor_copy(k[:, :, 0:P], k[:, :, HALF:])
            nc.vector.tensor_copy(masks[:, 0, :], masks[:, 1, :])
            nc.vector.tensor_copy(v[:, 0, :], v[:, TT, :])
            for g in range(NG):
                dve.wait_ge(mix_ready, hf * NG + g + 1)
                nc.vector.tensor_scalar(pooled[:, g, :], ps[:, (0, 1, 4, 5)[g], :], bias[:, B_PS + g:B_PS + g + 1], None, ALU.mult).then_inc(mix_evac, 1)
            for m in range(KT):
                bank, g2 = 4 * (m % 2), 2 * (m % 2)
                if m == KT - 1:
                    for done in range(KT - 1):
                        merged_lo(hf, done)
                    lo_part(dve, hf, PROJ_SLOTS + m + 2)
                dve.wait_ge(gate_done, hf * 2 * KT + 2 * m + 2)
                dve.wait_ge(br_ready, hf * KT + m + 1)
                nc.vector.tensor_tensor(gate[:, g2, :], ps[:, bank + 2, :], gate[:, g2, :], ALU.mult)
                st.link(nc.vector.tensor_tensor(gate[:, g2 + 1, :], ps[:, bank + 3, :], gate[:, g2 + 1, :], ALU.mult))
                nc.vector.tensor_tensor(merged[:, m, :], gate[:, g2, :], gate[:, g2 + 1, :], ALU.add).then_inc(merged_done, 1)
                if m < KT - 1:
                    lo_part(dve, hf, PROJ_SLOTS + m + 2)
            merged_lo(hf, KT - 1)
            lo_part(dve, hf, SPLITS - 2)
            if hf == 0:
                find_angles(1)
            for n in range(2):
                if n == 1:
                    lo_part(dve, hf, SPLITS - 1)
                for t in range(TT):
                    dve.wait_ge(out_ready, hf * 2 * TT + n * TT + t + 1)
                    part = xs[:, t, 512 * n:512 * n + 512]
                    nc.vector.tensor_tensor(part, ps[:, n * TT + t, :], part, ALU.add).then_inc(x2_done, 1)
                    if n == 1 and t >= 1:
                        mean(hf, 1, t - 1)
                    if n == 1 and t >= 2:
                        normalise(hf, 1, t - 2)
            mean(hf, 1, TT - 1)
            normalise(hf, 1, TT - 2)
            normalise(hf, 1, TT - 1)
            if hf == 0:
                normalise_x(1)
            read_logits(hf)
        choose(1)
        place(1)

        dve.wait_ge(ready_const, 2)
        st.link(nc.vector.scalar_tensor_tensor(count[:], e_row[:], float(-SLOTS_PER_EXPERT), base[:], ALU.mult, ALU.add))
        for r in range(1, ROUNDS):
            nc.vector.tensor_scalar(x_count[:, E * (r - 1):E * r], count[:], float(-ITEM * r), None, ALU.add)
            ins = nc.vector.tensor_scalar(over[:, E * (r - 1):E * r], count[:], float(ITEM * r), None, ALU.is_gt)
        st.link(ins)
        st.link(nc.vector.tensor_tensor_scan(order, one_x, over, 0.0, ALU.mult, ALU.add))
        st.link(nc.vector.tensor_scalar(items_f[:], order[:, NX - 1:NX], float(E), None, ALU.add))
        nc.vector.tensor_copy(n_items[:], items_f[:])
        st.link(nc.vector.tensor_scalar(x_pick, order, part1[:, 0:1], None, ALU.is_equal))
        st.link(nc.vector.tensor_tensor(x_pick, x_pick, over, ALU.mult))
        nc.vector.tensor_tensor(x_expert, x_expert, x_pick, ALU.mult)
        nc.vector.tensor_tensor(x_count, x_count, x_pick, ALU.mult)
        st.link(nc.vector.tensor_tensor(x_base, x_base, x_pick, ALU.mult))
        nc.vector.reduce_sum(extra_f[:, 0:1], x_expert, AX_X)
        nc.vector.reduce_sum(extra_f[:, 2:3], x_count, AX_X)
        st.link(nc.vector.tensor_tensor(count[:], count[:], ident[:, 0:E], ALU.mult))
        nc.vector.reduce_sum(first_n[:], count[:], AX_X)
        st.link(nc.vector.reduce_sum(extra_f[:, 1:2], x_base, AX_X))
        nc.vector.tensor_copy(first_i[:, 2:3], first_n[:])
        nc.vector.tensor_copy(extra_i[:], extra_f[:]).then_inc(items_done, 1)


def experts(nc, scope, keep, w_up, b_up, w_down, h2_dram, y_dram, slot_dram, x2_dram, x2):
    def sb(name, shape, dt=F32):
        return scope.enter_context(nc.sbuf_tensor(name, shape, dt))

    def sem(name):
        return scope.enter_context(nc.semaphore(name))

    ps, ident, item_row, n_items = keep["ps"], keep["ident"], keep["item_row"], keep["n_items"]
    raw = sb("raw_e", [P, ITEM_SLOTS, SLOT])
    fetched = sb("fetched", [SUB, 2, 2], I32)
    waiting = sb("waiting", [SUB, 2, 2], I32)
    in_work = sb("in_work", [SUB, 2, 2], I32)
    tokens = sb("tokens", [SUB, 2, D])
    xt = sb("xt", [P, KT, ITEM])
    act = sb("act", [P, KT, ITEM])
    glu, lin, sig = sb("glu", [P, 2, 2, ITEM]), sb("lin", [P, 2, 2, ITEM]), sb("sig", [P, 2, 2, ITEM])
    yt = sb("yt", [P, KT, ITEM])
    y = sb("y", [SUB, 2, D])
    bup_rows, bup_t = sb("bup_rows", [E, 2 * DFF]), sb("bup_t", [P, 2 * KT, E])
    bup = sb("bup", [P, 2 * KT])

    raw_loaded = [sem(f"raw_loaded_e{r}") for r in range(ITEM_SLOTS)]
    bup_loaded, bup_tr, bup_ready = sem("bup_loaded"), sem("bup_tr"), sem("bup_ready")
    fetch, copied, gathered, y_scattered = sem("fetch"), sem("copied"), sem("gathered"), sem("y_scattered")
    slot_used, xt_ready, xt_done = sem("slot_used"), sem("xt_ready"), sem("xt_done")
    up_read, glu_done, sig_done, act_done = sem("up_read"), sem("glu_done"), sem("sig_done"), sem("act_done")
    yt_done, y_ready, y_done = sem("yt_done"), sem("y_ready"), sem("y_done")
    act_zero, bias_picked, ticked, y_free, x2_loaded, vstep = sem("act_zero"), sem("bias_picked"), sem("ticked"), sem("y_free"), sem("x2_loaded"), sem("vstep_e")

    XT = [(0, 0, 3), (1, 3, 3), (1, 6, 2)]
    QUARTERS = 4
    VSTEPS = QUARTERS

    block = scope.enter_context(nc.Block())

    def n_of(eng):
        return eng.value_load(n_items[0:1, 0:1], min_val=E, max_val=MAX_ITEMS)

    @block.sync
    def _(sp):
        n = n_of(sp)
        sp.dma_start(bup_rows[:], b_up).then_inc(bup_loaded, 16)
        sp.wait_ge(fetch, 32)
        with sp.Fori(0, n) as item:
            e = sp.value_load(item_row[0:1, bass.ds(3 * item, 1)], min_val=0, max_val=E - 1)
            for s in range(ITEM_SLOTS):
                if s == 2:
                    sp.wait_ge(gathered, 32)
                if s < UP_SLOTS:
                    quarter, which = divmod(s, 2)
                    w, c0 = w_up, DFF * which + 256 * quarter
                else:
                    w, c0 = w_down, 256 * (s - UP_SLOTS)
                sp.wait_ge(slot_used, item * ITEM_SLOTS + s + 1)
                sp.dma_start(raw[:, s, :].rearrange("p (k n) -> p k n", n=256),
                             w[bass.ds(e, 1)].rearrange("a (k p) n -> p (a k) n", p=P)[:, :, c0:c0 + 256]).then_inc(raw_loaded[s], 16)
        sp.dma_start(x2[:], x2_dram.rearrange("(t p) n -> p t n", p=P)).then_inc(x2_loaded, 16)
        sp.wait_ge(x2_loaded, 16)

    @block.scalar
    def _(se):
        def xt_part(item, i):
            bank, k0, nk = XT[i]
            se.wait_ge(xt_ready, item * len(XT) + i + 1)
            nc.scalar.activation(xt[:, k0:k0 + nk, :].rearrange("p k n -> p (k n)"), ps[:, bank, 0:nk * ITEM], ACT.Copy).then_inc(xt_done, 1)

        se.sem_inc(yt_done, DOWN_SLOTS)
        n = n_of(se)
        for i in range(len(XT)):
            xt_part(0, i)
        with se.Fori(0, n) as item:
            for j in range(QUARTERS):
                se.wait_ge(glu_done, item * QUARTERS + j + 1)
                nc.scalar.activation(sig[:, j % 2], glu[:, j % 2], ACT.Sigmoid, scale=ALPHA).then_inc(sig_done, 1)
            xt_part(item + 1, 0)
            xt_part(item + 1, 1)
            for d in range(DOWN_SLOTS):
                se.wait_ge(slot_used, (item + 1) * ITEM_SLOTS + UP_SLOTS + d + 1)
                nc.scalar.activation(yt[:, 2 * d:2 * d + 2, :].rearrange("p k n -> p (k n)"), ps[:, 3 - d % 2, 0:2 * ITEM], ACT.Copy).then_inc(yt_done, 1)
            xt_part(item + 1, 2)

    @block.vector
    def _(dve):
        dve.sem_inc(y_done, 1)
        nc.vector.memset(yt[:], 0.0)
        nc.vector.memset(y[:], 0.0)
        nc.vector.memset(act[:], 0.0).then_inc(act_zero, 1)
        n = n_of(dve)
        dve.wait_ge(bup_tr, 1)
        nc.vector.tensor_copy(bup_t[:, 0:KT, :], ps[:, 0, 0:KT * E].rearrange("p (m e) -> p m e", e=E))
        nc.vector.tensor_scalar(bup_t[:, KT:, :], ps[:, 0, KT * E:2 * KT * E].rearrange("p (m e) -> p m e", e=E), 1.0, None,
                                ALU.add).then_inc(bup_ready, 1)
        dve.wait_ge(bup_ready, 1)
        dve.wait_ge(act_zero, 1)

        def y_part(item, half, ready):
            dve.wait_ge(y_ready, ready)
            for b in range(2):
                ins = nc.vector.tensor_copy(y[:, b, 512 * half:512 * half + 512], ps[0:SUB, 4 + 2 * b + half, :])
            ins.then_inc(y_done, 1)

        with dve.Fori(0, n) as item:
            st = Steps(dve, vstep, item * VSTEPS)
            e = dve.value_load(item_row[0:1, bass.ds(3 * item, 1)], min_val=0, max_val=E - 1)
            nc.vector.tensor_copy(bup[:], bup_t[:, :, bass.ds(e, 1)].rearrange("p m a -> p (m a)")).then_inc(bias_picked, 1)
            dve.wait_ge(bias_picked, item + 1)
            for j in range(QUARTERS):
                bank, b = 2 * (j % 2), j % 2
                for which, to, clamp, done in ((0, glu, LIMIT, glu_done), (1, lin, LIMIT + 1, up_read)):
                    dve.wait_ge(slot_used, (item + 1) * ITEM_SLOTS + 2 * j + which + 1)
                    for c in range(2):
                        col = KT * which + 2 * j + c
                        ins = nc.vector.tensor_scalar(to[:, b, c, :], ps[:, bank + which, ITEM * c:ITEM * c + ITEM],
                                                      bup[:, col:col + 1], clamp, ALU.add, ALU.min)
                    ins.then_inc(done, 1)
                dve.wait_ge(sig_done, item * QUARTERS + j + 1)
                st.link(nc.vector.tensor_tensor(sig[:, b], glu[:, b], sig[:, b], ALU.mult))
                dve.wait_ge(up_read, item * QUARTERS + j + 1)
                nc.vector.scalar_tensor_tensor(act[:, 2 * j:2 * j + 2, :].rearrange("p c n -> p (c n)"), lin[:, b].rearrange("p c n -> p (c n)"),
                                               1.0 - LIMIT, sig[:, b].rearrange("p c n -> p (c n)"), ALU.max, ALU.mult).then_inc(act_done, 1)
                if j == 0:
                    y_part(item, 1, 2 * item + 1)
            dve.wait_ge(y_free, item + 1)
            y_part(item, 0, 2 * item + 2)
        y_part(n, 1, 2 * n + 1)

    @block.tensor
    def _(pe):
        pe.sem_inc(slot_used, ITEM_SLOTS)
        pe.wait_ge(bup_loaded, 16)
        for m in range(2 * KT):
            ins = nc.tensor.transpose(ps[:, 0, E * m:E * m + E], bup_rows[:, P * m:P * m + P], ident[0:E, 0:E])
        ins.then_inc(bup_tr, 1)
        pe.wait_ge(bup_ready, 1)
        n = n_of(pe)

        def transposes(item, i):
            bank, k0, nk = XT[i]
            if i == 0:
                pe.wait_ge(gathered, item * 32 + 32)
            if i == 2:
                pe.wait_ge(xt_done, item * len(XT) + 2)
            for kt in range(k0, k0 + nk):
                for b in range(2):
                    c = ITEM * (kt - k0) + SUB * b
                    ins = nc.tensor.transpose(ps[:, bank, c:c + SUB], tokens[:, b, P * kt:P * kt + P], ident[0:SUB, 0:SUB])
            ins.then_inc(xt_ready, 1)

        def y_transposes(item, d, wait=True, ready=True):
            if wait:
                pe.wait_ge(yt_done, (item + 1) * DOWN_SLOTS + d + 1)
            for m in (2 * d, 2 * d + 1):
                for b in range(2):
                    ins = nc.tensor.transpose(ps[0:SUB, 4 + 2 * b + m // 4, P * (m % 4):P * (m % 4) + P],
                                              yt[:, m, SUB * b:SUB * b + SUB], ident[:])
            if d % 2 and ready:
                ins.then_inc(y_ready, 1)

        def work(item, width):
            for s in range(ITEM_SLOTS):
                up = s < UP_SLOTS
                d = s - UP_SLOTS
                pe.wait_ge(raw_loaded[s], item * 16 + 16)
                if up:
                    quarter, which = divmod(s, 2)
                    bank = 2 * (quarter % 2) + which
                    if quarter >= 2 and not which:
                        pe.wait_ge(up_read, item * QUARTERS + quarter - 1)
                else:
                    bank = 3 - d % 2
                    if d == 0:
                        pe.wait_ge(up_read, item * QUARTERS + QUARTERS - 1)
                        transposes(item + 1, 0)
                        transposes(item + 1, 1)
                        pe.wait_ge(up_read, item * QUARTERS + QUARTERS)
                        pe.wait_ge(act_done, item * QUARTERS + QUARTERS - 1)
                    if d >= 2:
                        pe.wait_ge(yt_done, (item + 1) * DOWN_SLOTS + d - 1)
                w = raw[:, s, :].rearrange("p (k n) -> p k n", n=256)
                x = xt if up else act
                for c in range(2):
                    for kt in range(KT):
                        if s == 0 and c == 0 and kt in (0, XT[2][1]):
                            pe.wait_ge(xt_done, item * len(XT) + (3 if kt else 2))
                        if s == UP_SLOTS and c == 0 and kt == KT - 2:
                            pe.wait_ge(act_done, item * QUARTERS + QUARTERS)
                        ins = nc.tensor.matmul(ps[:, bank, ITEM * c:ITEM * c + width], w[:, kt, P * c:P * c + P], x[:, kt, 0:width],
                                               start=kt == 0, stop=kt == KT - 1)
                ins.then_inc(slot_used, 1)
                if s == 0:
                    pe.wait_ge(yt_done, item * DOWN_SLOTS + DOWN_SLOTS)
                    y_transposes(item, DOWN_SLOTS - 1, wait=False)
                if d == 1:
                    pe.wait_ge(y_done, item * 2 + 1)
                if d == 3:
                    pe.wait_ge(y_done, item * 2 + 2)
                if d >= 1:
                    y_transposes(item, d - 1)
            transposes(item + 1, 2)

        def choose(taken, item, widths):
            if len(widths) == 1:
                work(item, widths[0])
                return
            mid = len(widths) // 2
            with pe.If(taken <= widths[mid - 1]):
                choose(taken, item, widths[:mid])
            with pe.Else():
                choose(taken, item, widths[mid:])

        pe.wait_ge(act_zero, 1)
        for bank in range(4):
            ins = nc.tensor.matmul(ps[:, bank, 0:2 * ITEM], ident[:], act[:, 0:2, :].rearrange("p k n -> p (k n)"), start=True, stop=True)
        y_transposes(0, DOWN_SLOTS - 2, wait=False, ready=False)
        for i in range(len(XT)):
            transposes(0, i)
        with pe.Fori(0, n) as item:
            taken = pe.value_load(item_row[0:1, bass.ds(3 * item + 2, 1)], min_val=0, max_val=SEQ)
            choose(taken, item, WIDTHS)
        pe.wait_ge(yt_done, n * DOWN_SLOTS + DOWN_SLOTS)
        y_transposes(n, DOWN_SLOTS - 1, wait=False)

    @block.gpsimd
    def _(pool):
        pool.memset(in_work[:], FREE_CODE)
        n = n_of(pool)

        def held(eng):
            eng.sem_inc(ticked, 1)

        def fetch_item(item, first=False):
            b0 = pool.value_load(item_row[0:1, bass.ds(3 * item + 1, 1)], min_val=0, max_val=E * SLOTS_PER_EXPERT - ITEM)
            for b in range(2):
                pool.dma_start(fetched[:, b, :], slot_dram[bass.ds(b0 + SUB * b, SUB), :]).then_inc(fetch, 16)
            pool.wait_ge(fetch, item * 32 + 32)
            if not first:
                pool.wait_ge(xt_ready, item * len(XT))
            held(pool)
            for b in range(2):
                pool.indirect_dma_start(tokens[:, b, :], None, h2_dram,
                                        bass.IndirectOffsetOnAxis(ap=fetched[:, b, 1:2].bitcast(U32), axis=0)).then_inc(gathered, 16)

        def scatter(item):
            pool.wait_ge(y_done, item * 2 + 2)
            held(pool)
            for b in range(2):
                pool.indirect_dma_start(y_dram, bass.IndirectOffsetOnAxis(ap=in_work[:, b, 0:1].bitcast(U32), axis=0),
                                        y[:, b, :], None, bounds_check=NCODES - 1, oob_is_err=False).then_inc(y_scattered, 16)
            pool.wait_ge(y_scattered, item * 32 + 32)

        fetch_item(0, first=True)
        pool.wait_ge(act_zero, 1)
        with pool.Fori(0, n) as item:
            pool.wait_ge(gathered, item * 32 + 32)
            held(pool)
            nc.gpsimd.tensor_copy(waiting[:], fetched[:]).then_inc(copied, 1)
            pool.wait_ge(copied, 2 * item + 1)
            fetch_item(item + 1)
            scatter(item)
            pool.sem_inc(y_free, 1)
            nc.gpsimd.tensor_copy(in_work[:], waiting[:]).then_inc(copied, 1)
            pool.wait_ge(copied, 2 * item + 2)
        scatter(n)


def combine(nc, scope, keep, x2, y_dram, b_down, normf_g, out_rows):
    def sb(name, shape, dt=F32):
        return scope.enter_context(nc.sbuf_tensor(name, shape, dt))

    def sem(name):
        return scope.enter_context(nc.semaphore(name))

    ps, ident, gates, gate_of = keep["ps"], keep["ident"], keep["gates"], keep["gate_of"]
    TILES_C = SEQ // P
    DEEP = 4
    ON_PE = 2
    ys = sb("ys", [P, DEEP, TOPK, D])
    diag = sb("diag", [P, TILES_C, ON_PE, P])
    junk = sb("junk", [P, D])
    bd, gf_row = sb("bd", [E, D]), sb("gf_row", [P, D])
    g_t = sb("g_t", [E, TILES_C, P])
    sumsq, ms, rms, rstd = (sb(n, [P, DEEP]) for n in ("sumsq_c", "ms_c", "rms_c", "rstd_c"))

    loaded = [sem(f"loaded{b}") for b in range(DEEP)]
    pe_loaded = [sem(f"pe_loaded{b}") for b in range(DEEP)]
    c_loaded, stored = sem("c_loaded"), sem("stored")
    gt_ready, gt_done, diag_done, summed, added, squared, ms_done, rms_done, normed = (
        sem("gt_ready"), sem("gt_done"), sem("diag_done"), sem("summed"), sem("added"), sem("squared"), sem("ms_done_c"),
        sem("rms_done_c"), sem("normed"))
    vstep = sem("vstep_c")
    VSTEPS = TOPK - ON_PE + 1
    y4 = y_dram.rearrange("(k t p) n -> t p k n", p=P, t=TILES_C)
    out8 = out_rows.rearrange("(t p) n -> t p n", p=P)
    block = scope.enter_context(nc.Block())

    def x2_tile(t):
        return x2[:, bass.ds(t, 1), :].rearrange("p a n -> p (a n)")

    @block.sync
    def _(sp):
        sp.dma_start(bd[:], b_down).then_inc(c_loaded, 16)
        sp.dma_start(gf_row[:], normf_g.rearrange("(a n) -> a n", a=1).to_broadcast([P, D])).then_inc(c_loaded, 16)
        with sp.Fori(0, TILES_C // DEEP) as i:
            for b in range(DEEP):
                sp.wait_ge(added, DEEP * i + b + 1)
                for c in range(TOPK):
                    sp.dma_start(ys[:, b, c, :], y4[bass.ds(DEEP * i + b, 1), :, c, :].rearrange("a p n -> p (a n)")).then_inc((pe_loaded if c < ON_PE else loaded)[b], 16)

    @block.tensor
    def _(pe):
        for t in range(TILES_C):
            ins = nc.tensor.transpose(ps[0:E, t // 4, P * (t % 4):P * (t % 4) + P], gate_of[:, t, :], ident[:])
        ins.then_inc(gt_ready, 1)
        pe.wait_ge(gt_done, 1)
        pe.wait_ge(c_loaded, 32)
        pe.wait_ge(diag_done, 1)
        for t in range(TILES_C):
            b = t % DEEP
            if t >= DEEP:
                pe.wait_ge(added, t + 1)
            for c in range(2):
                at = slice(512 * c, 512 * c + 512)
                nc.tensor.matmul(ps[:, 2 * b + c, :], g_t[:, t, :], bd[:, at], start=True, stop=False)
                if c == 0:
                    pe.wait_ge(pe_loaded[b], (t // DEEP + 1) * 16 * ON_PE)
                for kk in range(ON_PE):
                    ins = nc.tensor.matmul(ps[:, 2 * b + c, :], diag[:, t, kk, :], ys[:, b, kk, at], start=False, stop=kk == ON_PE - 1)
            ins.then_inc(summed, 1)

    @block.vector
    def _(dve):
        dve.sem_inc(added, DEEP)
        dve.wait_ge(gt_ready, 1)
        nc.vector.tensor_copy(g_t[:].rearrange("p t n -> p (t n)"), ps[0:E, 0:2, :].rearrange("p b n -> p (b n)")).then_inc(gt_done, 1)
        dve.wait_ge(c_loaded, 32)
        with dve.Fori(0, TILES_C // DEEP) as i:
            st = Steps(dve, vstep, i * DEEP * VSTEPS)

            def finish(b):
                dve.wait_ge(squared, DEEP * i + b + 1)
                nc.vector.tensor_scalar(ms[:, b:b + 1], sumsq[:, b:b + 1], 1.0 / D, EPS, ALU.mult, ALU.add).then_inc(ms_done, 1)
                dve.wait_ge(rms_done, DEEP * i + b + 1)
                st.link(nc.vector.reciprocal(rstd[:, b:b + 1], rms[:, b:b + 1]))
                acc = x2_tile(DEEP * i + b)
                nc.vector.scalar_tensor_tensor(acc, acc, rstd[:, b:b + 1], gf_row[:], ALU.mult, ALU.mult).then_inc(normed, 1)

            for b in range(DEEP):
                g = gates[:, bass.ds(DEEP * i + b, 1), :].rearrange("p a k -> p (a k)")
                acc = x2_tile(DEEP * i + b)
                dve.wait_ge(loaded[b], (i + 1) * 16 * (TOPK - ON_PE))
                for c in range(ON_PE, TOPK):
                    st.link(nc.vector.scalar_tensor_tensor(acc, ys[:, b, c, :], g[:, c:c + 1], acc, ALU.mult, ALU.add))
                dve.wait_ge(summed, DEEP * i + b + 1)
                nc.vector.tensor_tensor(acc, ps[:, 2 * b:2 * b + 2, :].rearrange("p a n -> p (a n)"), acc, ALU.add).then_inc(added, 1)
                if b:
                    finish(b - 1)
            finish(DEEP - 1)
            assert st.n == DEEP * VSTEPS, st.n

    @block.scalar
    def _(act):
        for t in range(TILES_C):
            for kk in range(ON_PE):
                ins = nc.scalar.activation(diag[:, t, kk, :], ident[:], ACT.Copy, scale=gates[:, t, kk:kk + 1])
        ins.then_inc(diag_done, 1)

        def store(t):
            act.wait_ge(normed, t + 1)
            act.dma_start(out8[bass.ds(t, 1)].rearrange("a p n -> p (a n)"), x2_tile(t)).then_inc(stored, 16)

        with act.Fori(0, TILES_C // DEEP) as i:
            for b in range(DEEP):
                act.wait_ge(added, DEEP * i + b + 1 + DEEP)
                nc.scalar.activation(junk[:], x2_tile(DEEP * i + b), ACT.Square, accum_out=sumsq[:, b:b + 1]).then_inc(squared, 1)
                act.wait_ge(ms_done, DEEP * i + b + 1)
                nc.scalar.activation(rms[:, b:b + 1], ms[:, b:b + 1], ACT.Sqrt).then_inc(rms_done, 1)
                if b:
                    store(DEEP * i + b - 1)
            store(DEEP * i + DEEP - 1)
        act.wait_ge(stored, 16 * TILES_C)


INPUTS = ["x", "positions", "norm1_g", "w_in", "b_in", "attn_sinks", "w_attn_br", "pool_w", "pool_scale", "w_pool_br",
          "w_out", "norm2_g", "w_router", "b_router", "w_up", "b_up", "w_down", "b_down", "normf_g"]


def kernel(**inputs):
    import concourse.bacc as bacc
    from concourse.bass_utils import run_bass_kernel_spmd

    nc = bacc.Bacc("TRN2", target_bir_lowering=False, num_devices=1)
    arrays = {f"in_{n}": np.ascontiguousarray(inputs[n]) for n in INPUTS}
    arrays.update({f"in_{n}": a for n, a in shape_constants().items()})
    args = [nc.dram_tensor(n, a.shape, mybir.dt.from_np(a.dtype), kind="ExternalInput").ap() for n, a in arrays.items()]
    out = nc.dram_tensor("out_0", [1, SEQ, D], F32, kind="ExternalOutput").ap()
    decoder_layer(nc, *args, out)
    return run_bass_kernel_spmd(nc, [arrays], core_ids=[0]).results[0]["out_0"]
```
